# Optimizing a Trainium2 kernel written in Bass

```python
import math
import jax, jax.numpy as jnp
from jax import lax
import numpy as np

"""Two layers of a hybrid decoder trunk with parallel, gated token mixers.

Each layer (sandwich RMSNorm around every sub-layer):
  1. hybrid mixer: one combined input projection feeds three parallel causal mixers
     (stick-breaking attention, chunked spatial-gating MLP, S5 diagonal SSM), each
     projected to D_MODEL, merged by per-channel sigmoid gates, then one output projection.
  2. cross-attention (4 heads, softmax) into 256 memory tokens.
  3. dense SwiGLU FFN.
Inputs : x (BATCH, SEQ, D_MODEL) f32, mem (BATCH, 256, D_MODEL) f32, per-layer weights
         stacked on a leading DEPTH axis.
Output : (BATCH, SEQ, D_MODEL).
"""

D_MODEL = 2048
BATCH = 1
SEQ = 256
DEPTH = 1

SB_HEADS = 4
SB_HEAD_DIM = 256
SB_WIDTH = SB_HEADS * SB_HEAD_DIM
Q_BLOCK = 128
K_BLOCK = 128
GM_GROUPS = 4
GM_CHUNK = 128
GM_WIDTH = 512
GM_GROUP_DIM = GM_WIDTH // GM_GROUPS
S5_WIDTH = 512
S5_GROUP_DIM = 16
S5_GROUPS = S5_WIDTH // S5_GROUP_DIM
S5_STATE = 64
S5_DT_MIN = 1e-3
S5_DT_MAX = 1e-1
N_BRANCH = 3
MEM_LEN = 256
X_HEADS = 4
X_HEAD_DIM = 128
X_WIDTH = X_HEADS * X_HEAD_DIM
FFN_HIDDEN = ((8 * D_MODEL + 3 * 256 - 1) // (3 * 256)) * 256
RMS_EPS = 1e-6

OFF_Q = SB_WIDTH
OFF_K = OFF_Q + SB_WIDTH
OFF_V = OFF_K + SB_WIDTH
OFF_GM = OFF_V + 2 * GM_WIDTH
OFF_S5 = OFF_GM + S5_WIDTH
N_IN = OFF_S5 + N_BRANCH * D_MODEL

kernel_name = "hybrid_sb_gmlp_s5_gated_block"

def rms_norm(x, gain):
    xf = x.astype(jnp.float32)
    y = xf * lax.rsqrt(jnp.mean(xf * xf, axis=-1, keepdims=True) + RMS_EPS)
    return (y * gain.astype(jnp.float32)).astype(x.dtype)

def stick_breaking_attention(q, k, v):
    b, h, s, dh = q.shape
    nb = s // Q_BLOCK
    scale = dh ** -0.5
    kb_idx = jnp.arange(K_BLOCK)
    u_strict = (kb_idx[:, None] > kb_idx[None, :]).astype(jnp.float32)
    outs = []
    for i in range(nb):
        klen = (i + 1) * Q_BLOCK
        nkb = klen // K_BLOCK
        qi = q[:, :, i * Q_BLOCK:(i + 1) * Q_BLOCK]
        ki = k[:, :, :klen]
        vi = v[:, :, :klen]
        z = jnp.einsum('bhqd,bhkd->bhqk', qi, ki, preferred_element_type=jnp.float32) * scale
        qpos = i * Q_BLOCK + jnp.arange(Q_BLOCK)
        mask = jnp.arange(klen)[None, :] < qpos[:, None]
        ls_neg = jax.nn.log_sigmoid(-z)
        log_1m = jnp.where(mask, ls_neg, 0.0).reshape(b, h, Q_BLOCK, nkb, K_BLOCK)
        local = jnp.einsum('bhqcj,js->bhqcs', log_1m, u_strict)
        blk = jnp.sum(log_1m, axis=-1)
        c_idx = jnp.arange(nkb)
        m_strict = (c_idx[:, None] > c_idx[None, :]).astype(jnp.float32)
        carry = jnp.einsum('bhqc,cd->bhqd', blk, m_strict)
        log_w = (z + ls_neg).reshape(b, h, Q_BLOCK, nkb, K_BLOCK) + local + carry[..., None]
        w = jnp.where(mask, jnp.exp(log_w.reshape(b, h, Q_BLOCK, klen)), 0.0)
        o = jnp.einsum('bhqk,bhkd->bhqd', w.astype(v.dtype), vi, preferred_element_type=jnp.float32)
        outs.append(o.astype(v.dtype))
    return jnp.concatenate(outs, axis=2)

def spatial_gating(uv, v_gain, w_s, b_s):
    u, v = jnp.split(uv, 2, axis=-1)
    v = rms_norm(v, v_gain)
    b, s, _ = v.shape
    vc = v.reshape(b, s // GM_CHUNK, GM_CHUNK, GM_GROUPS, GM_GROUP_DIM)
    causal = jnp.tril(jnp.ones((GM_CHUNK, GM_CHUNK), dtype=bool))
    w = jnp.where(causal[None], w_s, 0.0).astype(v.dtype)
    mixed = jnp.einsum('gts,bcsgd->bctgd', w, vc) + b_s.T.astype(v.dtype)[None, None, :, :, None]
    return u * mixed.reshape(b, s, GM_WIDTH)

def _ssm_combine(left, right):
    a1r, a1i, b1r, b1i = left
    a2r, a2i, b2r, b2i = right
    return (a2r * a1r - a2i * a1i,
            a2r * a1i + a2i * a1r,
            a2r * b1r - a2i * b1i + b2r,
            a2r * b1i + a2i * b1r + b2i)

def s5_layer(u, lam_re, lam_im, log_dt, b_re, b_im, c_re, c_im, d_skip, w_glu):
    bsz, s, _ = u.shape
    f32 = jnp.float32
    ug = u.reshape(bsz, s, S5_GROUPS, S5_GROUP_DIM).astype(f32)
    lr, li = lam_re.astype(f32), lam_im.astype(f32)
    dt = jnp.exp(log_dt.astype(f32))[:, None]
    mag = jnp.exp(lr * dt)
    a_re, a_im = mag * jnp.cos(li * dt), mag * jnp.sin(li * dt)
    den = lr * lr + li * li
    x_ = a_re - 1.0
    f_re = (x_ * lr + a_im * li) / den
    f_im = (a_im * lr - x_ * li) / den
    br, bi = b_re.astype(f32), b_im.astype(f32)
    bb_re = f_re[..., None] * br - f_im[..., None] * bi
    bb_im = f_re[..., None] * bi + f_im[..., None] * br
    bu_re = jnp.einsum('bsgc,gnc->bsgn', ug, bb_re)
    bu_im = jnp.einsum('bsgc,gnc->bsgn', ug, bb_im)
    shp = (1, s, S5_GROUPS, S5_STATE)
    ar = jnp.broadcast_to(a_re[None, None], shp)
    ai = jnp.broadcast_to(a_im[None, None], shp)
    _, _, x_re, x_im = lax.associative_scan(_ssm_combine, (ar, ai, bu_re, bu_im), axis=1)
    y = (jnp.einsum('bsgn,gcn->bsgc', x_re, c_re.astype(f32))
         - jnp.einsum('bsgn,gcn->bsgc', x_im, c_im.astype(f32))
         + d_skip.astype(f32).reshape(S5_GROUPS, S5_GROUP_DIM) * ug)
    y = jax.nn.gelu(y.reshape(bsz, s, S5_WIDTH)).astype(u.dtype)
    a, g = jnp.split(y @ w_glu, 2, axis=-1)
    return a * jax.nn.sigmoid(g)

def memory_cross_attention(h, mem_n, w_q, w_kv, w_o):
    b, s, _ = h.shape
    q = (h @ w_q).reshape(b, s, X_HEADS, X_HEAD_DIM)
    k, v = jnp.split(mem_n @ w_kv, 2, axis=-1)
    k = k.reshape(b, MEM_LEN, X_HEADS, X_HEAD_DIM)
    v = v.reshape(b, MEM_LEN, X_HEADS, X_HEAD_DIM)
    z = jnp.einsum('bshd,bmhd->bhsm', q, k, preferred_element_type=jnp.float32) * (X_HEAD_DIM ** -0.5)
    p = jax.nn.softmax(z, axis=-1).astype(v.dtype)
    o = jnp.einsum('bhsm,bmhd->bshd', p, v)
    return o.reshape(b, s, X_WIDTH) @ w_o

def setup_inputs(seed: int = 0) -> dict:
    key = jax.random.key(seed)
    ks = jax.random.split(key, 32)
    L, D = DEPTH, D_MODEL

    def nrm(k, shape, fan_in):
        return jax.random.normal(k, shape, jnp.float32) * (fan_in ** -0.5)

    def gain(k, shape):
        return 1.0 + 0.02 * jax.random.normal(k, shape, jnp.float32)

    n_idx = jnp.arange(S5_STATE, dtype=jnp.float32)
    return {
        "x": jax.random.normal(ks[0], (BATCH, SEQ, D), jnp.float32),
        "mem": jax.random.normal(ks[1], (BATCH, MEM_LEN, D), jnp.float32),
        "mix_pre_gain": gain(ks[2], (L, D)),
        "mix_post_gain": gain(ks[3], (L, D)),
        "w_in": nrm(ks[4], (L, D, N_IN), D),
        "gm_v_gain": gain(ks[5], (L, GM_WIDTH)),
        "gm_w_s": nrm(ks[6], (L, GM_GROUPS, GM_CHUNK, GM_CHUNK), GM_CHUNK),
        "gm_b_s": gain(ks[7], (L, GM_GROUPS, GM_CHUNK)),
        "s5_lam_re": -0.5 + 0.01 * jax.random.normal(ks[8], (L, S5_GROUPS, S5_STATE), jnp.float32),
        "s5_lam_im": jnp.pi * n_idx + 0.01 * jax.random.normal(ks[9], (L, S5_GROUPS, S5_STATE), jnp.float32),
        "s5_log_dt": jax.random.uniform(ks[10], (L, S5_GROUPS), jnp.float32,
                                        minval=math.log(S5_DT_MIN), maxval=math.log(S5_DT_MAX)),
        "s5_b_re": nrm(ks[11], (L, S5_GROUPS, S5_STATE, S5_GROUP_DIM), 2 * S5_GROUP_DIM),
        "s5_b_im": nrm(ks[12], (L, S5_GROUPS, S5_STATE, S5_GROUP_DIM), 2 * S5_GROUP_DIM),
        "s5_c_re": nrm(ks[13], (L, S5_GROUPS, S5_GROUP_DIM, S5_STATE), 2 * S5_STATE),
        "s5_c_im": nrm(ks[14], (L, S5_GROUPS, S5_GROUP_DIM, S5_STATE), 2 * S5_STATE),
        "s5_d": jax.random.normal(ks[15], (L, S5_WIDTH), jnp.float32),
        "s5_w_glu": nrm(ks[16], (L, S5_WIDTH, 2 * S5_WIDTH), S5_WIDTH),
        "w_br_a": nrm(ks[17], (L, SB_WIDTH, D), SB_WIDTH),
        "w_br_b": nrm(ks[18], (L, GM_WIDTH, D), GM_WIDTH),
        "w_br_c": nrm(ks[19], (L, S5_WIDTH, D), S5_WIDTH),
        "w_out": nrm(ks[20], (L, D, D), D),
        "xattn_pre_gain": gain(ks[21], (L, D)),
        "xattn_post_gain": gain(ks[22], (L, D)),
        "mem_gain": gain(ks[23], (L, D)),
        "w_xq": nrm(ks[24], (L, D, X_WIDTH), D),
        "w_xkv": nrm(ks[25], (L, D, 2 * X_WIDTH), D),
        "w_xo": nrm(ks[26], (L, X_WIDTH, D), X_WIDTH),
        "ffn_pre_gain": gain(ks[27], (L, D)),
        "ffn_post_gain": gain(ks[28], (L, D)),
        "w_ffn_in": nrm(ks[29], (L, D, 2 * FFN_HIDDEN), D),
        "w_ffn_out": nrm(ks[30], (L, FFN_HIDDEN, D), FFN_HIDDEN),
    }

def reference(x, mem, mix_pre_gain, mix_post_gain, w_in, gm_v_gain, gm_w_s, gm_b_s,
              s5_lam_re, s5_lam_im, s5_log_dt, s5_b_re, s5_b_im, s5_c_re, s5_c_im, s5_d,
              s5_w_glu, w_br_a, w_br_b, w_br_c, w_out, xattn_pre_gain, xattn_post_gain,
              mem_gain, w_xq, w_xkv, w_xo, ffn_pre_gain, ffn_post_gain, w_ffn_in, w_ffn_out):
    b, s, d = x.shape
    for l in range(DEPTH):
        h = rms_norm(x, mix_pre_gain[l])
        proj = h @ w_in[l]
        q, k, v, gm_uv, s5_u, gates = jnp.split(proj, [OFF_Q, OFF_K, OFF_V, OFF_GM, OFF_S5], axis=-1)
        to_heads = lambda t: t.reshape(b, s, SB_HEADS, SB_HEAD_DIM).transpose(0, 2, 1, 3)
        y_a = stick_breaking_attention(to_heads(q), to_heads(k), to_heads(v))
        y_a = y_a.transpose(0, 2, 1, 3).reshape(b, s, SB_WIDTH) @ w_br_a[l]
        y_b = spatial_gating(jax.nn.gelu(gm_uv), gm_v_gain[l], gm_w_s[l], gm_b_s[l]) @ w_br_b[l]
        y_c = s5_layer(s5_u, s5_lam_re[l], s5_lam_im[l], s5_log_dt[l], s5_b_re[l], s5_b_im[l],
                       s5_c_re[l], s5_c_im[l], s5_d[l], s5_w_glu[l]) @ w_br_c[l]
        g = jax.nn.sigmoid(gates).reshape(b, s, N_BRANCH, d)
        merged = g[:, :, 0] * y_a + g[:, :, 1] * y_b + g[:, :, 2] * y_c
        x = x + rms_norm(merged @ w_out[l], mix_post_gain[l])
        h = rms_norm(x, xattn_pre_gain[l])
        m = rms_norm(mem, mem_gain[l])
        x = x + rms_norm(memory_cross_attention(h, m, w_xq[l], w_xkv[l], w_xo[l]), xattn_post_gain[l])
        h = rms_norm(x, ffn_pre_gain[l])
        gt, up = jnp.split(h @ w_ffn_in[l], 2, axis=-1)
        x = x + rms_norm((jax.nn.silu(gt) * up) @ w_ffn_out[l], ffn_post_gain[l])
    return x


_drawn_inputs = setup_inputs


def setup_inputs(seed=0):
    import zlib

    import numpy as np

    out = dict(_drawn_inputs(seed))
    spreads = {}
    factors = {'mix_pre_gain': 2.837,
     'mix_post_gain': 3.756,
     'gm_v_gain': 8.0,
     'gm_b_s': 6.261,
     's5_lam_re': 64.0,
     's5_lam_im': 33.648,
     's5_log_dt': 34.648,
     's5_b_re': 46.504,
     's5_b_im': 46.784,
     's5_c_re': 46.2,
     's5_c_im': 47.792,
     'xattn_pre_gain': 4.467,
     'xattn_post_gain': 13.451,
     'mem_gain': 3.202,
     'ffn_pre_gain': 11.316,
     'ffn_post_gain': 21.761}
    for name, (base, spread) in spreads.items():
        noise = np.random.default_rng([zlib.crc32(name.encode()), seed]).standard_normal(out[name].shape)
        drawn = base * np.exp(spread * noise) if base else spread * noise
        out[name] = __import__('jax').numpy.asarray(drawn.astype(out[name].dtype))
    for name, factor in factors.items():
        out[name] = (out[name] * factor).astype(out[name].dtype)
    return out
```

```python
from contextlib import ExitStack
import math

import concourse.bass as bass
from concourse import mybir

F32 = mybir.dt.float32
F32R = mybir.dt.float32r
ACT = mybir.ActivationFunctionType
ALU = mybir.AluOpType
AX = mybir.AxisListType

P = 128
HALVES = 2
SEQ = P * HALVES
D = 2048
NC = 512
KT = D // P
UK = 2
RING = 4
CU = KT // UK

HEADS, HDIM = 4, 256
GROUPS, GCHUNK = 4, 128
S5_PAIRS, S5_TILES = 16, 4
STATE, GCH = 64, 16
XHEADS, XDIM = 4, 128
FFN = 5632
OFF_GATES = 3072 + 1024 + 512
OFF_S5 = 3072 + 1024
EPS = 1e-6

U_S5, U_PROJ, U_GLU, U_GATE = 0, 8, 72, 76
U_BR, U_OUT, U_MK, U_XQ, U_MV = 172, 204, 236, 244, 252
U_XO, U_FI, U_FO, U_END = 260, 268, 444, 532
G_S5, G_PROJ, G_GLU, G_GATE, G_BR, G_OUT, G_MK, G_XQ, G_MV, G_XO, G_FI, G_FO = (
    0, 1, 9, 11, 23, 35, 39, 40, 41, 42, 46, 68)
T_X, T_GLU, T_BR, T_MEM, T_X1, T_X2, T_FFN = 0, 8, 10, 18, 26, 34, 42
N_X, N_GM, N_Y1, N_MEM, N_X1, N_Y2, N_X2, N_Y3 = range(8)
C_MIX, C_XAT, C_MEM, C_FFN, C_LRE, C_LIM, C_LDT, C_D, C_BS = 0, 16, 32, 48, 64, 80, 96, 112, 116

TWO_PI = 2 * math.pi
PI_A = 6.28125
PI_B = 0.0019350051879882812
PI_C = TWO_PI - PI_A - PI_B
ROUND = 1.5 * 2 ** 23
PI_MAX = 3.1415925


class Chain:

    def __init__(self, engine, sem):
        self.engine, self.sem, self.count, self.offset = engine, sem, 0, 0

    def enter(self, reg, first, per):
        self.entered, self.per = self.count, per
        self.offset = (reg - first) * per if first else reg * per

    def leave(self, n):
        assert self.count - self.entered == self.per, (self.count - self.entered, self.per)
        self.count, self.offset = self.entered + n * self.per, 0

    def link(self, instruction):
        instruction.then_inc(self.sem, 1)
        self.count += 1
        self.engine.wait_ge(self.sem, self.offset + self.count)


def trunk(nc, x, mem, mix_pre_gain, mix_post_gain, w_in, gm_v_gain, gm_w_s, gm_b_s,
          s5_lam_re, s5_lam_im, s5_log_dt, s5_b_re, s5_b_im, s5_c_re, s5_c_im, s5_d,
          s5_w_glu, w_br_a, w_br_b, w_br_c, w_out, xattn_pre_gain, xattn_post_gain,
          mem_gain, w_xq, w_xkv, w_xo, ffn_pre_gain, ffn_post_gain, w_ffn_in, w_ffn_out, out):
    with ExitStack() as ctx:
        base = (nc.sbuf_base + 31) // 32 * 32
        KB = 1024

        def at(name, kb, shape, dt=F32):
            return nc.alloc_sbuf_tensor_at(name, [P] + shape, dt, offset=base + int(kb * KB))

        def ps(name, shape):
            return ctx.enter_context(nc.psum_tensor(name, shape, F32))

        def sem(name):
            return ctx.enter_context(nc.semaphore(name))

        raw = at("raw", 0, [RING, UK, NC])
        w_hi = at("w_hi", 16, [RING, UK, NC], F32R)
        w_lo = at("w_lo", 32, [RING, UK, NC], F32R)
        xT_hi = at("xT_hi", 48, [KT, SEQ], F32R)
        xT_lo = at("xT_lo", 64, [KT, SEQ], F32R)
        x_tok = at("x_tok", 80, [HALVES, D])
        proj = at("proj", 80, [32, HALVES, P])
        yaT_hi = at("yaT_hi", 80, [8, SEQ], F32R)
        yaT_lo = at("yaT_lo", 88, [8, SEQ], F32R)
        ycT_hi = at("ycT_hi", 96, [4, SEQ], F32R)
        ycT_lo = at("ycT_lo", 100, [4, SEQ], F32R)
        gT_hi = at("gT_hi", 112, [4, SEQ], F32R)
        gT_lo = at("gT_lo", 116, [4, SEQ], F32R)
        ybT_hi = at("ybT_hi", 120, [4, SEQ], F32R)
        ybT_lo = at("ybT_lo", 124, [4, SEQ], F32R)
        vgain = at("vgain", 120, [NC])
        yc = at("yc", 128, [HALVES, NC])
        gates = at("gates", 132, [12, HALVES, NC])
        cosT = at("cosT", 132, [S5_PAIRS, SEQ])
        sinT = at("sinT", 148, [S5_PAIRS, SEQ])
        tabA = at("tabA", 164, [S5_PAIRS, P])
        tabB = at("tabB", 172, [S5_PAIRS, P])
        m1 = at("m1", 164, [4, SEQ])
        m2 = at("m2", 168, [4, SEQ])
        v_re = at("v_re", 172, [4, SEQ])
        v_im = at("v_im", 176, [4, SEQ])
        s5u = at("s5u", 180, [S5_TILES, HALVES, P])
        Bn = at("Bn", 184, [S5_PAIRS, 2, 32])
        Cn = at("Cn", 188, [S5_TILES, 2, P])
        rows = at("rows", 192, [P])
        u_st = at("u_st", 192, [HALVES, P])
        B_st = at("B_st", 193, [2, 4, 32])
        C_st = at("C_st", 194, [2, P])
        uB = at("uB", 195, [2, SEQ])
        Cp = at("Cp", 197, [2, P])
        y_sb = at("y_sb", 198, [SEQ])
        g_sb = at("g_sb", 199, [SEQ])
        ang = at("ang", 200, [8, S5_PAIRS])
        sinA = at("sinA", 200.5, [8, S5_PAIRS])
        cosA = at("cosA", 201, [8, S5_PAIRS])
        prm = at("prm", 201.5, [16, S5_PAIRS])
        sig_g = at("sig_g", 186, [HALVES, NC])
        q_st = at("q_st", 180, [2, HALVES, P])
        k_st = at("k_st", 182, [2, HALVES, P])
        v_st = at("v_st", 184, [2, HALVES, P])
        qT = at("qT", 186, [2, SEQ])
        kT = at("kT", 188, [2, SEQ])
        z_sb = at("z_sb", 190, [384])
        ez = at("ez", 191.5, [384])
        lz = at("lz", 193, [384])
        sp = at("sp", 194.5, [384])
        zm = at("zm", 196, [384])
        wz = at("wz", 197.5, [384])
        ws_st = at("ws_st", 199, [P])
        wsT = at("wsT", 199.5, [P])
        yb = at("yb", 200, [HALVES, P])
        xres = at("xres", 180, [HALVES, D])
        mg = at("mg", 196, [HALVES, NC])
        mt = at("mt", 200, [NC])
        mT_hi = at("mT_hi", 80, [KT, SEQ], F32R)
        mT_lo = at("mT_lo", 96, [KT, SEQ], F32R)
        mq = at("mq", 112, [HALVES, NC])
        yg = at("yg", 116, [HALVES, D])
        post_gain = at("post_gain", 132, [D])
        k_tok = at("k_tok", 140, [HALVES, XHEADS, XDIM])
        v_tok = at("v_tok", 144, [HALVES, XHEADS, XDIM])
        q_tok = at("q_tok", 148, [HALVES, XHEADS, XDIM])
        kxT = at("kxT", 152, [XHEADS, SEQ])
        qxT = at("qxT", 156, [XHEADS, SEQ])
        prob = at("prob", 160, [XHEADS, HALVES, SEQ])
        pT = at("pT", 168, [XHEADS, 2, SEQ])
        oT_hi = at("oT_hi", 176, [XHEADS, SEQ], F32R)
        oT_lo = at("oT_lo", 196, [XHEADS, SEQ], F32R)
        xsm = at("xsm", 200, [4, XHEADS * HALVES])
        hT_hi = at("hT_hi", 80, [FFN // P, SEQ], F32R)
        hT_lo = at("hT_lo", 124, [FFN // P, SEQ], F32R)
        silu_g = at("silu_g", 168, [HALVES, NC])
        hb = at("hb", 172, [HALVES, NC])
        yg3 = at("yg3", 48, [HALVES, D])
        post_gain3 = at("post_gain3", 64, [D])
        junk = at("junk", 202.5, [NC])
        ident = at("ident", 204.5, [P])
        lt = at("lt", 205, [P])
        gt = at("gt", 205.5, [P])
        le = at("le", 206, [P])
        ones = at("ones", 206.5, [P])
        cols = at("cols", 207, [P])
        ss = at("ss", 207.5, [4, HALVES, 4])
        inv = at("inv", 207.625, [8, HALVES])
        rstd = at("rstd", 207.6875, [8, HALVES])
        halfpi = at("halfpi", 207.75, [1])

        acc = ps("acc", [P, HALVES, NC])
        side = ps("side", [P, 4, NC])
        tr = ps("tr", [P, 2, NC])

        w_landed = [sem(f"w_landed{i}") for i in range(RING)]
        hi_ready, lo_ready, unit_used = sem("hi_ready"), sem("lo_ready"), sem("unit_used")
        acc0_full = sem("acc0_full")
        acc_taken = [sem("acc0_taken"), sem("acc1_taken")]
        turned, turn_hi, turn_lo = sem("turned"), sem("turn_hi"), sem("turn_lo")
        inv_ready, rstd_ready = sem("inv_ready"), sem("rstd_ready")
        act_own, dve_own, pool_own = sem("act_own"), sem("dve_own"), sem("pool_own")
        x_landed = [sem(f"x_landed{i}") for i in range(4)]
        rows_zero, rows_landed, ldt_spread = sem("rows_zero"), sem("rows_landed"), sem("ldt_spread")
        const_ready, cols_turned, cols_ready = sem("const_ready"), sem("cols_turned"), sem("cols_ready")
        bc_zero, bc_landed, vgain_landed = sem("bc_zero"), sem("bc_landed"), sem("vgain_landed")
        prm_dt, prm_ang, prm_sin, prm_ready, table_ready = (
            sem("prm_dt"), sem("prm_ang"), sem("prm_sin"), sem("prm_ready"), sem("table_ready"))
        s5_staged, s5_turned, s5_uB, s5_Cp, s5_bu = (
            sem("s5_staged"), sem("s5_turned"), sem("s5_uB"), sem("s5_Cp"), sem("s5_bu"))
        s5_x, s5_y, s5_ysb, s5_gelu, gT_hi_ready, gT_ready = (
            sem("s5_x"), sem("s5_y"), sem("s5_ysb"), sem("s5_gelu"), sem("gT_hi_ready"), sem("gT_ready"))
        gm_gelu, gm_ready, yc_ready = sem("gm_gelu"), sem("gm_ready"), sem("yc_ready")
        qkv_staged, qk_turned, qT_ready, kT_ready, z_done, z_ready, l_ready = (
            sem("qkv_staged"), sem("qk_turned"), sem("qT_ready"), sem("kT_ready"), sem("z_done"),
            sem("z_ready"), sem("l_ready"))
        sp_ready, tail_done, lw_ready, w_exp, wz_ready, ya_done, ya_hi, ya_lo = (
            sem("sp_ready"), sem("tail_done"), sem("lw_ready"), sem("w_exp"), sem("wz_ready"),
            sem("ya_done"), sem("ya_hi"), sem("ya_lo"))
        ws_landed, ws_turned, wsT_ready, mixed_done, yb_ready, yb_turned, yb_hi, yb_lo = (
            sem("ws_landed"), sem("ws_turned"), sem("wsT_ready"), sem("mixed_done"), sem("yb_ready"),
            sem("yb_turned"), sem("yb_hi"), sem("yb_lo"))
        mg_ready, xres_landed, gain_landed, mq_landed, mq_squared = (
            sem("mg_ready"), sem("xres_landed"), sem("gain_landed"), sem("mq_landed"), sem("mq_squared"))
        squared, x1_ready, x2_ready = sem("squared"), sem("x1_ready"), sem("x2_ready")
        k_turned, kx_ready, q_turned, qx_ready = sem("k_turned"), sem("kx_ready"), sem("q_turned"), sem("qx_ready")
        xz_done, xmax_ready, xexp_done, xp_ready, p_turned, pT_ready, xo_done, xo_hi, xo_lo = (
            sem("xz_done"), sem("xmax_ready"), sem("xexp_done"), sem("xp_ready"), sem("p_turned"),
            sem("pT_ready"), sem("xo_done"), sem("xo_hi"), sem("xo_lo"))
        silu_ready, hb_ready, out_ready, out_landed = (
            sem("silu_ready"), sem("hb_ready"), sem("out_ready"), sem("out_landed"))

        block = ctx.enter_context(nc.Block())

        def kview(w):
            return w.rearrange("(k p) n -> p k n", p=P)

        w_in_k, w_glu_k, wa_k, wb_k, wc_k = (kview(w[0]) for w in (w_in, s5_w_glu, w_br_a, w_br_b, w_br_c))
        w_out_k, w_xq_k, w_xkv_k, w_xo_k = (kview(w[0]) for w in (w_out, w_xq, w_xkv, w_xo))
        w_fi_k, w_fo_k = kview(w_ffn_in[0]), kview(w_ffn_out[0])
        x_v = x[0].rearrange("(h p) d -> p h d", p=P)
        mem_v = mem[0].rearrange("(h p) d -> p h d", p=P)
        out_v = out[0].rearrange("(h p) d -> p h d", p=P)

        @block.sync
        def _(sp_):
            def load(u, slot, src):
                if not isinstance(u, int) or u >= RING:
                    sp_.wait_ge(lo_ready, u - (RING - 1))
                sp_.dma_start(raw[:, slot], src).then_inc(w_landed[slot], 16)

            def load_chunk(u, j0, w, col, units, k0=0):
                for j in range(units):
                    load(u + j0 + j, (j0 + j) % RING,
                         w[:, k0 + UK * j:k0 + UK * (j + 1), bass.ds(col, NC)])

            load_chunk(U_S5, 0, w_in_k, OFF_S5, CU)
            with sp_.Fori(0, 4) as i:
                for c in range(2):
                    load_chunk(i * 16 + U_PROJ, CU * c, w_in_k, i * (2 * NC) + c * NC, CU)
            for c in range(2):
                load_chunk(U_GLU, 2 * c, w_glu_k, c * NC, 2)
            with sp_.Fori(0, 4) as i:
                for c in range(3):
                    load_chunk(i * 24 + U_GATE, CU * c, w_in_k, i * (3 * NC) + (OFF_GATES + c * NC), CU)
            with sp_.Fori(0, 4) as i:
                load_chunk(i * 8 + U_BR, 0, wa_k, i * NC, 4)
                load_chunk(i * 8 + U_BR, 4, wb_k, i * NC, 2)
                load_chunk(i * 8 + U_BR, 6, wc_k, i * NC, 2)
            with sp_.Fori(0, 4) as i:
                load_chunk(i * 8 + U_OUT, 0, w_out_k, i * NC, CU)
            load_chunk(U_MK, 0, w_xkv_k, 0, CU)
            load_chunk(U_XQ, 0, w_xq_k, 0, CU)
            load_chunk(U_MV, 0, w_xkv_k, NC, CU)
            for c in range(4):
                load_chunk(U_XO, 2 * c, w_xo_k, c * NC, 2)
            with sp_.Fori(0, 11) as i:
                load_chunk(i * 16 + U_FI, 0, w_fi_k, i * NC, CU)
                load_chunk(i * 16 + U_FI, CU, w_fi_k, i * NC + FFN, CU)
            with sp_.Fori(0, 2) as i:
                for c in range(2):
                    load_chunk(i * 44 + U_FO, 22 * c, w_fo_k, i * (2 * NC) + c * NC, 22)
            for n in range(4):
                sp_.wait_ge(out_ready, n + 1)
                sp_.dma_start(out_v[:, :, n * NC:(n + 1) * NC], xres[:, :, n * NC:(n + 1) * NC]).then_inc(out_landed, 16)
            sp_.wait_ge(out_landed, 64)

        @block.gpsimd
        def _(pool):
            own = Chain(pool, pool_own)
            g = nc.gpsimd
            g.memset(rows[:], 0.0).then_inc(rows_zero, 1)
            g.memset(Bn[:], 0.0).then_inc(bc_zero, 1)
            g.memset(Cn[:], 0.0).then_inc(bc_zero, 1)
            g.memset(halfpi[:], math.pi / 2).then_inc(const_ready, 1)
            own.link(g.memset(ident[:], 0.0))
            g.affine_select(out=ident[:], in_=ident[:], compare_op=ALU.not_equal, fill=1.0, base=0,
                            pattern=[[-1, P]], channel_multiplier=1).then_inc(const_ready, 1)
            own.link(g.memset(ones[:], 1.0))
            g.affine_select(out=lt[:], in_=ones[:], compare_op=ALU.is_gt, fill=0.0, base=0,
                            pattern=[[1, P]], channel_multiplier=-1).then_inc(const_ready, 1)
            g.affine_select(out=gt[:], in_=ones[:], compare_op=ALU.is_gt, fill=0.0, base=0,
                            pattern=[[-1, P]], channel_multiplier=1).then_inc(const_ready, 1)
            g.affine_select(out=le[:], in_=ones[:], compare_op=ALU.is_ge, fill=0.0, base=0,
                            pattern=[[1, P]], channel_multiplier=-1).then_inc(const_ready, 1)
            pool.wait_ge(bc_zero, 2)
            for r, b in enumerate((s5_b_re, s5_b_im)):
                bv = b[0].rearrange("(q e) n c -> e n q c", e=2)
                for e in range(2):
                    g.dma_start(Bn[e * STATE:(e + 1) * STATE, :, r, e * GCH:(e + 1) * GCH], bv[e]).then_inc(bc_landed, 16)
            for r, c_ in enumerate((s5_c_re, s5_c_im)):
                cv = c_[0].rearrange("(t q e) c n -> q e c t n", q=4, e=2)
                for q in range(4):
                    for e in range(2):
                        p0 = q * 32 + e * GCH
                        g.dma_start(Cn[p0:p0 + GCH, :, r, e * STATE:(e + 1) * STATE], cv[q, e]).then_inc(bc_landed, 16)

            pool.wait_ge(prm_sin, 1)
            own.link(g.memset(cosT[:, :, 0:1], 1.0))
            own.link(g.memset(sinT[:, :, 0:1], 0.0))
            for k in range(8):
                L = 1 << k
                c_, s_ = cosT[:, :, 0:L], sinT[:, :, 0:L]
                ck = cosA[:, k, :].unsqueeze(2).to_broadcast([P, S5_PAIRS, L])
                sk = sinA[:, k, :].unsqueeze(2).to_broadcast([P, S5_PAIRS, L])
                a, b = tabA[:, :, 0:L], tabB[:, :, 0:L]
                g.tensor_tensor(a, c_, ck, ALU.mult)
                own.link(g.tensor_tensor(b, s_, sk, ALU.mult))
                own.link(g.tensor_tensor(cosT[:, :, L:2 * L], a, b, ALU.subtract))
                g.tensor_tensor(a, c_, sk, ALU.mult)
                own.link(g.tensor_tensor(b, s_, ck, ALU.mult))
                last = g.tensor_tensor(sinT[:, :, L:2 * L], a, b, ALU.add)
                if k < 7:
                    own.link(last)
                else:
                    last.then_inc(table_ready, 1)

            def stage_s5(i):
                g.tensor_copy(u_st[:], s5u[:, bass.ds(i, 1)].rearrange("p o h c -> p (o h) c"))
                for r in range(2):
                    g.tensor_copy(B_st[:, r], Bn[:, bass.ds(i * 4, 4), r, :])
                g.tensor_copy(C_st[:], Cn[:, bass.ds(i, 1)].rearrange("p o r c -> p (o r) c")).then_inc(s5_staged, 1)

            for h in range(HALVES):
                pool.wait_ge(acc_taken[h], G_S5 + 1)
            pool.wait_ge(bc_landed, 16 * 20)
            stage_s5(0)
            with pool.Fori(1, S5_TILES) as i:
                pool.wait_ge(s5_turned, i)
                stage_s5(i)

            def stage_head(i):
                for dst, blk in ((q_st, 0), (k_st, 8), (v_st, 16)):
                    last = g.tensor_copy(dst[:], proj[:, bass.ds(i * 2 + blk, 2)])
                last.then_inc(qkv_staged, 1)

            def load_ws(i):
                g.dma_start(ws_st[:], gm_w_s[0][bass.ds(i, 1)].rearrange("o t s -> (o t) s")).then_inc(ws_landed, 16)

            for h in range(HALVES):
                pool.wait_ge(acc_taken[h], G_GATE)
            pool.wait_ge(yc_ready, 1)
            stage_head(0)
            load_ws(0)
            with pool.Fori(1, HEADS) as i:
                pool.wait_ge(ya_done, i)
                stage_head(i)
                pool.wait_ge(ws_turned, i)
                load_ws(i)

            pool.wait_ge(yb_lo, 4)
            pool.wait_ge(ya_lo, 4)
            g.dma_start(xres[:], x_v).then_inc(xres_landed, 16)

            def load_mem(i):
                g.dma_start(mq[:], mem_v[:, :, bass.ds(i * NC, NC)]).then_inc(mq_landed, 16)

            load_mem(0)
            pool.wait_ge(mg_ready, 4)
            g.dma_start(post_gain[:], mix_post_gain[0:1].to_broadcast([P, D])).then_inc(gain_landed, 16)
            with pool.Fori(1, 4) as i:
                pool.wait_ge(mq_squared, i)
                load_mem(i)
            for h in range(HALVES):
                pool.wait_ge(acc_taken[h], G_OUT + 4)
            g.dma_start(post_gain[:], xattn_post_gain[0:1].to_broadcast([P, D])).then_inc(gain_landed, 16)
            pool.wait_ge(unit_used, U_FO)
            g.dma_start(post_gain3[:], ffn_post_gain[0:1].to_broadcast([P, D])).then_inc(gain_landed, 16)

        @block.scalar
        def _(act):
            own = Chain(act, act_own)
            a_ = nc.scalar

            def r_of(n, h):
                return rstd[:, n, h:h + 1]

            def split(ub, qb, j):
                u = ub + j
                if isinstance(u, int) and u >= U_END:
                    return
                act.wait_ge(w_landed[j % RING], (qb + j // RING + 1) * 16)
                if not isinstance(u, int) or u >= RING:
                    act.wait_ge(unit_used, u - (RING - 1))
                a_.activation(w_hi[:, j % RING], raw[:, j % RING], ACT.Copy).then_inc(hi_ready, 1)

            def wait_acc(h, g, u_last):
                if h == 0:
                    act.wait_ge(acc0_full, g + 1)
                else:
                    act.wait_ge(unit_used, u_last + 1)

            def take(g, u_last, dst, func, norm=None):
                for h in range(HALVES):
                    wait_acc(h, g, u_last)
                    src = acc[:, h]
                    d = dst(h)
                    if len(d.shape) == 3:
                        src = src.rearrange("p (b c) -> p b c", c=P)
                    a_.activation(d, src, func, scale=r_of(norm, h) if norm is not None else 1.0).then_inc(acc_taken[h], 1)

            def square(g, u_last, n, col, before):
                for h in range(HALVES):
                    wait_acc(h, g, u_last)
                    a_.activation(junk[:], acc[:, h], ACT.Square,
                                  accum_out=ss[:, n % 4, h, bass.ds(col, 1)]).then_inc(squared, 1)
                    act.wait_ge(squared, before + (h + 1))

            def square_quarter(n, quarter, before):
                for h in range(HALVES):
                    a_.activation(junk[:], xres[:, h, quarter * NC:(quarter + 1) * NC], ACT.Square,
                                  accum_out=ss[:, n % 4, h, quarter:quarter + 1]).then_inc(squared, 1)
                    act.wait_ge(squared, before + h + 1)

            def turn_hi_parts(t, dst, k0, gain=None):
                for b in range(2):
                    act.wait_ge(turned, t + b + 1)
                    if gain is None:
                        last = a_.activation(dst[:, bass.ds(k0 + 2 * b, 2)].rearrange("p k t -> p (k t)"), tr[:, b], ACT.Copy)
                    else:
                        for k in range(2):
                            last = a_.activation(dst[:, bass.ds(k0 + (2 * b + k), 1)].rearrange("p k t -> p (k t)"),
                                                 tr[:, b, k * SEQ:(k + 1) * SEQ], ACT.Copy,
                                                 scale=cols[:, bass.ds(k0 + (gain + 2 * b + k), 1)])
                    last.then_inc(turn_hi, 1)

            def root(n, k):
                act.wait_ge(inv_ready, k + 1)
                a_.activation(rstd[:, n], inv[:, n], ACT.Sqrt).then_inc(rstd_ready, 1)

            act.wait_ge(rows_zero, 1)
            for r0, v in ((C_MIX, mix_pre_gain), (C_XAT, xattn_pre_gain), (C_MEM, mem_gain), (C_FFN, ffn_pre_gain)):
                act.dma_start(rows[r0:r0 + KT, :], v[0].rearrange("(k p) -> k p", p=P)).then_inc(rows_landed, 16)
            act.dma_start(junk[C_LDT:C_LDT + S5_PAIRS, 0:2], s5_log_dt[0].rearrange("(q e) -> q e", e=2)).then_inc(rows_landed, 16)
            for r0, v in ((C_LRE, s5_lam_re), (C_LIM, s5_lam_im)):
                act.dma_start(rows[r0:r0 + S5_PAIRS, :].rearrange("q (e n) -> q e n", e=2),
                              v[0].rearrange("(q e) n -> q e n", e=2)).then_inc(rows_landed, 16)
            act.dma_start(rows[C_D:C_D + 4, :], s5_d[0].rearrange("(k p) -> k p", p=P)).then_inc(rows_landed, 16)
            act.dma_start(rows[C_BS:C_BS + 4, :], gm_b_s[0]).then_inc(rows_landed, 16)
            for n in range(4):
                act.dma_start(x_tok[:, :, n * NC:(n + 1) * NC], x_v[:, :, n * NC:(n + 1) * NC]).then_inc(x_landed[n], 16)
            act.dma_start(vgain[:], gm_v_gain[0:1].to_broadcast([P, NC])).then_inc(vgain_landed, 16)

            act.wait_ge(cols_turned, 1)
            a_.activation(cols[:], side[:, 0, 0:P], ACT.Copy).then_inc(cols_ready, 1)
            act.wait_ge(cols_ready, 1)
            a_.activation(prm[:, 0], cols[:, C_LDT:C_LDT + S5_PAIRS], ACT.Exp).then_inc(prm_dt, 1)
            for n in range(4):
                turn_hi_parts(T_X + 2 * n, xT_hi, 4 * n, C_MIX)
                split(0, 0, n)
            act.wait_ge(prm_ang, 1)
            a_.activation(cosA[:], cosA[:], ACT.Sin, scale=-1.0, bias=halfpi[:])
            a_.activation(prm[:, 1], ang[:, 0], ACT.Sin, scale=0.5)
            a_.activation(sinA[:], ang[:], ACT.Sin).then_inc(prm_sin, 1)
            root(N_X, 0)
            a_.activation(prm[:, 2], prm[:, 3], ACT.Exp).then_inc(prm_sin, 1)

            for j in range(CU):
                if j == CU - 1:
                    act.wait_ge(rstd_ready, 1)
                    take(G_S5, U_S5 + j, lambda h: s5u[:, :, h, :], ACT.Copy, N_X)
                split(U_S5, 0, j + RING)

            with act.Fori(0, 4) as i:
                ub, qb = i * 16 + U_PROJ, i * 4 + U_PROJ // RING
                for j in range(16):
                    if j == 0:
                        act.wait_ge(s5_turned, i + 1)
                        a_.activation(uB[:].rearrange("p a b -> p (a b)"), side[:, 0], ACT.Copy).then_inc(s5_uB, 1)
                    if j % CU == CU - 1:
                        c = j // CU
                        take(i * 2 + (G_PROJ + c), ub + j,
                             lambda h: proj[:, bass.ds(i * 8 + 4 * c, 4), h, :], ACT.Copy, N_X)
                    if j == 15:
                        act.wait_ge(s5_ysb, i + 1)
                        a_.activation(g_sb[:], y_sb[:], ACT.Gelu_apprx_tanh).then_inc(s5_gelu, 1)
                        act.wait_ge(s5_gelu, i + 1)
                        a_.activation(gT_hi[:, bass.ds(i, 1)].rearrange("p k t -> p (k t)"), g_sb[:], ACT.Copy).then_inc(gT_hi_ready, 1)
                    split(ub, qb, j + RING)

            for j in range(4):
                if j == 0:
                    act.wait_ge(acc_taken[1], G_GLU)
                    a_.activation(proj[:, 24:32], proj[:, 24:32], ACT.Gelu_apprx_tanh).then_inc(gm_gelu, 1)
                    act.wait_ge(gm_gelu, 1)
                    for h in range(HALVES):
                        a_.activation(junk[:].rearrange("p (g c) -> p g c", c=P), proj[:, 28:32, h, :], ACT.Square,
                                      accum_out=ss[:, N_GM % 4, h, 0:1]).then_inc(squared, 1)
                        act.wait_ge(squared, h + 1)
                if j == 1:
                    take(G_GLU, U_GLU + j, lambda h: yc[:, h], ACT.Copy)
                    root(N_GM, 1)
                if j == 3:
                    take(G_GLU + 1, U_GLU + j, lambda h: sig_g[:, h], ACT.Sigmoid)
                split(U_GLU, U_GLU // RING, j + RING)

            with act.Fori(0, 4) as i:
                own.enter(i, 0, 2)
                ub, qb = i * 24 + U_GATE, i * 6 + U_GATE // RING
                for j in range(24):
                    if j == 1:
                        act.wait_ge(qk_turned, i + 1)
                        a_.activation(qT[:].rearrange("p a b -> p (a b)"), side[:, 0], ACT.Copy).then_inc(qT_ready, 1)
                    if j == 3:
                        act.wait_ge(z_done, i + 1)
                        a_.activation(z_sb[:], side[:, 2, 0:384], ACT.Copy, scale=HDIM ** -0.5).then_inc(z_ready, 1)
                        act.wait_ge(z_ready, i + 1)
                        own.link(a_.activation(ez[:], z_sb[:], ACT.Abs))
                        own.link(a_.activation(ez[:], ez[:], ACT.Exp, scale=-1.0))
                        a_.activation(lz[:], ez[:], ACT.Ln, bias=1.0).then_inc(l_ready, 1)
                    if j == 8:
                        act.wait_ge(lw_ready, i + 1)
                        a_.activation(wz[:], zm[:], ACT.Exp).then_inc(w_exp, 1)
                    if j == 11:
                        act.wait_ge(ya_done, i + 1)
                        a_.activation(yaT_hi[:, bass.ds(i * 2, 2)].rearrange("p k t -> p (k t)"), side[:, 0], ACT.Copy).then_inc(ya_hi, 1)
                    if j == 17:
                        act.wait_ge(yb_turned, i + 1)
                        a_.activation(ybT_hi[:, bass.ds(i, 1)].rearrange("p k t -> p (k t)"), side[:, 1, 0:SEQ], ACT.Copy).then_inc(yb_hi, 1)
                    if j % CU == CU - 1:
                        c = j // CU
                        take(i * 3 + (G_GATE + c), ub + j,
                             lambda h: gates[:, bass.ds(i * 3 + c, 1), h, :].rearrange("p o n -> p (o n)"), ACT.Sigmoid, N_X)
                    split(ub, qb, j + RING)
                own.leave(4)
            turn_hi_parts(T_GLU, ycT_hi, 0)

            def branches(i, before):
                ub, qb = i * 8 + U_BR, i * 2 + U_BR // RING
                for j in range(8):
                    if j == 1 and before:
                        turn_hi_parts(i * 2 + (T_BR - 2), xT_hi, i * 4 - 4)
                    split(ub, qb, j + RING)

            branches(0, False)
            with act.Fori(1, 4) as i:
                branches(i, True)
            turn_hi_parts(T_BR + 6, xT_hi, 12)

            with act.Fori(0, 4) as i:
                own.enter(i, 0, 1)
                ub, qb = i * 8 + U_OUT, i * 2 + U_OUT // RING
                for j in range(8):
                    if j == 1:
                        for b in range(2):
                            act.wait_ge(turned, i * 2 + (T_MEM + b + 1))
                            for k in range(2):
                                kk = i * 4 + (2 * b + k)
                                last = a_.activation(mT_hi[:, bass.ds(kk, 1)].rearrange("p k t -> p (k t)"),
                                                     tr[:, b, k * SEQ:(k + 1) * SEQ], ACT.Copy,
                                                     scale=cols[:, bass.ds(kk + C_MEM, 1)])
                            last.then_inc(turn_hi, 1)
                    if j == 3:
                        act.wait_ge(mq_landed, (i + 1) * 16)
                        own.link(a_.activation(junk[:], mq[:, 0], ACT.Square, accum_out=ss[:, N_MEM % 4, 0, bass.ds(i, 1)]))
                        a_.activation(junk[:], mq[:, 1], ACT.Square, accum_out=ss[:, N_MEM % 4, 1, bass.ds(i, 1)]).then_inc(mq_squared, 1)
                        act.wait_ge(mq_squared, i + 1)
                    if j == 7:
                        square(i + G_OUT, ub + j, N_Y1, i, i * 2 + 2)
                    split(ub, qb, j + RING)
                own.leave(4)

            for j in range(CU):
                if j == 0:
                    root(N_Y1, 2)
                if 3 <= j < 7:
                    turn_hi_parts(T_X1 + 2 * (j - 3), xT_hi, 4 * (j - 3), C_XAT)
                if j == 6:
                    root(N_MEM, 3)
                if j == 7:
                    act.wait_ge(rstd_ready, 4)
                    take(G_MK, U_MK + j, lambda h: k_tok[:, h].rearrange("p a b -> p (a b)"), ACT.Copy, N_MEM)
                split(U_MK, U_MK // RING, j + RING)
            for j in range(CU):
                if j < 4:
                    square_quarter(N_X1, j, 10 + 2 * j)
                if j == 2:
                    act.wait_ge(k_turned, 1)
                    a_.activation(kxT[:, 0:2].rearrange("p a b -> p (a b)"), side[:, 0], ACT.Copy).then_inc(kx_ready, 1)
                if j == 5:
                    root(N_X1, 4)
                if j == 7:
                    act.wait_ge(rstd_ready, 5)
                    take(G_XQ, U_XQ + j, lambda h: q_tok[:, h].rearrange("p a b -> p (a b)"), ACT.Copy, N_X1)
                split(U_XQ, U_XQ // RING, j + RING)
            def exps(heads):
                for hd in heads:
                    for h in range(HALVES):
                        c = hd * HALVES + h
                        last = a_.activation(prob[:, hd, h], side[:, hd, h * SEQ:(h + 1) * SEQ], ACT.Exp,
                                             scale=XDIM ** -0.5, bias=xsm[:, 1, c:c + 1], accum_out=xsm[:, 2, c:c + 1])
                    last.then_inc(xexp_done, 1)

            for j in range(CU):
                if j == 1:
                    act.wait_ge(q_turned, 1)
                    a_.activation(qxT[:, 0:2].rearrange("p a b -> p (a b)"), side[:, 0], ACT.Copy).then_inc(qx_ready, 1)
                if j == 4:
                    act.wait_ge(xmax_ready, 1)
                    exps((0, 1))
                if j == 5:
                    exps((2, 3))
                if j == 7:
                    take(G_MV, U_MV + j, lambda h: v_tok[:, h].rearrange("p a b -> p (a b)"), ACT.Copy, N_MEM)
                    for hd in range(2):
                        act.wait_ge(p_turned, hd + 1)
                        a_.activation(pT[:, hd].rearrange("p a b -> p (a b)"), side[:, hd], ACT.Copy).then_inc(pT_ready, 1)
                    for b in range(2):
                        act.wait_ge(xo_done, b + 1)
                        a_.activation(oT_hi[:, 2 * b:2 * b + 2].rearrange("p a b -> p (a b)"), tr[:, b], ACT.Copy).then_inc(xo_hi, 1)
                split(U_MV, U_MV // RING, j + RING)
            for j in range(8):
                if j % 2:
                    square(G_XO + j // 2, U_XO + j, N_Y2, j // 2, 18 + j - 1)
                split(U_XO, U_XO // RING, j + RING)
            root(N_Y2, 5)
            for n in range(4):
                turn_hi_parts(T_X2 + 2 * n, xT_hi, 4 * n, C_FFN)

            def ffn_in(i, first):
                ub, qb = i * 16 + U_FI, i * 4 + U_FI // RING
                for j in range(16):
                    if first and j < 4:
                        square_quarter(N_X2, j, 26 + 2 * j)
                    if first and j == 5:
                        root(N_X2, 6)
                    if not first and j == 2:
                        turn_hi_parts(i * 2 + (T_FFN - 2), hT_hi, i * 4 - 4)
                    if j == 7:
                        if first:
                            act.wait_ge(rstd_ready, 7)
                        for h in range(HALVES):
                            wait_acc(h, i * 2 + G_FI, ub + j)
                            a_.activation(silu_g[:, h], acc[:, h], ACT.Silu, scale=r_of(N_X2, h)).then_inc(acc_taken[h], 1)
                    split(ub, qb, j + RING)

            ffn_in(0, True)
            with act.Fori(1, 11) as i:
                ffn_in(i, False)
            turn_hi_parts(T_FFN + 20, hT_hi, 40)

            for n in range(4):
                for j in range(22 * n, 22 * n + 22):
                    if j == 22 * n + 21:
                        square(G_FO + n, U_FO + j, N_Y3, n, 34 + 2 * n)
                    split(U_FO, U_FO // RING, j + RING)
            root(N_Y3, 7)

        @block.vector
        def _(dve):
            own = Chain(dve, dve_own)
            v_ = nc.vector

            def split(ub, j):
                u = ub + j
                if isinstance(u, int) and u >= U_END:
                    return
                s = j % RING
                dve.wait_ge(hi_ready, u + 1)
                v_.tensor_tensor(w_lo[:, s], raw[:, s], w_hi[:, s].bitcast(F32), ALU.subtract).then_inc(lo_ready, 1)

            def wait_acc(h, g, u_last):
                if h == 0:
                    dve.wait_ge(acc0_full, g + 1)
                else:
                    dve.wait_ge(unit_used, u_last + 1)

            def turn_lo_parts(t, dst_hi, dst_lo, k0, gain=None, k0_gain=None):
                for b in range(2):
                    dve.wait_ge(turn_hi, t + b + 1)
                    if gain is None:
                        ks = bass.ds(k0 + 2 * b, 2)
                        last = v_.tensor_tensor(dst_lo[:, ks].rearrange("p k t -> p (k t)"), tr[:, b],
                                                dst_hi[:, ks].rearrange("p k t -> p (k t)").bitcast(F32), ALU.subtract)
                    else:
                        for k in range(2):
                            ks = bass.ds(k0 + (2 * b + k), 1)
                            last = v_.scalar_tensor_tensor(
                                dst_lo[:, ks].rearrange("p k t -> p (k t)"), tr[:, b, k * SEQ:(k + 1) * SEQ],
                                cols[:, bass.ds(k0 + (gain + 2 * b + k), 1)],
                                dst_hi[:, ks].rearrange("p k t -> p (k t)").bitcast(F32), ALU.mult, ALU.subtract)
                    last.then_inc(turn_lo, 1)

            def inverse(n, width, squares):
                if squares:
                    dve.wait_ge(squared, squares)
                parts = 1 if n == N_GM else 4
                own.link(v_.tensor_reduce(inv[:, n], ss[:, n % 4, :, 0:parts], AX.X, ALU.add))
                own.link(v_.tensor_scalar(inv[:, n], inv[:, n], 1.0 / width, EPS, ALU.mult, ALU.add))
                v_.reciprocal(inv[:, n], inv[:, n]).then_inc(inv_ready, 1)

            def gained(g, u_last, sq, dst, gain, col):
                for h in range(HALVES):
                    dve.wait_ge(squared, sq + h)
                    v_.tensor_tensor(dst[:, h, bass.ds(col, NC)], acc[:, h], gain[:, bass.ds(col, NC)],
                                     ALU.mult).then_inc(acc_taken[h], 1)

            def residual(n, src, norm, ready):
                for h in range(HALVES):
                    q = slice(n * NC, (n + 1) * NC)
                    last = v_.scalar_tensor_tensor(xres[:, h, q], src[:, h, q], rstd[:, norm, h:h + 1],
                                                   xres[:, h, q], ALU.mult, ALU.add)
                last.then_inc(ready, 1)

            dve.wait_ge(rows_zero, 1)
            dve.wait_ge(rows_landed, 16 * 9)
            v_.tensor_copy(rows[C_LDT:C_LDT + S5_PAIRS].rearrange("q (e n) -> q e n", e=2),
                           junk[C_LDT:C_LDT + S5_PAIRS, 0:2].unsqueeze(2).to_broadcast([S5_PAIRS, 2, STATE])).then_inc(ldt_spread, 1)

            DT, S2, EX, XR, TH, KR, RR, XC, PO, MAG, F_RE, F_IM, T1, T2, T3, DEN = range(16)

            def p_(k):
                return prm[:, k]

            lre, lim = cols[:, C_LRE:C_LRE + S5_PAIRS], cols[:, C_LIM:C_LIM + S5_PAIRS]
            dve.wait_ge(prm_dt, 1)
            v_.tensor_tensor(p_(XR), lre, p_(DT), ALU.mult)
            own.link(v_.tensor_tensor(p_(TH), lim, p_(DT), ALU.mult))
            for k in range(8):
                src = p_(TH)
                if k:
                    own.link(v_.tensor_scalar(p_(TH), ang[:, k - 1], 2.0, None, ALU.mult))
                own.link(v_.tensor_scalar(p_(KR), src, 1 / TWO_PI, ROUND, ALU.mult, ALU.add))
                own.link(v_.tensor_scalar(p_(KR), p_(KR), -ROUND, None, ALU.add))
                own.link(v_.scalar_tensor_tensor(p_(RR), p_(KR), -PI_A, src, ALU.mult, ALU.add))
                own.link(v_.scalar_tensor_tensor(p_(RR), p_(KR), -PI_B, p_(RR), ALU.mult, ALU.add))
                own.link(v_.scalar_tensor_tensor(p_(RR), p_(KR), -PI_C, p_(RR), ALU.mult, ALU.add))
                own.link(v_.tensor_scalar(ang[:, k], p_(RR), PI_MAX, -PI_MAX, ALU.min, ALU.max))
            v_.scalar_tensor_tensor(cosA[:], ang[:], -1.0, ang[:], ALU.mult, ALU.max).then_inc(prm_ang, 1)

            for n in range(4):
                dve.wait_ge(x_landed[n], 16)
                for h in range(HALVES):
                    q = x_tok[:, h, n * NC:(n + 1) * NC]
                    own.link(v_.tensor_tensor_reduce(junk[:], q, q, 1.0, 0.0, ALU.mult, ALU.add, ss[:, N_X % 4, h, n:n + 1]))
                turn_lo_parts(T_X + 2 * n, xT_hi, xT_lo, 4 * n, C_MIX)
                split(0, n)
            inverse(N_X, D, 0)

            dve.wait_ge(prm_sin, 2)
            own.link(v_.tensor_scalar(p_(XC), p_(XR), 0.5, -0.5, ALU.min, ALU.max))
            own.link(v_.tensor_scalar(p_(PO), p_(XC), 1.0 / 10, 1.0, ALU.mult, ALU.add))
            for k in range(9, 1, -1):
                own.link(v_.scalar_tensor_tensor(p_(PO), p_(PO), 1.0 / k, p_(XC), ALU.mult, ALU.mult))
                own.link(v_.tensor_scalar(p_(PO), p_(PO), 1.0, None, ALU.add))
            own.link(v_.tensor_tensor(p_(PO), p_(PO), p_(XC), ALU.mult))
            own.link(v_.tensor_tensor(p_(T1), p_(XC), p_(XR), ALU.not_equal))
            own.link(v_.scalar_tensor_tensor(p_(T2), p_(EX), -1.0, p_(PO), ALU.add, ALU.subtract))
            own.link(v_.tensor_tensor(p_(T2), p_(T2), p_(T1), ALU.mult))
            own.link(v_.tensor_tensor(p_(PO), p_(PO), p_(T2), ALU.add))
            own.link(v_.tensor_scalar(p_(MAG), p_(PO), 1.0, None, ALU.add))
            own.link(v_.tensor_tensor(p_(T1), p_(PO), cosA[:, 0], ALU.mult))
            own.link(v_.scalar_tensor_tensor(p_(T2), p_(S2), -2.0, p_(S2), ALU.mult, ALU.mult))
            own.link(v_.tensor_tensor(p_(T1), p_(T1), p_(T2), ALU.add))
            own.link(v_.tensor_tensor(p_(T2), p_(MAG), sinA[:, 0], ALU.mult))
            own.link(v_.tensor_tensor(p_(DEN), lre, lre, ALU.mult))
            own.link(v_.tensor_tensor(p_(T3), lim, lim, ALU.mult))
            own.link(v_.tensor_tensor(p_(DEN), p_(DEN), p_(T3), ALU.add))
            own.link(v_.reciprocal(p_(DEN), p_(DEN)))
            own.link(v_.tensor_tensor(p_(F_RE), p_(T1), lre, ALU.mult))
            own.link(v_.tensor_tensor(p_(T3), p_(T2), lim, ALU.mult))
            own.link(v_.tensor_tensor(p_(F_RE), p_(F_RE), p_(T3), ALU.add))
            own.link(v_.tensor_tensor(p_(F_RE), p_(F_RE), p_(DEN), ALU.mult))
            own.link(v_.tensor_tensor(p_(F_IM), p_(T2), lre, ALU.mult))
            own.link(v_.tensor_tensor(p_(T3), p_(T1), lim, ALU.mult))
            own.link(v_.tensor_tensor(p_(F_IM), p_(F_IM), p_(T3), ALU.subtract))
            own.link(v_.tensor_tensor(p_(F_IM), p_(F_IM), p_(DEN), ALU.mult))

            for j in range(CU):
                split(U_S5, j + RING)
            dve.wait_ge(table_ready, 1)

            with dve.Fori(0, 4) as i:
                own.enter(i, 0, 9)
                ub = i * 16 + U_PROJ
                b_re, b_im = side[:, :, 0:SEQ], side[:, :, SEQ:2 * SEQ]
                ct, st = cosT[:, bass.ds(i * 4, 4)], sinT[:, bass.ds(i * 4, 4)]

                def mul(o, a, b):
                    return v_.tensor_tensor(o, a, b, ALU.mult)

                for j in range(16):
                    if j == 1:
                        dve.wait_ge(s5_turned, i + 1)
                        fr = prm[:, F_RE, bass.ds(i * 4, 4)].unsqueeze(2).to_broadcast([P, 4, 32])
                        fi = prm[:, F_IM, bass.ds(i * 4, 4)].unsqueeze(2).to_broadcast([P, 4, 32])
                        cr = tr[:, 0, 0:P].rearrange("p (q c) -> p q c", q=4)
                        ci = tr[:, 0, P:2 * P].rearrange("p (q c) -> p q c", q=4)
                        t = [m1[:, k, 0:P].rearrange("p (q c) -> p q c", q=4) for k in range(4)]
                        mul(t[0], cr, fr)
                        mul(t[1], ci, fi)
                        mul(t[2], cr, fi)
                        own.link(mul(t[3], ci, fr))
                        v_.tensor_tensor(Cp[:, 0], m1[:, 0, 0:P], m1[:, 1, 0:P], ALU.subtract)
                        v_.scalar_tensor_tensor(Cp[:, 1], m1[:, 2, 0:P], -1.0, m1[:, 3, 0:P], ALU.mult, ALU.subtract).then_inc(s5_Cp, 1)
                    if j == 2:
                        dve.wait_ge(s5_Cp, i + 1)
                        dve.wait_ge(s5_bu, i + 1)
                        mul(m1[:], b_re, ct)
                    if j == 3:
                        own.link(mul(m2[:], b_im, st))
                    if j == 4:
                        own.link(v_.tensor_tensor(v_re[:], m1[:], m2[:], ALU.add))
                    if j == 5:
                        mul(m1[:], b_im, ct)
                        own.link(mul(m2[:], b_re, st))
                    if j == 6:
                        own.link(v_.tensor_tensor(v_im[:], m1[:], m2[:], ALU.subtract))
                    if 7 <= j < 11:
                        q = j - 7
                        mag = prm[:, MAG, bass.ds(i * 4 + q, 1)].to_broadcast([P, SEQ])
                        v_.tensor_tensor_scan(v_re[:, q], mag, v_re[:, q], 0.0, ALU.mult, ALU.add)
                        last = v_.tensor_tensor_scan(v_im[:, q], mag, v_im[:, q], 0.0, ALU.mult, ALU.add)
                        if j == 10:
                            own.link(last)
                    if j == 11:
                        mul(m1[:], v_re[:], ct)
                    if j == 12:
                        own.link(mul(m2[:], v_im[:], st))
                    if j == 13:
                        own.link(v_.tensor_tensor(m1[:], m1[:], m2[:], ALU.subtract))
                        mul(m2[:], v_re[:], st)
                    if j == 14:
                        own.link(mul(v_im[:], v_im[:], ct))
                        v_.tensor_tensor(v_im[:], v_im[:], m2[:], ALU.add).then_inc(s5_x, 1)
                    if j == 15:
                        dve.wait_ge(s5_y, i + 1)
                        v_.scalar_tensor_tensor(y_sb[:], uB[:, 0], cols[:, bass.ds(i + C_D, 1)], tr[:, 1, 0:SEQ],
                                                ALU.mult, ALU.add).then_inc(s5_ysb, 1)
                        dve.wait_ge(gT_hi_ready, i + 1)
                        k1 = bass.ds(i, 1)
                        v_.tensor_tensor(gT_lo[:, k1].rearrange("p k t -> p (k t)"), g_sb[:],
                                         gT_hi[:, k1].rearrange("p k t -> p (k t)").bitcast(F32), ALU.subtract).then_inc(gT_ready, 1)
                    split(ub, j + RING)
                own.leave(4)

            for j in range(4):
                if j == 1:
                    inverse(N_GM, NC, 2)
                if j == 2:
                    dve.wait_ge(rstd_ready, 2)
                    dve.wait_ge(vgain_landed, 16)
                    for h in range(HALVES):
                        pv = proj[:, 28:32, h, :]
                        last = v_.scalar_tensor_tensor(pv, pv, rstd[:, N_GM, h:h + 1],
                                                       vgain[:].rearrange("p (g c) -> p g c", c=P), ALU.mult, ALU.mult)
                    last.then_inc(gm_ready, 1)
                if j == 3:
                    for h in range(HALVES):
                        dve.wait_ge(acc_taken[h], G_GATE)
                    v_.tensor_tensor(yc[:], yc[:], sig_g[:], ALU.mult).then_inc(yc_ready, 1)
                split(U_GLU, j + RING)

            with dve.Fori(0, 4) as i:
                own.enter(i, 0, 2)
                ub = i * 24 + U_GATE
                for j in range(24):
                    if j == 1:
                        dve.wait_ge(qk_turned, i + 1)
                        v_.tensor_copy(kT[:].rearrange("p a b -> p (a b)"), side[:, 1]).then_inc(kT_ready, 1)
                    if j == 4:
                        dve.wait_ge(l_ready, i + 1)
                        own.link(v_.scalar_tensor_tensor(sp[:], z_sb[:], 0.0, lz[:], ALU.max, ALU.add))
                        own.link(v_.tensor_tensor(zm[:], z_sb[:], sp[:], ALU.subtract))
                        v_.tensor_tensor(sp[:, 0:P], sp[:, 0:P], lt[:], ALU.mult)
                        v_.tensor_tensor(sp[:, SEQ:], sp[:, SEQ:], lt[:], ALU.mult).then_inc(sp_ready, 1)
                    if j == 7:
                        dve.wait_ge(tail_done, i + 1)
                        v_.tensor_tensor(zm[:], zm[:], side[:, 3, 0:384], ALU.subtract).then_inc(lw_ready, 1)
                    if j == 9:
                        dve.wait_ge(w_exp, i + 1)
                        v_.tensor_tensor(wz[:, 0:P], wz[:, 0:P], lt[:], ALU.mult)
                        v_.tensor_tensor(wz[:, SEQ:], wz[:, SEQ:], lt[:], ALU.mult).then_inc(wz_ready, 1)
                    if j == 12:
                        dve.wait_ge(ya_hi, i + 1)
                        k2 = bass.ds(i * 2, 2)
                        v_.tensor_tensor(yaT_lo[:, k2].rearrange("p k t -> p (k t)"), side[:, 0],
                                         yaT_hi[:, k2].rearrange("p k t -> p (k t)").bitcast(F32), ALU.subtract).then_inc(ya_lo, 1)
                    if j == 13:
                        dve.wait_ge(ws_turned, i + 1)
                        v_.tensor_tensor(wsT[:], side[:, 1, 0:P], le[:], ALU.mult).then_inc(wsT_ready, 1)
                    if j == 15:
                        dve.wait_ge(mixed_done, i + 1)
                        v_.scalar_tensor_tensor(yb[:], side[:, 1, P:3 * P].rearrange("p (h c) -> p h c", h=2),
                                                cols[:, bass.ds(i + C_BS, 1)],
                                                proj[:, bass.ds(i + 24, 1)].rearrange("p o h c -> p (o h) c"),
                                                ALU.add, ALU.mult).then_inc(yb_ready, 1)
                    if j == 18:
                        dve.wait_ge(yb_hi, i + 1)
                        k1 = bass.ds(i, 1)
                        v_.tensor_tensor(ybT_lo[:, k1].rearrange("p k t -> p (k t)"), side[:, 1, 0:SEQ],
                                         ybT_hi[:, k1].rearrange("p k t -> p (k t)").bitcast(F32), ALU.subtract).then_inc(yb_lo, 1)
                    split(ub, j + RING)
                own.leave(4)
            turn_lo_parts(T_GLU, ycT_hi, ycT_lo, 0)

            def branches(i, before):
                ub = i * 8 + U_BR
                for j in range(8):
                    if j == 1 and before:
                        turn_lo_parts(i * 2 + (T_BR - 2), xT_hi, xT_lo, i * 4 - 4)
                    if j in (3, 5, 7):
                        br = (j - 3) // 2
                        for h in range(HALVES):
                            wait_acc(h, i * 3 + (G_BR + br), ub + j)
                            if br == 0 and h == 0:
                                dve.wait_ge(acc_taken[1], G_BR)
                            gate = gates[:, bass.ds(i + 4 * br, 1), h].rearrange("p o n -> p (o n)")
                            if br == 0:
                                v_.tensor_tensor(mg[:, h], acc[:, h], gate, ALU.mult).then_inc(acc_taken[h], 1)
                            else:
                                v_.tensor_tensor(mt[:], acc[:, h], gate, ALU.mult).then_inc(acc_taken[h], 1)
                                dve.wait_ge(acc_taken[h], i * 3 + (G_BR + br + 1))
                                last = v_.tensor_tensor(mg[:, h], mg[:, h], mt[:], ALU.add)
                                if br == 2 and h == 1:
                                    last.then_inc(mg_ready, 1)
                                    dve.wait_ge(mg_ready, i + 1)
                                else:
                                    own.link(last)
                    split(ub, j + RING)

            branches(0, False)
            with dve.Fori(1, 4) as i:
                own.enter(i, 1, 3)
                branches(i, True)
                own.leave(3)
            turn_lo_parts(T_BR + 6, xT_hi, xT_lo, 12)

            with dve.Fori(0, 4) as i:
                ub = i * 8 + U_OUT
                for j in range(8):
                    if j == 1:
                        for b in range(2):
                            dve.wait_ge(turn_hi, i * 2 + (T_MEM + b + 1))
                            for k in range(2):
                                kk = i * 4 + (2 * b + k)
                                last = v_.scalar_tensor_tensor(
                                    mT_lo[:, bass.ds(kk, 1)].rearrange("p k t -> p (k t)"), tr[:, b, k * SEQ:(k + 1) * SEQ],
                                    cols[:, bass.ds(kk + C_MEM, 1)],
                                    mT_hi[:, bass.ds(kk, 1)].rearrange("p k t -> p (k t)").bitcast(F32), ALU.mult, ALU.subtract)
                            last.then_inc(turn_lo, 1)
                    if j == 7:
                        dve.wait_ge(gain_landed, 16)
                        gained(None, None, i * 2 + 3, yg, post_gain, i * NC)
                    split(ub, j + RING)

            inverse(N_Y1, D, 10)
            for j in range(CU):
                if j == 0:
                    dve.wait_ge(rstd_ready, 3)
                    dve.wait_ge(xres_landed, 16)
                if 1 <= j < 5:
                    residual(j - 1, yg, N_Y1, x1_ready)
                if 3 <= j < 7:
                    turn_lo_parts(T_X1 + 2 * (j - 3), xT_hi, xT_lo, 4 * (j - 3), C_XAT)
                if j == 5:
                    dve.wait_ge(mq_squared, 4)
                    inverse(N_MEM, D, 0)
                split(U_MK, j + RING)
            for j in range(CU):
                if j == 2:
                    dve.wait_ge(k_turned, 2)
                    v_.tensor_copy(kxT[:, 2:4].rearrange("p a b -> p (a b)"), side[:, 1]).then_inc(kx_ready, 1)
                if j == 4:
                    inverse(N_X1, D, 18)
                split(U_XQ, j + RING)
            MX, NB, SUM, INV = range(4)
            for j in range(CU):
                if j == 1:
                    dve.wait_ge(q_turned, 2)
                    v_.tensor_copy(qxT[:, 2:4].rearrange("p a b -> p (a b)"), side[:, 1]).then_inc(qx_ready, 1)
                if j == 3:
                    dve.wait_ge(xz_done, 1)
                    own.link(v_.tensor_reduce(xsm[:, MX], side[:].rearrange("p a (h m) -> p (a h) m", h=2), AX.X, ALU.max))
                    v_.tensor_scalar(xsm[:, NB], xsm[:, MX], -(XDIM ** -0.5), None, ALU.mult).then_inc(xmax_ready, 1)
                if j in (5, 6):
                    for hd in (0, 1) if j == 5 else (2, 3):
                        dve.wait_ge(xexp_done, hd + 1)
                        own.link(v_.reciprocal(xsm[:, INV, 2 * hd:2 * hd + 2], xsm[:, SUM, 2 * hd:2 * hd + 2]))
                        for h in range(HALVES):
                            last = v_.tensor_scalar(prob[:, hd, h], prob[:, hd, h], xsm[:, INV, 2 * hd + h:2 * hd + h + 1], None, ALU.mult)
                        last.then_inc(xp_ready, 1)
                if j == 7:
                    for hd in range(2, 4):
                        dve.wait_ge(p_turned, hd + 1)
                        v_.tensor_copy(pT[:, hd].rearrange("p a b -> p (a b)"), side[:, hd]).then_inc(pT_ready, 1)
                    for b in range(2):
                        dve.wait_ge(xo_hi, b + 1)
                        v_.tensor_tensor(oT_lo[:, 2 * b:2 * b + 2].rearrange("p a b -> p (a b)"), tr[:, b],
                                         oT_hi[:, 2 * b:2 * b + 2].rearrange("p a b -> p (a b)").bitcast(F32), ALU.subtract).then_inc(xo_lo, 1)
                split(U_MV, j + RING)
            for j in range(8):
                if j % 2:
                    if j == 1:
                        dve.wait_ge(gain_landed, 32)
                    gained(None, None, 19 + 2 * (j // 2), yg, post_gain, (j // 2) * NC)
                split(U_XO, j + RING)
            inverse(N_Y2, D, 26)
            dve.wait_ge(rstd_ready, 6)
            residual(0, yg, N_Y2, x2_ready)
            for n in range(4):
                if n < 3:
                    residual(n + 1, yg, N_Y2, x2_ready)
                turn_lo_parts(T_X2 + 2 * n, xT_hi, xT_lo, 4 * n, C_FFN)

            def ffn_in(i, first):
                ub = i * 16 + U_FI
                for j in range(16):
                    if first and j == 4:
                        inverse(N_X2, D, 34)
                    if not first and j == 2:
                        turn_lo_parts(i * 2 + (T_FFN - 2), hT_hi, hT_lo, i * 4 - 4)
                    if j == 15:
                        if first:
                            dve.wait_ge(rstd_ready, 7)
                        for h in range(HALVES):
                            wait_acc(h, i * 2 + (G_FI + 1), ub + j)
                            dve.wait_ge(acc_taken[h], i * 2 + (G_FI + 1))
                            last = v_.scalar_tensor_tensor(hb[:, h], acc[:, h], rstd[:, N_X2, h:h + 1], silu_g[:, h],
                                                           ALU.mult, ALU.mult)
                            last.then_inc(acc_taken[h], 1)
                    split(ub, j + RING)

            ffn_in(0, True)
            with dve.Fori(1, 11) as i:
                ffn_in(i, False)
            turn_lo_parts(T_FFN + 20, hT_hi, hT_lo, 40)

            for n in range(4):
                for j in range(22 * n, 22 * n + 22):
                    if j == 22 * n + 21:
                        if n == 0:
                            dve.wait_ge(gain_landed, 48)
                        gained(None, None, 35 + 2 * n, yg3, post_gain3, n * NC)
                    split(U_FO, j + RING)
            inverse(N_Y3, D, 42)
            dve.wait_ge(rstd_ready, 8)
            for n in range(4):
                residual(n, yg3, N_Y3, out_ready)

        @block.tensor
        def _(pe):
            def chunk(ub, j0, g, units, hi, lo, side_step=None, first=True, last=True, k0=0, free=True):
                for j in range(units):
                    s = (j0 + j) % RING
                    pe.wait_ge(lo_ready, ub + (j0 + j + 1))
                    for h in range(HALVES):
                        if first and j == 0 and free:
                            pe.wait_ge(acc_taken[h], g)
                        tok = slice(h * P, (h + 1) * P)
                        for k in range(UK):
                            kt = k0 + UK * j + k
                            begin, end = first and j == 0 and k == 0, last and j == units - 1 and k == UK - 1
                            pe.matmul(acc[:, h], hi[:, kt, tok], w_hi[:, s, k], start=begin, stop=False)
                            pe.matmul(acc[:, h], hi[:, kt, tok], w_lo[:, s, k], start=False, stop=False)
                            mm = pe.matmul(acc[:, h], lo[:, kt, tok], w_hi[:, s, k], start=False, stop=end)
                        if h == 0 and last and j == units - 1:
                            mm.then_inc(acc0_full, 1)
                    mm.then_inc(unit_used, 1)
                    if side_step is not None:
                        side_step(j0 + j)

            def turn(t, src):
                for b in range(2):
                    if not isinstance(t, int) or t + b >= 2:
                        pe.wait_ge(turn_lo, t + (b - 1))
                    for k in range(2):
                        for h in range(HALVES):
                            c = (2 * b + k) * P
                            tt = pe.transpose(tr[:, b, k * SEQ + h * P:k * SEQ + (h + 1) * P], src[:, h, c:c + P], ident[:])
                    tt.then_inc(turned, 1)

            pe.wait_ge(const_ready, 5)
            pe.wait_ge(rows_landed, 16 * 9)
            pe.wait_ge(ldt_spread, 1)
            pe.transpose(side[:, 0, 0:P], rows[:], ident[:]).then_inc(cols_turned, 1)
            for n in range(4):
                pe.wait_ge(x_landed[n], 16)
                turn(T_X + 2 * n, x_tok[:, :, n * NC:(n + 1) * NC])
            pe.wait_ge(turn_lo, 8)
            chunk(U_S5, 0, G_S5, CU, xT_hi, xT_lo, free=False)

            with pe.Fori(0, 4) as i:
                def s5_step(j):
                    if j == 0:
                        pe.wait_ge(s5_staged, i + 1)
                        for h in range(HALVES):
                            pe.transpose(side[:, 0, h * P:(h + 1) * P], u_st[:, h], ident[:])
                        for r in range(2):
                            pe.transpose(side[:, 0, SEQ + r * P:SEQ + (r + 1) * P], B_st[:, r].rearrange("p q c -> p (q c)"), ident[:])
                            tt = pe.transpose(tr[:, 0, r * P:(r + 1) * P], C_st[:, r], ident[:])
                        tt.then_inc(s5_turned, 1)
                    if j == 1:
                        pe.wait_ge(s5_uB, i + 1)
                        for q in range(4):
                            rws = slice(32 * q, 32 * q + 32)
                            for r in range(2):
                                mm = pe.matmul(side[:, q, r * SEQ:(r + 1) * SEQ], uB[rws, 1, r * P:(r + 1) * P],
                                               uB[rws, 0, :], start=True, stop=True)
                        mm.then_inc(s5_bu, 1)
                    if j == 14:
                        pe.wait_ge(s5_x, i + 1)
                        for q in range(4):
                            rws = slice(32 * q, 32 * q + 32)
                            pe.matmul(tr[rws, 1, 0:SEQ], Cp[:, 0, rws], m1[:, q], start=True, stop=False)
                            mm = pe.matmul(tr[rws, 1, 0:SEQ], Cp[:, 1, rws], v_im[:, q], start=False, stop=True)
                        mm.then_inc(s5_y, 1)

                for c in range(2):
                    chunk(i * 16 + U_PROJ, CU * c, i * 2 + (G_PROJ + c), CU, xT_hi, xT_lo, s5_step)
            pe.wait_ge(gT_ready, 4)
            for c in range(2):
                chunk(U_GLU, 2 * c, G_GLU + c, 2, gT_hi, gT_lo)

            with pe.Fori(0, 4) as i:
                def head_step(j):
                    if j == 0:
                        pe.wait_ge(qkv_staged, i + 1)
                        for dst, src in ((0, q_st), (1, k_st)):
                            for dc in range(2):
                                for h in range(HALVES):
                                    tt = pe.transpose(side[:, dst, dc * SEQ + h * P:dc * SEQ + (h + 1) * P], src[:, dc, h], ident[:])
                        tt.then_inc(qk_turned, 1)
                    if j == 2:
                        pe.wait_ge(qT_ready, i + 1)
                        pe.wait_ge(kT_ready, i + 1)
                        for dc in range(2):
                            pe.matmul(side[:, 2, 0:SEQ], kT[:, dc, 0:P], qT[:, dc, :], start=(dc == 0), stop=(dc == 1))
                        for dc in range(2):
                            mm = pe.matmul(side[:, 2, SEQ:SEQ + P], kT[:, dc, P:], qT[:, dc, P:], start=(dc == 0), stop=(dc == 1))
                        mm.then_inc(z_done, 1)
                    if j == 5:
                        pe.wait_ge(sp_ready, i + 1)
                        pe.matmul(side[:, 3, 0:SEQ], gt[:], sp[:, 0:SEQ], start=True, stop=False)
                        pe.matmul(side[:, 3, P:SEQ], ones[:], sp[:, SEQ:], start=False, stop=True)
                        pe.matmul(side[:, 3, SEQ:SEQ + P], gt[:], sp[:, SEQ:], start=True, stop=True).then_inc(tail_done, 1)
                    if j == 10:
                        pe.wait_ge(wz_ready, i + 1)
                        for dc in range(2):
                            pe.matmul(side[:, 0, dc * SEQ:(dc + 1) * SEQ], v_st[:, dc, 0], wz[:, 0:SEQ], start=True, stop=False)
                            mm = pe.matmul(side[:, 0, dc * SEQ + P:(dc + 1) * SEQ], v_st[:, dc, 1], wz[:, SEQ:], start=False, stop=True)
                        mm.then_inc(ya_done, 1)
                    if j == 12:
                        pe.wait_ge(ws_landed, (i + 1) * 16)
                        pe.transpose(side[:, 1, 0:P], ws_st[:], ident[:]).then_inc(ws_turned, 1)
                    if j == 14:
                        pe.wait_ge(wsT_ready, i + 1)
                        for c in range(2):
                            mm = pe.matmul(side[:, 1, (1 + c) * P:(2 + c) * P], wsT[:],
                                           proj[:, bass.ds(i + 28, 1), c].rearrange("p o c -> p (o c)"), start=True, stop=True)
                        mm.then_inc(mixed_done, 1)
                    if j == 16:
                        pe.wait_ge(yb_ready, i + 1)
                        for h in range(HALVES):
                            tt = pe.transpose(side[:, 1, h * P:(h + 1) * P], yb[:, h], ident[:])
                        tt.then_inc(yb_turned, 1)

                for c in range(3):
                    chunk(i * 24 + U_GATE, CU * c, i * 3 + (G_GATE + c), CU, xT_hi, xT_lo, head_step)
            turn(T_GLU, yc[:])

            def branches(i, before):
                def step(j):
                    if j == 1 and before:
                        pe.wait_ge(mg_ready, i)
                        turn(i * 2 + (T_BR - 2), mg[:])

                ub = i * 8 + U_BR
                chunk(ub, 0, i * 3 + G_BR, 4, yaT_hi, yaT_lo, step)
                chunk(ub, 4, i * 3 + (G_BR + 1), 2, ybT_hi, ybT_lo)
                if not before:
                    pe.wait_ge(turn_lo, T_GLU + 2)
                chunk(ub, 6, i * 3 + (G_BR + 2), 2, ycT_hi, ycT_lo)

            pe.wait_ge(ya_lo, 4)
            pe.wait_ge(yb_lo, 4)
            branches(0, False)
            with pe.Fori(1, 4) as i:
                branches(i, True)
            pe.wait_ge(mg_ready, 4)
            turn(T_BR + 6, mg[:])
            pe.wait_ge(turn_lo, T_BR + 8)

            with pe.Fori(0, 4) as i:
                def mem_step(j):
                    if j == 0:
                        pe.wait_ge(mq_landed, (i + 1) * 16)
                        turn(i * 2 + T_MEM, mq[:])

                chunk(i * 8 + U_OUT, 0, i + G_OUT, CU, xT_hi, xT_lo, mem_step)

            def x1_step(j):
                if 2 <= j < 6:
                    pe.wait_ge(x1_ready, j - 1)
                    turn(T_X1 + 2 * (j - 2), xres[:, :, (j - 2) * NC:(j - 1) * NC])

            def heads_turned(src, done):
                for b in range(2):
                    for hd in range(2 * b, 2 * b + 2):
                        for h in range(HALVES):
                            c = (hd % 2) * SEQ + h * P
                            tt = pe.transpose(side[:, b, c:c + P], src[:, h, hd], ident[:])
                    tt.then_inc(done, 1)

            pe.wait_ge(turn_lo, T_MEM + 8)
            chunk(U_MK, 0, G_MK, CU, mT_hi, mT_lo, x1_step)

            def k_step(j):
                if j == 1:
                    for h in range(HALVES):
                        pe.wait_ge(acc_taken[h], G_MK + 1)
                    heads_turned(k_tok, k_turned)

            pe.wait_ge(turn_lo, T_X1 + 8)
            chunk(U_XQ, 0, G_XQ, CU, xT_hi, xT_lo, k_step)

            def soft_step(j):
                if j == 0:
                    for h in range(HALVES):
                        pe.wait_ge(acc_taken[h], G_XQ + 1)
                    pe.wait_ge(kx_ready, 2)
                    heads_turned(q_tok, q_turned)
                if j == 2:
                    pe.wait_ge(qx_ready, 2)
                    for hd in range(XHEADS):
                        for h in range(HALVES):
                            mm = pe.matmul(side[:, hd, h * SEQ:(h + 1) * SEQ], qxT[:, hd, h * P:(h + 1) * P], kxT[:, hd], start=True, stop=True)
                    mm.then_inc(xz_done, 1)

            chunk(U_MV, 0, G_MV, CU, mT_hi, mT_lo, soft_step)
            for hd in range(XHEADS):
                pe.wait_ge(xp_ready, hd + 1)
                for m in range(2):
                    for h in range(HALVES):
                        c = m * SEQ + h * P
                        tt = pe.transpose(side[:, hd, c:c + P], prob[:, hd, h, m * P:(m + 1) * P], ident[:])
                tt.then_inc(p_turned, 1)
            for h in range(HALVES):
                pe.wait_ge(acc_taken[h], G_MV + 1)
            pe.wait_ge(pT_ready, 4)
            for hd in range(XHEADS):
                for m in range(2):
                    mm = pe.matmul(tr[:, hd // 2, (hd % 2) * SEQ:(hd % 2 + 1) * SEQ], v_tok[:, m, hd], pT[:, hd, m], start=(m == 0), stop=(m == 1))
                if hd % 2:
                    mm.then_inc(xo_done, 1)
            pe.wait_ge(xo_lo, 2)
            for c in range(4):
                chunk(U_XO, 2 * c, G_XO + c, 2, oT_hi, oT_lo)
            for n in range(4):
                pe.wait_ge(x2_ready, n + 1)
                turn(T_X2 + 2 * n, xres[:, :, n * NC:(n + 1) * NC])
            pe.wait_ge(turn_lo, T_X2 + 8)

            def ffn_in(i, first):
                def step(j):
                    if j == 1 and not first:
                        for h in range(HALVES):
                            pe.wait_ge(acc_taken[h], i * 2 + G_FI)
                        turn(i * 2 + (T_FFN - 2), hb[:])

                chunk(i * 16 + U_FI, 0, i * 2 + G_FI, CU, xT_hi, xT_lo, step)
                chunk(i * 16 + U_FI, CU, i * 2 + (G_FI + 1), CU, xT_hi, xT_lo)

            ffn_in(0, True)
            with pe.Fori(1, 11) as i:
                ffn_in(i, False)
            for h in range(HALVES):
                pe.wait_ge(acc_taken[h], G_FO)
            turn(T_FFN + 20, hb[:])
            pe.wait_ge(turn_lo, T_FFN + 22)
            with pe.Fori(0, 2) as i:
                for c in range(2):
                    chunk(i * 44 + U_FO, 22 * c, i * 2 + (G_FO + c), 22, hT_hi, hT_lo)


_INS = ["x", "mem", "mix_pre_gain", "mix_post_gain", "w_in", "gm_v_gain", "gm_w_s", "gm_b_s",
        "s5_lam_re", "s5_lam_im", "s5_log_dt", "s5_b_re", "s5_b_im", "s5_c_re", "s5_c_im", "s5_d",
        "s5_w_glu", "w_br_a", "w_br_b", "w_br_c", "w_out", "xattn_pre_gain", "xattn_post_gain",
        "mem_gain", "w_xq", "w_xkv", "w_xo", "ffn_pre_gain", "ffn_post_gain", "w_ffn_in", "w_ffn_out"]


def kernel(**inputs):
    import numpy as _np
    import concourse.bacc as _bacc
    from concourse import mybir as _mybir
    from concourse.bass_utils import run_bass_kernel_spmd as _run

    nc = _bacc.Bacc("TRN2", target_bir_lowering=False, num_devices=1)
    arrays, args = {}, []
    for name in _INS:
        a = _np.ascontiguousarray(inputs[name])
        arrays[f"in_{name}"] = a
        args.append(nc.dram_tensor(f"in_{name}", a.shape, _mybir.dt.from_np(a.dtype), kind="ExternalInput").ap())
    args.append(nc.dram_tensor("out_0", (1, SEQ, D), F32, kind="ExternalOutput").ap())
    trunk(nc, *args)
    r = _run(nc, [arrays], core_ids=[0])
    return r.results[0]["out_0"]
```

```python
from contextlib import ExitStack
import math

import concourse.bass as bass
from concourse import mybir

F32 = mybir.dt.float32
F32R = mybir.dt.float32r
ACT = mybir.ActivationFunctionType
ALU = mybir.AluOpType
AX = mybir.AxisListType

P = 128
HALVES = 2
SEQ = P * HALVES
D = 2048
NC = 512
KT = D // P
UK = 2
RING = 4
CU = KT // UK

HEADS, HDIM = 4, 256
GROUPS, GCHUNK = 4, 128
S5_PAIRS, S5_TILES = 16, 4
STATE, GCH = 64, 16
XHEADS, XDIM = 4, 128
FFN = 5632
OFF_GATES = 3072 + 1024 + 512
OFF_S5 = 3072 + 1024
EPS = 1e-6

U_S5, U_PRE, U_PROJ, U_MID, U_GLU, U_GATE = 0, 8, 24, 88, 104, 108
U_BR, U_OUT, U_MK, U_XQ, U_MV = 172, 204, 236, 244, 252
U_XO, U_FI, U_FO, U_END = 260, 268, 444, 532
G_S5, G_PRE, G_PROJ, G_MID, G_GLU, G_GATE, G_BR, G_OUT, G_MK, G_XQ, G_MV, G_XO, G_FI, G_FO = (
    0, 1, 3, 11, 13, 15, 23, 35, 39, 40, 41, 42, 46, 68)
T_X, T_GLU, T_BR, T_MEM, T_X1, T_X2, T_FFN = 0, 8, 10, 18, 26, 34, 42
N_X, N_GM, N_Y1, N_MEM, N_X1, N_Y2, N_X2, N_Y3 = range(8)
C_MIX, C_XAT, C_MEM, C_FFN, C_LRE, C_LIM, C_LDT, C_D, C_BS, C_END = 0, 16, 32, 48, 64, 80, 96, 112, 116, 120

TWO_PI = 2 * math.pi
PI_A = 6.28125
PI_B = 0.0019350051879882812
PI_C = TWO_PI - PI_A - PI_B
ROUND = 1.5 * 2 ** 23
PI_MAX = 3.1415925


class Chain:

    def __init__(self, engine, sem):
        self.engine, self.sem, self.count, self.offset = engine, sem, 0, 0

    def enter(self, reg, first, per):
        self.entered, self.per = self.count, per
        self.offset = (reg - first) * per if first else reg * per

    def leave(self, n):
        assert self.count - self.entered == self.per, (self.count - self.entered, self.per)
        self.count, self.offset = self.entered + n * self.per, 0

    def link(self, instruction):
        instruction.then_inc(self.sem, 1)
        self.count += 1
        self.engine.wait_ge(self.sem, self.offset + self.count)


def trunk(nc, x, mem, mix_pre_gain, mix_post_gain, w_in, gm_v_gain, gm_w_s, gm_b_s,
          s5_lam_re, s5_lam_im, s5_log_dt, s5_b_re, s5_b_im, s5_c_re, s5_c_im, s5_d,
          s5_w_glu, w_br_a, w_br_b, w_br_c, w_out, xattn_pre_gain, xattn_post_gain,
          mem_gain, w_xq, w_xkv, w_xo, ffn_pre_gain, ffn_post_gain, w_ffn_in, w_ffn_out, out):
    with ExitStack() as ctx:
        base = (nc.sbuf_base + 31) // 32 * 32
        KB = 1024

        def at(name, kb, shape, dt=F32):
            return nc.alloc_sbuf_tensor_at(name, [P] + shape, dt, offset=base + int(kb * KB))

        def ps(name, shape):
            return ctx.enter_context(nc.psum_tensor(name, shape, F32))

        def sem(name):
            return ctx.enter_context(nc.semaphore(name))

        raw = at("raw", 0, [RING, UK, NC])
        w_hi = at("w_hi", 16, [RING, UK, NC], F32R)
        w_lo = at("w_lo", 32, [RING, UK, NC], F32R)
        xT_hi = at("xT_hi", 48, [KT, SEQ], F32R)
        xT_lo = at("xT_lo", 64, [KT, SEQ], F32R)
        x_tok = at("x_tok", 80, [HALVES, D])
        proj = at("proj", 80, [32, HALVES, P])
        yaT_hi = at("yaT_hi", 80, [8, SEQ], F32R)
        yaT_lo = at("yaT_lo", 88, [8, SEQ], F32R)
        ycT_hi = at("ycT_hi", 96, [4, SEQ], F32R)
        ycT_lo = at("ycT_lo", 100, [4, SEQ], F32R)
        gT_hi = at("gT_hi", 112, [4, SEQ], F32R)
        gT_lo = at("gT_lo", 116, [4, SEQ], F32R)
        ybT_hi = at("ybT_hi", 120, [4, SEQ], F32R)
        ybT_lo = at("ybT_lo", 124, [4, SEQ], F32R)
        vgain = at("vgain", 120, [NC])
        yc = at("yc", 128, [HALVES, NC])
        gates = at("gates", 132, [12, HALVES, NC])
        cosT = at("cosT", 132, [S5_PAIRS, P])
        sinT = at("sinT", 140, [S5_PAIRS, P])
        tabA = at("tabA", 148, [S5_PAIRS, P // 2])
        tabB = at("tabB", 152, [S5_PAIRS, P // 2])
        m1 = at("m1", 148, [4, SEQ])
        m2 = at("m2", 152, [4, SEQ])
        v_re = at("v_re", 156, [4, SEQ])
        v_im = at("v_im", 160, [4, SEQ])
        s5u = at("s5u", 180, [S5_TILES, HALVES, P])
        Bn = at("Bn", 184, [S5_PAIRS, 2, 32])
        Cn = at("Cn", 188, [S5_TILES, 2, P])
        rows = at("rows", 192, [P])
        u_st = at("u_st", 192, [HALVES, P])
        B_st = at("B_st", 193, [2, 4, 32])
        C_st = at("C_st", 194, [2, P])
        uB = at("uB", 195, [2, SEQ])
        Cp = at("Cp", 197, [2, P])
        y_sb = at("y_sb", 198, [SEQ])
        g_sb = at("g_sb", 199, [SEQ])
        ang = at("ang", 200, [8, S5_PAIRS])
        sinA = at("sinA", 200.5, [8, S5_PAIRS])
        cosA = at("cosA", 201, [8, S5_PAIRS])
        prm = at("prm", 201.5, [16, S5_PAIRS])
        carry = at("carry", 202.5 - 4 * 4 * 4 / 1024, [4, 4])
        sig_g = at("sig_g", 132, [HALVES, NC])
        q_st = at("q_st", 180, [2, HALVES, P])
        k_st = at("k_st", 182, [2, HALVES, P])
        v_st = at("v_st", 184, [2, HALVES, P])
        qT = at("qT", 186, [2, SEQ])
        kT = at("kT", 188, [2, SEQ])
        z_sb = at("z_sb", 190, [384])
        ez = at("ez", 191.5, [384])
        lz = at("lz", 193, [384])
        sp = at("sp", 194.5, [384])
        zm = at("zm", 196, [384])
        wz = at("wz", 197.5, [384])
        ws_st = at("ws_st", 199, [P])
        wsT = at("wsT", 199.5, [P])
        yb = at("yb", 200, [HALVES, P])
        xres = at("xres", 180, [HALVES, D])
        mg = at("mg", 196, [HALVES, NC])
        mt = at("mt", 200, [NC])
        mT_hi = at("mT_hi", 80, [KT, SEQ], F32R)
        mT_lo = at("mT_lo", 96, [KT, SEQ], F32R)
        mq = at("mq", 112, [HALVES, NC])
        yg = at("yg", 116, [HALVES, D])
        post_gain = at("post_gain", 132, [D])
        k_tok = at("k_tok", 140, [HALVES, XHEADS, XDIM])
        v_tok = at("v_tok", 144, [HALVES, XHEADS, XDIM])
        q_tok = at("q_tok", 148, [HALVES, XHEADS, XDIM])
        kxT = at("kxT", 152, [XHEADS, SEQ])
        qxT = at("qxT", 156, [XHEADS, SEQ])
        prob = at("prob", 160, [XHEADS, HALVES, SEQ])
        pT = at("pT", 168, [XHEADS, 2, SEQ])
        oT_hi = at("oT_hi", 176, [XHEADS, SEQ], F32R)
        oT_lo = at("oT_lo", 196, [XHEADS, SEQ], F32R)
        xsm = at("xsm", 200, [4, XHEADS * HALVES])
        hT_hi = at("hT_hi", 80, [FFN // P, SEQ], F32R)
        hT_lo = at("hT_lo", 124, [FFN // P, SEQ], F32R)
        silu_g = at("silu_g", 168, [HALVES, NC])
        hb = at("hb", 172, [HALVES, NC])
        yg3 = at("yg3", 48, [HALVES, D])
        post_gain3 = at("post_gain3", 64, [D])
        junk = at("junk", 202.5, [NC])
        ident = at("ident", 204.5, [P])
        lt = at("lt", 205, [P])
        gt = at("gt", 205.5, [P])
        le = at("le", 206, [P])
        ones = at("ones", 206.5, [P])
        cols = at("cols", 207, [P])
        ss = at("ss", 207.5, [4, HALVES, 4])
        inv = at("inv", 207.625, [8, HALVES])
        rstd = at("rstd", 207.6875, [8, HALVES])
        halfpi = at("halfpi", 207.75, [1])

        acc = ps("acc", [P, HALVES, NC])
        side = ps("side", [P, 4, NC])
        tr = ps("tr", [P, 2, NC])

        w_landed = [sem(f"w_landed{i}") for i in range(RING)]
        hi_ready, lo_ready, unit_used = sem("hi_ready"), sem("lo_ready"), sem("unit_used")
        acc0_full = sem("acc0_full")
        acc_taken = [sem("acc0_taken"), sem("acc1_taken")]
        turned, turn_hi, turn_lo = sem("turned"), sem("turn_hi"), sem("turn_lo")
        inv_ready, rstd_ready = sem("inv_ready"), sem("rstd_ready")
        act_own, dve_own, pool_own = sem("act_own"), sem("dve_own"), sem("pool_own")
        x_landed = [sem(f"x_landed{i}") for i in range(4)]
        gain_row_landed, rows_landed, ldt_spread = sem("gain_row_landed"), sem("rows_landed"), sem("ldt_spread")
        x_squared = sem("x_squared")
        const_ready, cols_turned, cols_ready = sem("const_ready"), sem("cols_turned"), sem("cols_ready")
        bc_zero, bc_landed, vgain_landed = sem("bc_zero"), sem("bc_landed"), sem("vgain_landed")
        prm_dt, prm_ang, prm_sin, prm_ready, table_ready = (
            sem("prm_dt"), sem("prm_ang"), sem("prm_sin"), sem("prm_ready"), sem("table_ready"))
        s5_staged, s5_turned, s5_uB, s5_Cp, s5_bu = (
            sem("s5_staged"), sem("s5_turned"), sem("s5_uB"), sem("s5_Cp"), sem("s5_bu"))
        s5_x, s5_y, s5_ysb, s5_gelu, gT_hi_ready, gT_ready = (
            sem("s5_x"), sem("s5_y"), sem("s5_ysb"), sem("s5_gelu"), sem("gT_hi_ready"), sem("gT_ready"))
        gm_gelu, gm_ready, yc_ready = sem("gm_gelu"), sem("gm_ready"), sem("yc_ready")
        qkv_staged, qk_turned, qT_ready, kT_ready, z_done, z_ready, l_ready = (
            sem("qkv_staged"), sem("qk_turned"), sem("qT_ready"), sem("kT_ready"), sem("z_done"),
            sem("z_ready"), sem("l_ready"))
        sp_ready, tail_done, lw_ready, w_exp, wz_ready, ya_done, ya_hi, ya_lo = (
            sem("sp_ready"), sem("tail_done"), sem("lw_ready"), sem("w_exp"), sem("wz_ready"),
            sem("ya_done"), sem("ya_hi"), sem("ya_lo"))
        ws_landed, ws_turned, wsT_ready, mixed_done, yb_ready, yb_turned, yb_hi, yb_lo = (
            sem("ws_landed"), sem("ws_turned"), sem("wsT_ready"), sem("mixed_done"), sem("yb_ready"),
            sem("yb_turned"), sem("yb_hi"), sem("yb_lo"))
        mg_ready, xres_landed, gain_landed, mq_landed, mq_squared = (
            sem("mg_ready"), sem("xres_landed"), sem("gain_landed"), sem("mq_landed"), sem("mq_squared"))
        squared, x1_ready, x2_ready = sem("squared"), sem("x1_ready"), sem("x2_ready")
        k_turned, kx_ready, q_turned, qx_ready = sem("k_turned"), sem("kx_ready"), sem("q_turned"), sem("qx_ready")
        xz_done, xmax_ready, xexp_done, xp_ready, p_turned, pT_ready, xo_done, xo_hi, xo_lo = (
            sem("xz_done"), sem("xmax_ready"), sem("xexp_done"), sem("xp_ready"), sem("p_turned"),
            sem("pT_ready"), sem("xo_done"), sem("xo_hi"), sem("xo_lo"))
        silu_ready, hb_ready, out_ready, out_landed = (
            sem("silu_ready"), sem("hb_ready"), sem("out_ready"), sem("out_landed"))

        block = ctx.enter_context(nc.Block())

        def kview(w):
            return w.rearrange("(k p) n -> p k n", p=P)

        w_in_k, w_glu_k, wa_k, wb_k, wc_k = (kview(w[0]) for w in (w_in, s5_w_glu, w_br_a, w_br_b, w_br_c))
        w_out_k, w_xq_k, w_xkv_k, w_xo_k = (kview(w[0]) for w in (w_out, w_xq, w_xkv, w_xo))
        w_fi_k, w_fo_k = kview(w_ffn_in[0]), kview(w_ffn_out[0])
        x_v = x[0].rearrange("(h p) d -> p h d", p=P)
        mem_v = mem[0].rearrange("(h p) d -> p h d", p=P)
        out_v = out[0].rearrange("(h p) d -> p h d", p=P)

        @block.sync
        def _(sp_):
            def load(u, slot, src):
                if not isinstance(u, int) or u >= RING:
                    sp_.wait_ge(lo_ready, u - (RING - 1))
                sp_.dma_start(raw[:, slot], src).then_inc(w_landed[slot], 16)

            def load_chunk(u, j0, w, col, units, k0=0):
                for j in range(units):
                    load(u + j0 + j, (j0 + j) % RING,
                         w[:, k0 + UK * j:k0 + UK * (j + 1), bass.ds(col, NC)])

            def load_x(n):
                sp_.dma_start(x_tok[:, :, n * NC:(n + 1) * NC], x_v[:, :, n * NC:(n + 1) * NC]).then_inc(x_landed[n], 16)

            load_x(0)
            load_chunk(U_S5, 0, w_in_k, OFF_S5, 1)
            load_x(1)
            load_chunk(U_S5, 1, w_in_k, OFF_S5, 1, UK)
            load_x(2)
            load_chunk(U_S5, 2, w_in_k, OFF_S5, 1, 2 * UK)
            load_x(3)
            load_chunk(U_S5, 3, w_in_k, OFF_S5, CU - 3, 3 * UK)
            for c in range(2):
                load_chunk(U_PRE, CU * c, w_in_k, OFF_GATES + (8 + c) * NC, CU)
            with sp_.Fori(0, 4) as i:
                for c in range(2):
                    load_chunk(i * 16 + U_PROJ, CU * c, w_in_k, i * (2 * NC) + c * NC, CU)
            for c in range(2):
                load_chunk(U_MID, CU * c, w_in_k, OFF_GATES + (10 + c) * NC, CU)
            for c in range(2):
                load_chunk(U_GLU, 2 * c, w_glu_k, c * NC, 2)
            with sp_.Fori(0, 4) as i:
                for c in range(2):
                    load_chunk(i * 16 + U_GATE, CU * c, w_in_k, i * (2 * NC) + (OFF_GATES + c * NC), CU)
            with sp_.Fori(0, 4) as i:
                load_chunk(i * 8 + U_BR, 0, wa_k, i * NC, 4)
                load_chunk(i * 8 + U_BR, 4, wb_k, i * NC, 2)
                load_chunk(i * 8 + U_BR, 6, wc_k, i * NC, 2)
            with sp_.Fori(0, 4) as i:
                load_chunk(i * 8 + U_OUT, 0, w_out_k, i * NC, CU)
            load_chunk(U_MK, 0, w_xkv_k, 0, CU)
            load_chunk(U_XQ, 0, w_xq_k, 0, CU)
            load_chunk(U_MV, 0, w_xkv_k, NC, CU)
            for c in range(4):
                load_chunk(U_XO, 2 * c, w_xo_k, c * NC, 2)
            with sp_.Fori(0, 11) as i:
                load_chunk(i * 16 + U_FI, 0, w_fi_k, i * NC, CU)
                load_chunk(i * 16 + U_FI, CU, w_fi_k, i * NC + FFN, CU)
            with sp_.Fori(0, 2) as i:
                for c in range(2):
                    load_chunk(i * 44 + U_FO, 22 * c, w_fo_k, i * (2 * NC) + c * NC, 22)
            for n in range(4):
                sp_.wait_ge(out_ready, n + 1)
                sp_.dma_start(out_v[:, :, n * NC:(n + 1) * NC], xres[:, :, n * NC:(n + 1) * NC]).then_inc(out_landed, 16)
            sp_.wait_ge(out_landed, 64)

        @block.gpsimd
        def _(pool):
            own = Chain(pool, pool_own)
            g = nc.gpsimd
            g.memset(halfpi[:], math.pi / 2).then_inc(const_ready, 1)
            own.link(g.memset(ident[:], 0.0))
            g.affine_select(out=ident[:], in_=ident[:], compare_op=ALU.not_equal, fill=1.0, base=0,
                            pattern=[[-1, P]], channel_multiplier=1).then_inc(const_ready, 1)
            g.memset(Bn[:], 0.0).then_inc(bc_zero, 1)
            g.memset(Cn[:], 0.0).then_inc(bc_zero, 1)
            own.link(g.memset(ones[:], 1.0))
            g.affine_select(out=lt[:], in_=ones[:], compare_op=ALU.is_gt, fill=0.0, base=0,
                            pattern=[[1, P]], channel_multiplier=-1).then_inc(const_ready, 1)
            g.affine_select(out=gt[:], in_=ones[:], compare_op=ALU.is_gt, fill=0.0, base=0,
                            pattern=[[-1, P]], channel_multiplier=1).then_inc(const_ready, 1)
            g.affine_select(out=le[:], in_=ones[:], compare_op=ALU.is_ge, fill=0.0, base=0,
                            pattern=[[1, P]], channel_multiplier=-1).then_inc(const_ready, 1)
            pool.wait_ge(bc_zero, 2)
            for r, b in enumerate((s5_b_re, s5_b_im)):
                bv = b[0].rearrange("(q e) n c -> e n q c", e=2)
                for e in range(2):
                    g.dma_start(Bn[e * STATE:(e + 1) * STATE, :, r, e * GCH:(e + 1) * GCH], bv[e]).then_inc(bc_landed, 16)
            for r, c_ in enumerate((s5_c_re, s5_c_im)):
                cv = c_[0].rearrange("(t q e) c n -> q e c t n", q=4, e=2)
                for q in range(4):
                    for e in range(2):
                        p0 = q * 32 + e * GCH
                        g.dma_start(Cn[p0:p0 + GCH, :, r, e * STATE:(e + 1) * STATE], cv[q, e]).then_inc(bc_landed, 16)

            pool.wait_ge(prm_sin, 2)
            own.link(g.memset(cosT[:, :, 0:1], 1.0))
            own.link(g.memset(sinT[:, :, 0:1], 0.0))
            for k in range(7):
                L = 1 << k
                c_, s_ = cosT[:, :, 0:L], sinT[:, :, 0:L]
                ck = cosA[:, k, :].unsqueeze(2).to_broadcast([P, S5_PAIRS, L])
                sk = sinA[:, k, :].unsqueeze(2).to_broadcast([P, S5_PAIRS, L])
                a, b = tabA[:, :, 0:L], tabB[:, :, 0:L]
                g.tensor_tensor(a, c_, ck, ALU.mult)
                own.link(g.tensor_tensor(b, s_, sk, ALU.mult))
                own.link(g.tensor_tensor(cosT[:, :, L:2 * L], a, b, ALU.subtract))
                g.tensor_tensor(a, c_, sk, ALU.mult)
                own.link(g.tensor_tensor(b, s_, ck, ALU.mult))
                last = g.tensor_tensor(sinT[:, :, L:2 * L], a, b, ALU.add)
                if k < 6:
                    own.link(last)
                else:
                    last.then_inc(table_ready, 1)

            def stage_s5(i):
                g.tensor_copy(u_st[:], s5u[:, bass.ds(i, 1)].rearrange("p o h c -> p (o h) c"))
                for r in range(2):
                    g.tensor_copy(B_st[:, r], Bn[:, bass.ds(i * 4, 4), r, :])
                g.tensor_copy(C_st[:], Cn[:, bass.ds(i, 1)].rearrange("p o r c -> p (o r) c")).then_inc(s5_staged, 1)

            for h in range(HALVES):
                pool.wait_ge(acc_taken[h], G_S5 + 1)
            pool.wait_ge(bc_landed, 16 * 20)
            stage_s5(0)
            with pool.Fori(1, S5_TILES) as i:
                pool.wait_ge(s5_turned, i)
                stage_s5(i)

            def stage_head(i):
                for dst, blk in ((q_st, 0), (k_st, 8), (v_st, 16)):
                    last = g.tensor_copy(dst[:], proj[:, bass.ds(i * 2 + blk, 2)])
                last.then_inc(qkv_staged, 1)

            def load_ws(i):
                g.dma_start(ws_st[:], gm_w_s[0][bass.ds(i, 1)].rearrange("o t s -> (o t) s")).then_inc(ws_landed, 16)

            for h in range(HALVES):
                pool.wait_ge(acc_taken[h], G_MID)
            pool.wait_ge(gT_ready, 4)
            stage_head(0)
            load_ws(0)
            with pool.Fori(1, HEADS) as i:
                pool.wait_ge(ya_done, i)
                stage_head(i)
                pool.wait_ge(ws_turned, i)
                load_ws(i)

            pool.wait_ge(yb_lo, 4)
            pool.wait_ge(ya_lo, 4)
            g.dma_start(xres[:], x_v).then_inc(xres_landed, 16)

            def load_mem(i):
                g.dma_start(mq[:], mem_v[:, :, bass.ds(i * NC, NC)]).then_inc(mq_landed, 16)

            load_mem(0)
            pool.wait_ge(mg_ready, 4)
            g.dma_start(post_gain[:], mix_post_gain[0:1].to_broadcast([P, D])).then_inc(gain_landed, 16)
            with pool.Fori(1, 4) as i:
                pool.wait_ge(mq_squared, i)
                load_mem(i)
            for h in range(HALVES):
                pool.wait_ge(acc_taken[h], G_OUT + 4)
            g.dma_start(post_gain[:], xattn_post_gain[0:1].to_broadcast([P, D])).then_inc(gain_landed, 16)
            pool.wait_ge(unit_used, U_FO)
            g.dma_start(post_gain3[:], ffn_post_gain[0:1].to_broadcast([P, D])).then_inc(gain_landed, 16)

        @block.scalar
        def _(act):
            own = Chain(act, act_own)
            a_ = nc.scalar

            def r_of(n, h):
                return rstd[:, n, h:h + 1]

            def split(ub, qb, j):
                u = ub + j
                if isinstance(u, int) and u >= U_END:
                    return
                act.wait_ge(w_landed[j % RING], (qb + j // RING + 1) * 16)
                if not isinstance(u, int) or u >= RING:
                    act.wait_ge(unit_used, u - (RING - 1))
                a_.activation(w_hi[:, j % RING], raw[:, j % RING], ACT.Copy).then_inc(hi_ready, 1)

            def wait_acc(h, g, u_last):
                if h == 0:
                    act.wait_ge(acc0_full, g + 1)
                else:
                    act.wait_ge(unit_used, u_last + 1)

            def take(g, u_last, dst, func, norm=None):
                for h in range(HALVES):
                    wait_acc(h, g, u_last)
                    src = acc[:, h]
                    d = dst(h)
                    if len(d.shape) == 3:
                        src = src.rearrange("p (b c) -> p b c", c=P)
                    a_.activation(d, src, func, scale=r_of(norm, h) if norm is not None else 1.0).then_inc(acc_taken[h], 1)

            def square(g, u_last, n, col, before):
                for h in range(HALVES):
                    wait_acc(h, g, u_last)
                    a_.activation(junk[:], acc[:, h], ACT.Square,
                                  accum_out=ss[:, n % 4, h, bass.ds(col, 1)]).then_inc(squared, 1)
                    act.wait_ge(squared, before + (h + 1))

            def square_quarter(n, quarter, before):
                for h in range(HALVES):
                    a_.activation(junk[:], xres[:, h, quarter * NC:(quarter + 1) * NC], ACT.Square,
                                  accum_out=ss[:, n % 4, h, quarter:quarter + 1]).then_inc(squared, 1)
                    act.wait_ge(squared, before + h + 1)

            def turn_hi_parts(t, dst, k0, gain=None):
                for b in range(2):
                    act.wait_ge(turned, t + b + 1)
                    if gain is None:
                        last = a_.activation(dst[:, bass.ds(k0 + 2 * b, 2)].rearrange("p k t -> p (k t)"), tr[:, b], ACT.Copy)
                    else:
                        for k in range(2):
                            last = a_.activation(dst[:, bass.ds(k0 + (2 * b + k), 1)].rearrange("p k t -> p (k t)"),
                                                 tr[:, b, k * SEQ:(k + 1) * SEQ], ACT.Copy,
                                                 scale=cols[:, bass.ds(k0 + (gain + 2 * b + k), 1)])
                    last.then_inc(turn_hi, 1)

            def root(n, k):
                act.wait_ge(inv_ready, k + 1)
                a_.activation(rstd[:, n], inv[:, n], ACT.Sqrt).then_inc(rstd_ready, 1)

            act.dma_start(rows[C_MIX:C_MIX + KT, :], mix_pre_gain[0].rearrange("(k p) -> k p", p=P)).then_inc(gain_row_landed, 16)
            act.dma_start(junk[C_LDT:C_LDT + S5_PAIRS, 0:2], s5_log_dt[0].rearrange("(q e) -> q e", e=2)).then_inc(rows_landed, 16)
            for r0, v in ((C_LRE, s5_lam_re), (C_LIM, s5_lam_im)):
                act.dma_start(rows[r0:r0 + S5_PAIRS, :].rearrange("q (e n) -> q e n", e=2),
                              v[0].rearrange("(q e) n -> q e n", e=2)).then_inc(rows_landed, 16)
            for r0, v in ((C_XAT, xattn_pre_gain), (C_MEM, mem_gain), (C_FFN, ffn_pre_gain)):
                act.dma_start(rows[r0:r0 + KT, :], v[0].rearrange("(k p) -> k p", p=P)).then_inc(rows_landed, 16)
            act.dma_start(rows[C_D:C_D + 4, :], s5_d[0].rearrange("(k p) -> k p", p=P)).then_inc(rows_landed, 16)
            act.dma_start(rows[C_BS:C_BS + 4, :], gm_b_s[0]).then_inc(rows_landed, 16)
            act.wait_ge(const_ready, 1)
            a_.activation(inv[:, 0, 0:1], halfpi[:], ACT.Exp)

            act.wait_ge(cols_turned, 1)
            a_.activation(cols[:, 0:KT], side[:, 0, 0:KT], ACT.Copy).then_inc(cols_ready, 1)
            act.wait_ge(cols_ready, 1)
            turn_hi_parts(T_X, xT_hi, 0, C_MIX)
            split(0, 0, 0)
            split(0, 0, 1)
            turn_hi_parts(T_X + 2, xT_hi, 4, C_MIX)
            split(0, 0, 2)
            split(0, 0, 3)

            for j in range(CU):
                if j == 0:
                    act.wait_ge(cols_turned, 2)
                    a_.activation(cols[:, KT:C_END], side[:, 1, KT:C_END], ACT.Copy).then_inc(cols_ready, 1)
                    act.wait_ge(cols_ready, 2)
                    a_.activation(prm[:, 0], cols[:, C_LDT:C_LDT + S5_PAIRS], ACT.Exp).then_inc(prm_dt, 1)
                if j in (0, 2):
                    turn_hi_parts(T_X + j + 4, xT_hi, 2 * j + 8, C_MIX)
                if 1 <= j < 5:
                    for h in range(HALVES):
                        a_.activation(junk[:], x_tok[:, h, (j - 1) * NC:j * NC], ACT.Square,
                                      accum_out=ss[:, N_X % 4, h, j - 1:j]).then_inc(x_squared, 1)
                        act.wait_ge(x_squared, 2 * j - 1 + h)
                if j == 5:
                    act.wait_ge(prm_ang, 1)
                    a_.activation(prm[:, 2], prm[:, 3], ACT.Exp).then_inc(prm_sin, 1)
                    a_.activation(cosA[:], cosA[:], ACT.Sin, scale=-1.0, bias=halfpi[:])
                    a_.activation(prm[:, 1], ang[:, 0], ACT.Sin, scale=0.5)
                    a_.activation(sinA[:], ang[:], ACT.Sin).then_inc(prm_sin, 1)
                if j == 6:
                    root(N_X, 0)
                if j == 7:
                    act.wait_ge(rstd_ready, 1)
                    take(G_S5, U_S5 + j, lambda h: s5u[:, :, h, :], ACT.Copy, N_X)
                split(U_S5, 0, j + RING)
            act.dma_start(vgain[:], gm_v_gain[0:1].to_broadcast([P, NC])).then_inc(vgain_landed, 16)

            def gate_chunks(ub, qb, g, slot, n, step):
                for j in range(CU * n):
                    step(j)
                    if j % CU == CU - 1:
                        c = j // CU
                        take(g + c, ub + j,
                             lambda h: gates[:, bass.ds(slot + c, 1), h, :].rearrange("p o n -> p (o n)"), ACT.Sigmoid, N_X)
                    split(ub, qb, j + RING)

            gate_chunks(U_PRE, U_PRE // RING, G_PRE, 8, 2, lambda j: None)

            with act.Fori(0, 4) as i:
                ub, qb = i * 16 + U_PROJ, i * 4 + U_PROJ // RING
                for j in range(16):
                    if j == 0:
                        act.wait_ge(s5_turned, i + 1)
                        a_.activation(uB[:].rearrange("p a b -> p (a b)"), side[:, 0], ACT.Copy).then_inc(s5_uB, 1)
                    if j % CU == CU - 1:
                        c = j // CU
                        take(i * 2 + (G_PROJ + c), ub + j,
                             lambda h: proj[:, bass.ds(i * 8 + 4 * c, 4), h, :], ACT.Copy, N_X)
                    if j == 15:
                        act.wait_ge(s5_ysb, i + 1)
                        a_.activation(g_sb[:], y_sb[:], ACT.Gelu_apprx_tanh).then_inc(s5_gelu, 1)
                        act.wait_ge(s5_gelu, i + 1)
                        a_.activation(gT_hi[:, bass.ds(i, 1)].rearrange("p k t -> p (k t)"), g_sb[:], ACT.Copy).then_inc(gT_hi_ready, 1)
                    split(ub, qb, j + RING)

            def gelu_step(j):
                if j == 0:
                    act.wait_ge(acc_taken[1], G_MID)
                    a_.activation(proj[:, 24:32], proj[:, 24:32], ACT.Gelu_apprx_tanh).then_inc(gm_gelu, 1)
                if j == 1:
                    act.wait_ge(gm_gelu, 1)
                    for h in range(HALVES):
                        a_.activation(junk[:].rearrange("p (g c) -> p g c", c=P), proj[:, 28:32, h, :], ACT.Square,
                                      accum_out=ss[:, N_GM % 4, h, 0:1]).then_inc(squared, 1)
                        act.wait_ge(squared, h + 1)
                if j == 3:
                    root(N_GM, 1)

            gate_chunks(U_MID, U_MID // RING, G_MID, 10, 2, gelu_step)
            for j in range(4):
                if j == 1:
                    take(G_GLU, U_GLU + j, lambda h: yc[:, h], ACT.Copy)
                if j == 3:
                    take(G_GLU + 1, U_GLU + j, lambda h: sig_g[:, h], ACT.Sigmoid)
                split(U_GLU, U_GLU // RING, j + RING)

            act.wait_ge(yc_ready, 1)
            with act.Fori(0, 4) as i:
                own.enter(i, 0, 2)

                def head_step(j):
                    if j == 1:
                        act.wait_ge(qk_turned, i + 1)
                        a_.activation(qT[:].rearrange("p a b -> p (a b)"), side[:, 0], ACT.Copy).then_inc(qT_ready, 1)
                    if j == 3:
                        act.wait_ge(z_done, i + 1)
                        a_.activation(z_sb[:], side[:, 2, 0:384], ACT.Copy, scale=HDIM ** -0.5).then_inc(z_ready, 1)
                        act.wait_ge(z_ready, i + 1)
                        own.link(a_.activation(ez[:], z_sb[:], ACT.Abs))
                        own.link(a_.activation(ez[:], ez[:], ACT.Exp, scale=-1.0))
                        a_.activation(lz[:], ez[:], ACT.Ln, bias=1.0).then_inc(l_ready, 1)
                    if j == 7:
                        act.wait_ge(yb_turned, i + 1)
                        a_.activation(ybT_hi[:, bass.ds(i, 1)].rearrange("p k t -> p (k t)"), side[:, 1, SEQ:], ACT.Copy).then_inc(yb_hi, 1)
                    if j == 8:
                        act.wait_ge(lw_ready, i + 1)
                        a_.activation(wz[:], zm[:], ACT.Exp).then_inc(w_exp, 1)
                    if j == 11:
                        act.wait_ge(ya_done, i + 1)
                        a_.activation(yaT_hi[:, bass.ds(i * 2, 2)].rearrange("p k t -> p (k t)"), side[:, 0], ACT.Copy).then_inc(ya_hi, 1)

                gate_chunks(i * 16 + U_GATE, i * 4 + U_GATE // RING, i * 2 + G_GATE, i * 2, 2, head_step)
                own.leave(4)
            turn_hi_parts(T_GLU, ycT_hi, 0)

            def branches(i, before):
                ub, qb = i * 8 + U_BR, i * 2 + U_BR // RING
                for j in range(8):
                    if j == 1 and before:
                        turn_hi_parts(i * 2 + (T_BR - 2), xT_hi, i * 4 - 4)
                    split(ub, qb, j + RING)

            branches(0, False)
            with act.Fori(1, 4) as i:
                branches(i, True)
            turn_hi_parts(T_BR + 6, xT_hi, 12)

            with act.Fori(0, 4) as i:
                own.enter(i, 0, 1)
                ub, qb = i * 8 + U_OUT, i * 2 + U_OUT // RING
                for j in range(8):
                    if j == 1:
                        for b in range(2):
                            act.wait_ge(turned, i * 2 + (T_MEM + b + 1))
                            for k in range(2):
                                kk = i * 4 + (2 * b + k)
                                last = a_.activation(mT_hi[:, bass.ds(kk, 1)].rearrange("p k t -> p (k t)"),
                                                     tr[:, b, k * SEQ:(k + 1) * SEQ], ACT.Copy,
                                                     scale=cols[:, bass.ds(kk + C_MEM, 1)])
                            last.then_inc(turn_hi, 1)
                    if j == 3:
                        act.wait_ge(mq_landed, (i + 1) * 16)
                        own.link(a_.activation(junk[:], mq[:, 0], ACT.Square, accum_out=ss[:, N_MEM % 4, 0, bass.ds(i, 1)]))
                        a_.activation(junk[:], mq[:, 1], ACT.Square, accum_out=ss[:, N_MEM % 4, 1, bass.ds(i, 1)]).then_inc(mq_squared, 1)
                        act.wait_ge(mq_squared, i + 1)
                    if j == 7:
                        square(i + G_OUT, ub + j, N_Y1, i, i * 2 + 2)
                    split(ub, qb, j + RING)
                own.leave(4)

            for j in range(CU):
                if j == 0:
                    root(N_Y1, 2)
                if 3 <= j < 7:
                    turn_hi_parts(T_X1 + 2 * (j - 3), xT_hi, 4 * (j - 3), C_XAT)
                if j == 6:
                    root(N_MEM, 3)
                if j == 7:
                    act.wait_ge(rstd_ready, 4)
                    take(G_MK, U_MK + j, lambda h: k_tok[:, h].rearrange("p a b -> p (a b)"), ACT.Copy, N_MEM)
                split(U_MK, U_MK // RING, j + RING)
            for j in range(CU):
                if j < 4:
                    square_quarter(N_X1, j, 10 + 2 * j)
                if j == 2:
                    act.wait_ge(k_turned, 1)
                    a_.activation(kxT[:, 0:2].rearrange("p a b -> p (a b)"), side[:, 0], ACT.Copy).then_inc(kx_ready, 1)
                if j == 5:
                    root(N_X1, 4)
                if j == 7:
                    act.wait_ge(rstd_ready, 5)
                    take(G_XQ, U_XQ + j, lambda h: q_tok[:, h].rearrange("p a b -> p (a b)"), ACT.Copy, N_X1)
                split(U_XQ, U_XQ // RING, j + RING)
            def exps(heads):
                for hd in heads:
                    for h in range(HALVES):
                        c = hd * HALVES + h
                        last = a_.activation(prob[:, hd, h], side[:, hd, h * SEQ:(h + 1) * SEQ], ACT.Exp,
                                             scale=XDIM ** -0.5, bias=xsm[:, 1, c:c + 1], accum_out=xsm[:, 2, c:c + 1])
                    last.then_inc(xexp_done, 1)

            for j in range(CU):
                if j == 1:
                    act.wait_ge(q_turned, 1)
                    a_.activation(qxT[:, 0:2].rearrange("p a b -> p (a b)"), side[:, 0], ACT.Copy).then_inc(qx_ready, 1)
                if j == 4:
                    act.wait_ge(xmax_ready, 1)
                    exps((0, 1))
                if j == 5:
                    exps((2, 3))
                if j == 7:
                    take(G_MV, U_MV + j, lambda h: v_tok[:, h].rearrange("p a b -> p (a b)"), ACT.Copy, N_MEM)
                    for hd in range(2):
                        act.wait_ge(p_turned, hd + 1)
                        a_.activation(pT[:, hd].rearrange("p a b -> p (a b)"), side[:, hd], ACT.Copy).then_inc(pT_ready, 1)
                    for b in range(2):
                        act.wait_ge(xo_done, b + 1)
                        a_.activation(oT_hi[:, 2 * b:2 * b + 2].rearrange("p a b -> p (a b)"), tr[:, b], ACT.Copy).then_inc(xo_hi, 1)
                split(U_MV, U_MV // RING, j + RING)
            for j in range(8):
                if j % 2:
                    square(G_XO + j // 2, U_XO + j, N_Y2, j // 2, 18 + j - 1)
                split(U_XO, U_XO // RING, j + RING)
            root(N_Y2, 5)
            for n in range(4):
                turn_hi_parts(T_X2 + 2 * n, xT_hi, 4 * n, C_FFN)

            def ffn_in(i, first):
                ub, qb = i * 16 + U_FI, i * 4 + U_FI // RING
                for j in range(16):
                    if first and j < 4:
                        square_quarter(N_X2, j, 26 + 2 * j)
                    if first and j == 5:
                        root(N_X2, 6)
                    if not first and j == 2:
                        turn_hi_parts(i * 2 + (T_FFN - 2), hT_hi, i * 4 - 4)
                    if j == 7:
                        if first:
                            act.wait_ge(rstd_ready, 7)
                        for h in range(HALVES):
                            wait_acc(h, i * 2 + G_FI, ub + j)
                            a_.activation(silu_g[:, h], acc[:, h], ACT.Silu, scale=r_of(N_X2, h)).then_inc(acc_taken[h], 1)
                    split(ub, qb, j + RING)

            ffn_in(0, True)
            with act.Fori(1, 11) as i:
                ffn_in(i, False)
            turn_hi_parts(T_FFN + 20, hT_hi, 40)

            for n in range(4):
                for j in range(22 * n, 22 * n + 22):
                    if j == 22 * n + 21:
                        square(G_FO + n, U_FO + j, N_Y3, n, 34 + 2 * n)
                    split(U_FO, U_FO // RING, j + RING)
            root(N_Y3, 7)

        @block.vector
        def _(dve):
            own = Chain(dve, dve_own)
            v_ = nc.vector

            def split(ub, j):
                u = ub + j
                if isinstance(u, int) and u >= U_END:
                    return
                s = j % RING
                dve.wait_ge(hi_ready, u + 1)
                v_.tensor_tensor(w_lo[:, s], raw[:, s], w_hi[:, s].bitcast(F32), ALU.subtract).then_inc(lo_ready, 1)

            def wait_acc(h, g, u_last):
                if h == 0:
                    dve.wait_ge(acc0_full, g + 1)
                else:
                    dve.wait_ge(unit_used, u_last + 1)

            def turn_lo_parts(t, dst_hi, dst_lo, k0, gain=None, k0_gain=None):
                for b in range(2):
                    dve.wait_ge(turn_hi, t + b + 1)
                    if gain is None:
                        ks = bass.ds(k0 + 2 * b, 2)
                        last = v_.tensor_tensor(dst_lo[:, ks].rearrange("p k t -> p (k t)"), tr[:, b],
                                                dst_hi[:, ks].rearrange("p k t -> p (k t)").bitcast(F32), ALU.subtract)
                    else:
                        for k in range(2):
                            ks = bass.ds(k0 + (2 * b + k), 1)
                            last = v_.scalar_tensor_tensor(
                                dst_lo[:, ks].rearrange("p k t -> p (k t)"), tr[:, b, k * SEQ:(k + 1) * SEQ],
                                cols[:, bass.ds(k0 + (gain + 2 * b + k), 1)],
                                dst_hi[:, ks].rearrange("p k t -> p (k t)").bitcast(F32), ALU.mult, ALU.subtract)
                    last.then_inc(turn_lo, 1)

            def inverse(n, width, squares):
                if squares:
                    dve.wait_ge(squared, squares)
                parts = 1 if n == N_GM else 4
                own.link(v_.tensor_reduce(inv[:, n], ss[:, n % 4, :, 0:parts], AX.X, ALU.add))
                own.link(v_.tensor_scalar(inv[:, n], inv[:, n], 1.0 / width, EPS, ALU.mult, ALU.add))
                v_.reciprocal(inv[:, n], inv[:, n]).then_inc(inv_ready, 1)

            def gained(g, u_last, sq, dst, gain, col):
                for h in range(HALVES):
                    dve.wait_ge(squared, sq + h)
                    v_.tensor_tensor(dst[:, h, bass.ds(col, NC)], acc[:, h], gain[:, bass.ds(col, NC)],
                                     ALU.mult).then_inc(acc_taken[h], 1)

            def residual(n, src, norm, ready):
                for h in range(HALVES):
                    q = slice(n * NC, (n + 1) * NC)
                    last = v_.scalar_tensor_tensor(xres[:, h, q], src[:, h, q], rstd[:, norm, h:h + 1],
                                                   xres[:, h, q], ALU.mult, ALU.add)
                last.then_inc(ready, 1)

            turn_lo_parts(T_X, xT_hi, xT_lo, 0, C_MIX)
            split(0, 0)
            split(0, 1)
            turn_lo_parts(T_X + 2, xT_hi, xT_lo, 4, C_MIX)
            dve.wait_ge(rows_landed, 16 * 8)
            v_.tensor_copy(rows[C_LDT:C_LDT + S5_PAIRS].rearrange("q (e n) -> q e n", e=2),
                           junk[C_LDT:C_LDT + S5_PAIRS, 0:2].unsqueeze(2).to_broadcast([S5_PAIRS, 2, STATE])).then_inc(ldt_spread, 1)
            split(0, 2)
            split(0, 3)

            DT, S2, EX, XR, TH, KR, RR, XC, PO, MAG, F_RE, F_IM, T1, T2, T3, DEN = range(16)

            def p_(k):
                return prm[:, k]

            def reduce_angle(a, k):
                own.link(v_.tensor_scalar(k, a, 1 / TWO_PI, ROUND, ALU.mult, ALU.add))
                own.link(v_.tensor_scalar(k, k, -ROUND, None, ALU.add))
                for part in (PI_A, PI_B, PI_C):
                    own.link(v_.scalar_tensor_tensor(a, k, -part, a, ALU.mult, ALU.add))

            lre, lim = cols[:, C_LRE:C_LRE + S5_PAIRS], cols[:, C_LIM:C_LIM + S5_PAIRS]

            def s5_angles(step):
                if step == 0:
                    dve.wait_ge(prm_dt, 1)
                    v_.tensor_tensor(p_(XR), lre, p_(DT), ALU.mult)
                    own.link(v_.tensor_tensor(ang[:, 0], lim, p_(DT), ALU.mult))
                    reduce_angle(ang[:, 0], p_(KR))
                    for k in range(1, 8):
                        last = v_.tensor_scalar(ang[:, k], ang[:, 0], float(1 << k), None, ALU.mult)
                    own.link(last)
                else:
                    reduce_angle(ang[:], sinA[:])
                    own.link(v_.tensor_scalar(ang[:], ang[:], PI_MAX, -PI_MAX, ALU.min, ALU.max))
                    v_.scalar_tensor_tensor(cosA[:], ang[:], -1.0, ang[:], ALU.mult, ALU.max).then_inc(prm_ang, 1)

            def s5_magnitude():
                dve.wait_ge(prm_sin, 2)
                own.link(v_.tensor_scalar(p_(XC), p_(XR), 0.5, -0.5, ALU.min, ALU.max))
                own.link(v_.tensor_scalar(p_(PO), p_(XC), 1.0 / math.factorial(10), None, ALU.mult))
                for k in range(9, 0, -1):
                    own.link(v_.scalar_tensor_tensor(p_(PO), p_(PO), 1.0 / math.factorial(k), p_(XC), ALU.add, ALU.mult))
                own.link(v_.tensor_tensor(p_(T1), p_(XC), p_(XR), ALU.not_equal))
                own.link(v_.scalar_tensor_tensor(p_(T2), p_(EX), -1.0, p_(PO), ALU.add, ALU.subtract))
                own.link(v_.tensor_tensor(p_(T2), p_(T2), p_(T1), ALU.mult))
                own.link(v_.tensor_tensor(p_(PO), p_(PO), p_(T2), ALU.add))
                own.link(v_.tensor_scalar(p_(MAG), p_(PO), 1.0, None, ALU.add))

            def s5_factor():
                own.link(v_.tensor_tensor(p_(T1), p_(PO), cosA[:, 0], ALU.mult))
                own.link(v_.scalar_tensor_tensor(p_(T2), p_(S2), -2.0, p_(S2), ALU.mult, ALU.mult))
                own.link(v_.tensor_tensor(p_(T1), p_(T1), p_(T2), ALU.add))
                own.link(v_.tensor_tensor(p_(T2), p_(MAG), sinA[:, 0], ALU.mult))
                own.link(v_.tensor_tensor(p_(DEN), lre, lre, ALU.mult))
                own.link(v_.tensor_tensor(p_(T3), lim, lim, ALU.mult))
                own.link(v_.tensor_tensor(p_(DEN), p_(DEN), p_(T3), ALU.add))
                own.link(v_.reciprocal(p_(DEN), p_(DEN)))
                own.link(v_.tensor_tensor(p_(F_RE), p_(T1), lre, ALU.mult))
                own.link(v_.tensor_tensor(p_(T3), p_(T2), lim, ALU.mult))
                own.link(v_.tensor_tensor(p_(F_RE), p_(F_RE), p_(T3), ALU.add))
                own.link(v_.tensor_tensor(p_(F_RE), p_(F_RE), p_(DEN), ALU.mult))
                own.link(v_.tensor_tensor(p_(F_IM), p_(T2), lre, ALU.mult))
                own.link(v_.tensor_tensor(p_(T3), p_(T1), lim, ALU.mult))
                own.link(v_.tensor_tensor(p_(F_IM), p_(F_IM), p_(T3), ALU.subtract))
                own.link(v_.tensor_tensor(p_(F_IM), p_(F_IM), p_(DEN), ALU.mult))

            for j in range(CU):
                if j in (0, 2):
                    turn_lo_parts(T_X + j + 4, xT_hi, xT_lo, 2 * j + 8, C_MIX)
                if j in (1, 3):
                    s5_angles(j // 2)
                if j == 5:
                    dve.wait_ge(x_squared, 8)
                    inverse(N_X, D, 0)
                split(U_S5, j + RING)
            for j in range(2 * CU):
                if j == 4:
                    s5_magnitude()
                if j == 8:
                    s5_factor()
                split(U_PRE, j + RING)
            dve.wait_ge(table_ready, 1)

            with dve.Fori(0, 4) as i:
                own.enter(i, 0, 12)
                ub = i * 16 + U_PROJ

                def blocks(a):
                    return a.rearrange("p q (c t) -> p q c t", c=2)

                b_re, b_im = blocks(side[:, :, 0:SEQ]), blocks(side[:, :, SEQ:2 * SEQ])
                ct, st = (tab[:, bass.ds(i * 4, 4)].unsqueeze(2).to_broadcast([P, 4, 2, P]) for tab in (cosT, sinT))
                M1, M2, VR, VI = (blocks(a[:]) for a in (m1, m2, v_re, v_im))

                def mul(o, a, b):
                    return v_.tensor_tensor(o, a, b, ALU.mult)

                for j in range(16):
                    if j == 1:
                        dve.wait_ge(s5_turned, i + 1)
                        fr = prm[:, F_RE, bass.ds(i * 4, 4)].unsqueeze(2).to_broadcast([P, 4, 32])
                        fi = prm[:, F_IM, bass.ds(i * 4, 4)].unsqueeze(2).to_broadcast([P, 4, 32])
                        cr = tr[:, 0, 0:P].rearrange("p (q c) -> p q c", q=4)
                        ci = tr[:, 0, P:2 * P].rearrange("p (q c) -> p q c", q=4)
                        t = [m1[:, k, 0:P].rearrange("p (q c) -> p q c", q=4) for k in range(4)]
                        mul(t[0], cr, fr)
                        mul(t[1], ci, fi)
                        mul(t[2], cr, fi)
                        own.link(mul(t[3], ci, fr))
                        v_.tensor_tensor(Cp[:, 0], m1[:, 0, 0:P], m1[:, 1, 0:P], ALU.subtract)
                        v_.scalar_tensor_tensor(Cp[:, 1], m1[:, 2, 0:P], -1.0, m1[:, 3, 0:P], ALU.mult, ALU.subtract).then_inc(s5_Cp, 1)
                    if j == 2:
                        dve.wait_ge(s5_Cp, i + 1)
                        dve.wait_ge(s5_bu, i + 1)
                        mul(M1, b_re, ct)
                    if j == 3:
                        own.link(mul(M2, b_im, st))
                    if j == 4:
                        own.link(v_.tensor_tensor(v_re[:], m1[:], m2[:], ALU.add))
                    if j == 5:
                        mul(M1, b_im, ct)
                        own.link(mul(M2, b_re, st))
                    if j == 6:
                        own.link(v_.tensor_tensor(v_im[:], m1[:], m2[:], ALU.subtract))
                    if j in (7, 9):
                        for q in range(4):
                            mag = prm[:, MAG, bass.ds(i * 4 + q, 1)].to_broadcast([P, P])
                            for r, v in enumerate((VR, VI)):
                                blk = v[:, q, (j - 7) // 2]
                                before = 0.0 if j == 7 else carry[:, r, q:q + 1]
                                last = v_.tensor_tensor_scan(blk, mag, blk, before, ALU.mult, ALU.add)
                        own.link(last)
                    if j == 8:
                        c7, s7 = cosA[:, 7, bass.ds(i * 4, 4)], sinA[:, 7, bass.ds(i * 4, 4)]
                        vr, vi = v_re[:, :, P - 1], v_im[:, :, P - 1]
                        mul(carry[:, 0], vr, c7)
                        mul(carry[:, 1], vi, c7)
                        mul(carry[:, 2], vi, s7)
                        own.link(mul(carry[:, 3], vr, s7))
                        v_.tensor_tensor(carry[:, 0], carry[:, 0], carry[:, 2], ALU.subtract)
                        own.link(v_.tensor_tensor(carry[:, 1], carry[:, 1], carry[:, 3], ALU.add))
                    if j == 10:
                        mul(M1, VR, ct)
                    if j == 11:
                        own.link(mul(M2, VI, st))
                    if j == 12:
                        own.link(v_.tensor_tensor(m1[:], m1[:], m2[:], ALU.subtract))
                        mul(M2, VR, st)
                    if j == 13:
                        own.link(mul(VI, VI, ct))
                        v_.tensor_tensor(v_im[:], v_im[:], m2[:], ALU.add).then_inc(s5_x, 1)
                    if j == 15:
                        dve.wait_ge(s5_y, i + 1)
                        v_.scalar_tensor_tensor(y_sb[:], uB[:, 0], cols[:, bass.ds(i + C_D, 1)], tr[:, 1, 0:SEQ],
                                                ALU.mult, ALU.add).then_inc(s5_ysb, 1)
                        dve.wait_ge(gT_hi_ready, i + 1)
                        k1 = bass.ds(i, 1)
                        v_.tensor_tensor(gT_lo[:, k1].rearrange("p k t -> p (k t)"), g_sb[:],
                                         gT_hi[:, k1].rearrange("p k t -> p (k t)").bitcast(F32), ALU.subtract).then_inc(gT_ready, 1)
                    split(ub, j + RING)
                own.leave(4)

            for j in range(16):
                if j == 2:
                    inverse(N_GM, NC, 2)
                if j == 4:
                    dve.wait_ge(rstd_ready, 2)
                    dve.wait_ge(vgain_landed, 16)
                    for h in range(HALVES):
                        pv = proj[:, 28:32, h, :]
                        last = v_.scalar_tensor_tensor(pv, pv, rstd[:, N_GM, h:h + 1],
                                                       vgain[:].rearrange("p (g c) -> p g c", c=P), ALU.mult, ALU.mult)
                    last.then_inc(gm_ready, 1)
                split(U_MID, j + RING)
            for j in range(4):
                if j == 3:
                    for h in range(HALVES):
                        dve.wait_ge(acc_taken[h], G_GATE)
                    v_.tensor_tensor(yc[:], yc[:], sig_g[:], ALU.mult).then_inc(yc_ready, 1)
                split(U_GLU, j + RING)

            with dve.Fori(0, 4) as i:
                own.enter(i, 0, 2)
                ub = i * 16 + U_GATE
                for j in range(16):
                    if j == 1:
                        dve.wait_ge(qk_turned, i + 1)
                        v_.tensor_copy(kT[:].rearrange("p a b -> p (a b)"), side[:, 1]).then_inc(kT_ready, 1)
                    if j == 2:
                        dve.wait_ge(ws_turned, i + 1)
                        v_.tensor_tensor(wsT[:], side[:, 3, 0:P], le[:], ALU.mult).then_inc(wsT_ready, 1)
                    if j == 4:
                        dve.wait_ge(l_ready, i + 1)
                        own.link(v_.scalar_tensor_tensor(sp[:], z_sb[:], 0.0, lz[:], ALU.max, ALU.add))
                        own.link(v_.tensor_tensor(zm[:], z_sb[:], sp[:], ALU.subtract))
                        v_.tensor_tensor(sp[:, 0:P], sp[:, 0:P], lt[:], ALU.mult)
                        v_.tensor_tensor(sp[:, SEQ:], sp[:, SEQ:], lt[:], ALU.mult).then_inc(sp_ready, 1)
                    if j == 5:
                        dve.wait_ge(mixed_done, i + 1)
                        v_.scalar_tensor_tensor(yb[:], side[:, 1, 0:SEQ].rearrange("p (h c) -> p h c", h=2),
                                                cols[:, bass.ds(i + C_BS, 1)],
                                                proj[:, bass.ds(i + 24, 1)].rearrange("p o h c -> p (o h) c"),
                                                ALU.add, ALU.mult).then_inc(yb_ready, 1)
                    if j == 7:
                        dve.wait_ge(tail_done, i + 1)
                        v_.tensor_tensor(zm[:], zm[:], side[:, 3, 0:384], ALU.subtract).then_inc(lw_ready, 1)
                    if j == 8:
                        dve.wait_ge(yb_hi, i + 1)
                        k1 = bass.ds(i, 1)
                        v_.tensor_tensor(ybT_lo[:, k1].rearrange("p k t -> p (k t)"), side[:, 1, SEQ:],
                                         ybT_hi[:, k1].rearrange("p k t -> p (k t)").bitcast(F32), ALU.subtract).then_inc(yb_lo, 1)
                    if j == 9:
                        dve.wait_ge(w_exp, i + 1)
                        v_.tensor_tensor(wz[:, 0:P], wz[:, 0:P], lt[:], ALU.mult)
                        v_.tensor_tensor(wz[:, SEQ:], wz[:, SEQ:], lt[:], ALU.mult).then_inc(wz_ready, 1)
                    if j == 12:
                        dve.wait_ge(ya_hi, i + 1)
                        k2 = bass.ds(i * 2, 2)
                        v_.tensor_tensor(yaT_lo[:, k2].rearrange("p k t -> p (k t)"), side[:, 0],
                                         yaT_hi[:, k2].rearrange("p k t -> p (k t)").bitcast(F32), ALU.subtract).then_inc(ya_lo, 1)
                    split(ub, j + RING)
                own.leave(4)
            turn_lo_parts(T_GLU, ycT_hi, ycT_lo, 0)

            def branches(i, before):
                ub = i * 8 + U_BR
                for j in range(8):
                    if j == 1 and before:
                        turn_lo_parts(i * 2 + (T_BR - 2), xT_hi, xT_lo, i * 4 - 4)
                    if j in (3, 5, 7):
                        br = (j - 3) // 2
                        for h in range(HALVES):
                            wait_acc(h, i * 3 + (G_BR + br), ub + j)
                            if br == 0 and h == 0:
                                dve.wait_ge(acc_taken[1], G_BR)
                            gate = gates[:, bass.ds(i + 4 * br, 1), h].rearrange("p o n -> p (o n)")
                            if br == 0:
                                v_.tensor_tensor(mg[:, h], acc[:, h], gate, ALU.mult).then_inc(acc_taken[h], 1)
                            else:
                                v_.tensor_tensor(mt[:], acc[:, h], gate, ALU.mult).then_inc(acc_taken[h], 1)
                                dve.wait_ge(acc_taken[h], i * 3 + (G_BR + br + 1))
                                last = v_.tensor_tensor(mg[:, h], mg[:, h], mt[:], ALU.add)
                                if br == 2 and h == 1:
                                    last.then_inc(mg_ready, 1)
                                    dve.wait_ge(mg_ready, i + 1)
                                else:
                                    own.link(last)
                    split(ub, j + RING)

            branches(0, False)
            with dve.Fori(1, 4) as i:
                own.enter(i, 1, 3)
                branches(i, True)
                own.leave(3)
            turn_lo_parts(T_BR + 6, xT_hi, xT_lo, 12)

            with dve.Fori(0, 4) as i:
                ub = i * 8 + U_OUT
                for j in range(8):
                    if j == 1:
                        for b in range(2):
                            dve.wait_ge(turn_hi, i * 2 + (T_MEM + b + 1))
                            for k in range(2):
                                kk = i * 4 + (2 * b + k)
                                last = v_.scalar_tensor_tensor(
                                    mT_lo[:, bass.ds(kk, 1)].rearrange("p k t -> p (k t)"), tr[:, b, k * SEQ:(k + 1) * SEQ],
                                    cols[:, bass.ds(kk + C_MEM, 1)],
                                    mT_hi[:, bass.ds(kk, 1)].rearrange("p k t -> p (k t)").bitcast(F32), ALU.mult, ALU.subtract)
                            last.then_inc(turn_lo, 1)
                    if j == 7:
                        dve.wait_ge(gain_landed, 16)
                        gained(None, None, i * 2 + 3, yg, post_gain, i * NC)
                    split(ub, j + RING)

            inverse(N_Y1, D, 10)
            for j in range(CU):
                if j == 0:
                    dve.wait_ge(rstd_ready, 3)
                    dve.wait_ge(xres_landed, 16)
                if 1 <= j < 5:
                    residual(j - 1, yg, N_Y1, x1_ready)
                if 3 <= j < 7:
                    turn_lo_parts(T_X1 + 2 * (j - 3), xT_hi, xT_lo, 4 * (j - 3), C_XAT)
                if j == 5:
                    dve.wait_ge(mq_squared, 4)
                    inverse(N_MEM, D, 0)
                split(U_MK, j + RING)
            for j in range(CU):
                if j == 2:
                    dve.wait_ge(k_turned, 2)
                    v_.tensor_copy(kxT[:, 2:4].rearrange("p a b -> p (a b)"), side[:, 1]).then_inc(kx_ready, 1)
                if j == 4:
                    inverse(N_X1, D, 18)
                split(U_XQ, j + RING)
            MX, NB, SUM, INV = range(4)
            for j in range(CU):
                if j == 1:
                    dve.wait_ge(q_turned, 2)
                    v_.tensor_copy(qxT[:, 2:4].rearrange("p a b -> p (a b)"), side[:, 1]).then_inc(qx_ready, 1)
                if j == 3:
                    dve.wait_ge(xz_done, 1)
                    own.link(v_.tensor_reduce(xsm[:, MX], side[:].rearrange("p a (h m) -> p (a h) m", h=2), AX.X, ALU.max))
                    v_.tensor_scalar(xsm[:, NB], xsm[:, MX], -(XDIM ** -0.5), None, ALU.mult).then_inc(xmax_ready, 1)
                if j in (5, 6):
                    for hd in (0, 1) if j == 5 else (2, 3):
                        dve.wait_ge(xexp_done, hd + 1)
                        own.link(v_.reciprocal(xsm[:, INV, 2 * hd:2 * hd + 2], xsm[:, SUM, 2 * hd:2 * hd + 2]))
                        for h in range(HALVES):
                            last = v_.tensor_scalar(prob[:, hd, h], prob[:, hd, h], xsm[:, INV, 2 * hd + h:2 * hd + h + 1], None, ALU.mult)
                        last.then_inc(xp_ready, 1)
                if j == 7:
                    for hd in range(2, 4):
                        dve.wait_ge(p_turned, hd + 1)
                        v_.tensor_copy(pT[:, hd].rearrange("p a b -> p (a b)"), side[:, hd]).then_inc(pT_ready, 1)
                    for b in range(2):
                        dve.wait_ge(xo_hi, b + 1)
                        v_.tensor_tensor(oT_lo[:, 2 * b:2 * b + 2].rearrange("p a b -> p (a b)"), tr[:, b],
                                         oT_hi[:, 2 * b:2 * b + 2].rearrange("p a b -> p (a b)").bitcast(F32), ALU.subtract).then_inc(xo_lo, 1)
                split(U_MV, j + RING)
            for j in range(8):
                if j % 2:
                    if j == 1:
                        dve.wait_ge(gain_landed, 32)
                    gained(None, None, 19 + 2 * (j // 2), yg, post_gain, (j // 2) * NC)
                split(U_XO, j + RING)
            inverse(N_Y2, D, 26)
            dve.wait_ge(rstd_ready, 6)
            residual(0, yg, N_Y2, x2_ready)
            for n in range(4):
                if n < 3:
                    residual(n + 1, yg, N_Y2, x2_ready)
                turn_lo_parts(T_X2 + 2 * n, xT_hi, xT_lo, 4 * n, C_FFN)

            def ffn_in(i, first):
                ub = i * 16 + U_FI
                for j in range(16):
                    if first and j == 4:
                        inverse(N_X2, D, 34)
                    if not first and j == 2:
                        turn_lo_parts(i * 2 + (T_FFN - 2), hT_hi, hT_lo, i * 4 - 4)
                    if j == 15:
                        if first:
                            dve.wait_ge(rstd_ready, 7)
                        for h in range(HALVES):
                            wait_acc(h, i * 2 + (G_FI + 1), ub + j)
                            dve.wait_ge(acc_taken[h], i * 2 + (G_FI + 1))
                            last = v_.scalar_tensor_tensor(hb[:, h], acc[:, h], rstd[:, N_X2, h:h + 1], silu_g[:, h],
                                                           ALU.mult, ALU.mult)
                            last.then_inc(acc_taken[h], 1)
                    split(ub, j + RING)

            ffn_in(0, True)
            with dve.Fori(1, 11) as i:
                ffn_in(i, False)
            turn_lo_parts(T_FFN + 20, hT_hi, hT_lo, 40)

            for n in range(4):
                for j in range(22 * n, 22 * n + 22):
                    if j == 22 * n + 21:
                        if n == 0:
                            dve.wait_ge(gain_landed, 48)
                        gained(None, None, 35 + 2 * n, yg3, post_gain3, n * NC)
                    split(U_FO, j + RING)
            inverse(N_Y3, D, 42)
            dve.wait_ge(rstd_ready, 8)
            for n in range(4):
                residual(n, yg3, N_Y3, out_ready)

        @block.tensor
        def _(pe):
            def chunk(ub, j0, g, units, hi, lo, side_step=None, first=True, last=True, k0=0, free=True):
                for j in range(units):
                    s = (j0 + j) % RING
                    pe.wait_ge(lo_ready, ub + (j0 + j + 1))
                    for h in range(HALVES):
                        if first and j == 0 and free:
                            pe.wait_ge(acc_taken[h], g)
                        tok = slice(h * P, (h + 1) * P)
                        for k in range(UK):
                            kt = k0 + UK * j + k
                            begin, end = first and j == 0 and k == 0, last and j == units - 1 and k == UK - 1
                            pe.matmul(acc[:, h], hi[:, kt, tok], w_hi[:, s, k], start=begin, stop=False)
                            pe.matmul(acc[:, h], hi[:, kt, tok], w_lo[:, s, k], start=False, stop=False)
                            mm = pe.matmul(acc[:, h], lo[:, kt, tok], w_hi[:, s, k], start=False, stop=end)
                        if h == 0 and last and j == units - 1:
                            mm.then_inc(acc0_full, 1)
                    mm.then_inc(unit_used, 1)
                    if side_step is not None:
                        side_step(j0 + j)

            def turn(t, src):
                for b in range(2):
                    if not isinstance(t, int) or t + b >= 2:
                        pe.wait_ge(turn_lo, t + (b - 1))
                    for k in range(2):
                        for h in range(HALVES):
                            c = (2 * b + k) * P
                            tt = pe.transpose(tr[:, b, k * SEQ + h * P:k * SEQ + (h + 1) * P], src[:, h, c:c + P], ident[:])
                    tt.then_inc(turned, 1)

            def x_turn(n):
                pe.wait_ge(x_landed[n], 16)
                turn(T_X + 2 * n, x_tok[:, :, n * NC:(n + 1) * NC])

            def s5_units(j0, n):
                pe.wait_ge(turn_lo, j0 // 2 * 2 + 2)
                chunk(U_S5, j0, G_S5, n, xT_hi, xT_lo, first=(j0 == 0), last=(j0 + n == CU), k0=UK * j0, free=False)

            pe.wait_ge(const_ready, 2)
            pe.wait_ge(gain_row_landed, 16)
            pe.transpose(side[:, 0, 0:KT], rows[0:KT, :], ident[0:KT, 0:KT]).then_inc(cols_turned, 1)
            x_turn(0)
            x_turn(1)
            s5_units(0, 1)
            s5_units(1, 1)
            pe.wait_ge(ldt_spread, 1)
            pe.transpose(side[:, 1, 0:C_END], rows[0:C_END, :], ident[0:C_END, 0:C_END]).then_inc(cols_turned, 1)
            x_turn(2)
            s5_units(2, 1)
            s5_units(3, 1)
            x_turn(3)
            s5_units(4, 1)
            s5_units(5, 1)
            s5_units(6, 2)

            for c in range(2):
                chunk(U_PRE, CU * c, G_PRE + c, CU, xT_hi, xT_lo)

            with pe.Fori(0, 4) as i:
                def s5_step(j):
                    if j == 0:
                        pe.wait_ge(s5_staged, i + 1)
                        for h in range(HALVES):
                            pe.transpose(side[:, 0, h * P:(h + 1) * P], u_st[:, h], ident[:])
                        for r in range(2):
                            pe.transpose(side[:, 0, SEQ + r * P:SEQ + (r + 1) * P], B_st[:, r].rearrange("p q c -> p (q c)"), ident[:])
                            tt = pe.transpose(tr[:, 0, r * P:(r + 1) * P], C_st[:, r], ident[:])
                        tt.then_inc(s5_turned, 1)
                    if j == 1:
                        pe.wait_ge(s5_uB, i + 1)
                        for r in range(2):
                            for q in range(4):
                                rws = slice(32 * q, 32 * q + 32)
                                mm = pe.matmul(side[:, q, r * SEQ:(r + 1) * SEQ], uB[rws, 1, r * P:(r + 1) * P],
                                               uB[rws, 0, :], start=True, stop=True)
                        mm.then_inc(s5_bu, 1)
                    if j == 14:
                        pe.wait_ge(s5_x, i + 1)
                        for r, part in enumerate((m1, v_im)):
                            for q in range(4):
                                rws = slice(32 * q, 32 * q + 32)
                                mm = pe.matmul(tr[rws, 1, 0:SEQ], Cp[:, r, rws], part[:, q], start=(r == 0), stop=(r == 1))
                        mm.then_inc(s5_y, 1)

                for c in range(2):
                    chunk(i * 16 + U_PROJ, CU * c, i * 2 + (G_PROJ + c), CU, xT_hi, xT_lo, s5_step)
            for c in range(2):
                chunk(U_MID, CU * c, G_MID + c, CU, xT_hi, xT_lo)
            pe.wait_ge(gT_ready, 4)
            for c in range(2):
                chunk(U_GLU, 2 * c, G_GLU + c, 2, gT_hi, gT_lo)

            with pe.Fori(0, 4) as i:
                def head_step(j):
                    if j == 0:
                        pe.wait_ge(qkv_staged, i + 1)
                        for dst, src in ((0, q_st), (1, k_st)):
                            for dc in range(2):
                                for h in range(HALVES):
                                    tt = pe.transpose(side[:, dst, dc * SEQ + h * P:dc * SEQ + (h + 1) * P], src[:, dc, h], ident[:])
                        tt.then_inc(qk_turned, 1)
                    if j == 1:
                        pe.wait_ge(ws_landed, (i + 1) * 16)
                        pe.transpose(side[:, 3, 0:P], ws_st[:], ident[:]).then_inc(ws_turned, 1)
                    if j == 2:
                        pe.wait_ge(qT_ready, i + 1)
                        pe.wait_ge(kT_ready, i + 1)
                        for dc in range(2):
                            pe.matmul(side[:, 2, 0:SEQ], kT[:, dc, 0:P], qT[:, dc, :], start=(dc == 0), stop=(dc == 1))
                        for dc in range(2):
                            mm = pe.matmul(side[:, 2, SEQ:SEQ + P], kT[:, dc, P:], qT[:, dc, P:], start=(dc == 0), stop=(dc == 1))
                        mm.then_inc(z_done, 1)
                    if j == 4:
                        pe.wait_ge(wsT_ready, i + 1)
                        for c in range(2):
                            mm = pe.matmul(side[:, 1, c * P:(1 + c) * P], wsT[:],
                                           proj[:, bass.ds(i + 28, 1), c].rearrange("p o c -> p (o c)"), start=True, stop=True)
                        mm.then_inc(mixed_done, 1)
                    if j == 6:
                        pe.wait_ge(yb_ready, i + 1)
                        for h in range(HALVES):
                            tt = pe.transpose(side[:, 1, SEQ + h * P:SEQ + (h + 1) * P], yb[:, h], ident[:])
                        tt.then_inc(yb_turned, 1)
                    if j == 5:
                        pe.wait_ge(sp_ready, i + 1)
                        pe.matmul(side[:, 3, 0:SEQ], gt[:], sp[:, 0:SEQ], start=True, stop=False)
                        pe.matmul(side[:, 3, P:SEQ], ones[:], sp[:, SEQ:], start=False, stop=True)
                        pe.matmul(side[:, 3, SEQ:SEQ + P], gt[:], sp[:, SEQ:], start=True, stop=True).then_inc(tail_done, 1)
                    if j == 10:
                        pe.wait_ge(wz_ready, i + 1)
                        for dc in range(2):
                            pe.matmul(side[:, 0, dc * SEQ:(dc + 1) * SEQ], v_st[:, dc, 0], wz[:, 0:SEQ], start=True, stop=False)
                            mm = pe.matmul(side[:, 0, dc * SEQ + P:(dc + 1) * SEQ], v_st[:, dc, 1], wz[:, SEQ:], start=False, stop=True)
                        mm.then_inc(ya_done, 1)

                for c in range(2):
                    chunk(i * 16 + U_GATE, CU * c, i * 2 + (G_GATE + c), CU, xT_hi, xT_lo, head_step)
            turn(T_GLU, yc[:])

            def branches(i, before):
                def step(j):
                    if j == 1 and before:
                        pe.wait_ge(mg_ready, i)
                        turn(i * 2 + (T_BR - 2), mg[:])

                ub = i * 8 + U_BR
                chunk(ub, 0, i * 3 + G_BR, 4, yaT_hi, yaT_lo, step)
                chunk(ub, 4, i * 3 + (G_BR + 1), 2, ybT_hi, ybT_lo)
                if not before:
                    pe.wait_ge(turn_lo, T_GLU + 2)
                chunk(ub, 6, i * 3 + (G_BR + 2), 2, ycT_hi, ycT_lo)

            pe.wait_ge(ya_lo, 4)
            pe.wait_ge(yb_lo, 4)
            branches(0, False)
            with pe.Fori(1, 4) as i:
                branches(i, True)
            pe.wait_ge(mg_ready, 4)
            turn(T_BR + 6, mg[:])
            pe.wait_ge(turn_lo, T_BR + 8)

            with pe.Fori(0, 4) as i:
                def mem_step(j):
                    if j == 0:
                        pe.wait_ge(mq_landed, (i + 1) * 16)
                        turn(i * 2 + T_MEM, mq[:])

                chunk(i * 8 + U_OUT, 0, i + G_OUT, CU, xT_hi, xT_lo, mem_step)

            def x1_step(j):
                if 2 <= j < 6:
                    pe.wait_ge(x1_ready, j - 1)
                    turn(T_X1 + 2 * (j - 2), xres[:, :, (j - 2) * NC:(j - 1) * NC])

            def heads_turned(src, done):
                for b in range(2):
                    for hd in range(2 * b, 2 * b + 2):
                        for h in range(HALVES):
                            c = (hd % 2) * SEQ + h * P
                            tt = pe.transpose(side[:, b, c:c + P], src[:, h, hd], ident[:])
                    tt.then_inc(done, 1)

            pe.wait_ge(turn_lo, T_MEM + 8)
            chunk(U_MK, 0, G_MK, CU, mT_hi, mT_lo, x1_step)

            def k_step(j):
                if j == 1:
                    for h in range(HALVES):
                        pe.wait_ge(acc_taken[h], G_MK + 1)
                    heads_turned(k_tok, k_turned)

            pe.wait_ge(turn_lo, T_X1 + 8)
            chunk(U_XQ, 0, G_XQ, CU, xT_hi, xT_lo, k_step)

            def soft_step(j):
                if j == 0:
                    for h in range(HALVES):
                        pe.wait_ge(acc_taken[h], G_XQ + 1)
                    pe.wait_ge(kx_ready, 2)
                    heads_turned(q_tok, q_turned)
                if j == 2:
                    pe.wait_ge(qx_ready, 2)
                    for hd in range(XHEADS):
                        for h in range(HALVES):
                            mm = pe.matmul(side[:, hd, h * SEQ:(h + 1) * SEQ], qxT[:, hd, h * P:(h + 1) * P], kxT[:, hd], start=True, stop=True)
                    mm.then_inc(xz_done, 1)

            chunk(U_MV, 0, G_MV, CU, mT_hi, mT_lo, soft_step)
            for hd in range(XHEADS):
                pe.wait_ge(xp_ready, hd + 1)
                for m in range(2):
                    for h in range(HALVES):
                        c = m * SEQ + h * P
                        tt = pe.transpose(side[:, hd, c:c + P], prob[:, hd, h, m * P:(m + 1) * P], ident[:])
                tt.then_inc(p_turned, 1)
            for h in range(HALVES):
                pe.wait_ge(acc_taken[h], G_MV + 1)
            pe.wait_ge(pT_ready, 4)
            for hd in range(XHEADS):
                for m in range(2):
                    mm = pe.matmul(tr[:, hd // 2, (hd % 2) * SEQ:(hd % 2 + 1) * SEQ], v_tok[:, m, hd], pT[:, hd, m], start=(m == 0), stop=(m == 1))
                if hd % 2:
                    mm.then_inc(xo_done, 1)
            pe.wait_ge(xo_lo, 2)
            for c in range(4):
                chunk(U_XO, 2 * c, G_XO + c, 2, oT_hi, oT_lo)
            for n in range(4):
                pe.wait_ge(x2_ready, n + 1)
                turn(T_X2 + 2 * n, xres[:, :, n * NC:(n + 1) * NC])
            pe.wait_ge(turn_lo, T_X2 + 8)

            def ffn_in(i, first):
                def step(j):
                    if j == 1 and not first:
                        for h in range(HALVES):
                            pe.wait_ge(acc_taken[h], i * 2 + G_FI)
                        turn(i * 2 + (T_FFN - 2), hb[:])

                chunk(i * 16 + U_FI, 0, i * 2 + G_FI, CU, xT_hi, xT_lo, step)
                chunk(i * 16 + U_FI, CU, i * 2 + (G_FI + 1), CU, xT_hi, xT_lo)

            ffn_in(0, True)
            with pe.Fori(1, 11) as i:
                ffn_in(i, False)
            for h in range(HALVES):
                pe.wait_ge(acc_taken[h], G_FO)
            turn(T_FFN + 20, hb[:])
            pe.wait_ge(turn_lo, T_FFN + 22)
            with pe.Fori(0, 2) as i:
                for c in range(2):
                    chunk(i * 44 + U_FO, 22 * c, i * 2 + (G_FO + c), 22, hT_hi, hT_lo)


_INS = ["x", "mem", "mix_pre_gain", "mix_post_gain", "w_in", "gm_v_gain", "gm_w_s", "gm_b_s",
        "s5_lam_re", "s5_lam_im", "s5_log_dt", "s5_b_re", "s5_b_im", "s5_c_re", "s5_c_im", "s5_d",
        "s5_w_glu", "w_br_a", "w_br_b", "w_br_c", "w_out", "xattn_pre_gain", "xattn_post_gain",
        "mem_gain", "w_xq", "w_xkv", "w_xo", "ffn_pre_gain", "ffn_post_gain", "w_ffn_in", "w_ffn_out"]


def kernel(**inputs):
    import numpy as _np
    import concourse.bacc as _bacc
    from concourse import mybir as _mybir
    from concourse.bass_utils import run_bass_kernel_spmd as _run

    nc = _bacc.Bacc("TRN2", target_bir_lowering=False, num_devices=1)
    arrays, args = {}, []
    for name in _INS:
        a = _np.ascontiguousarray(inputs[name])
        arrays[f"in_{name}"] = a
        args.append(nc.dram_tensor(f"in_{name}", a.shape, _mybir.dt.from_np(a.dtype), kind="ExternalInput").ap())
    args.append(nc.dram_tensor("out_0", (1, SEQ, D), F32, kind="ExternalOutput").ap())
    trunk(nc, *args)
    r = _run(nc, [arrays], core_ids=[0])
    return r.results[0]["out_0"]
```

```python
from contextlib import ExitStack
import math

import concourse.bass as bass
from concourse import mybir

F32 = mybir.dt.float32
F32R = mybir.dt.float32r
ACT = mybir.ActivationFunctionType
ALU = mybir.AluOpType
AX = mybir.AxisListType

P = 128
HALVES = 2
SEQ = P * HALVES
D = 2048
NC = 512
KT = D // P
UK = 2
RING = 4
CU = KT // UK

HEADS, HDIM = 4, 256
GROUPS, GCHUNK = 4, 128
S5_PAIRS, S5_TILES = 16, 4
STATE, GCH = 64, 16
XHEADS, XDIM = 4, 128
FFN = 5632
OFF_GATES = 3072 + 1024 + 512
OFF_S5 = 3072 + 1024
EPS = 1e-6

U_S5, U_PRE, U_PROJ, U_MID, U_GLU, U_GATE = 0, 8, 24, 88, 104, 108
U_BR, U_OUT, U_MK, U_XQ, U_MV = 172, 204, 236, 244, 252
U_XO, U_FI, U_FO, U_END = 260, 268, 444, 532
G_S5, G_PRE, G_PROJ, G_MID, G_GLU, G_GATE, G_BR, G_OUT, G_MK, G_XQ, G_MV, G_XO, G_FI, G_FO = (
    0, 1, 3, 11, 13, 15, 23, 35, 39, 40, 41, 42, 46, 68)
T_X, T_GLU, T_BR, T_MEM, T_X1, T_X2, T_FFN = 0, 8, 10, 18, 26, 34, 42
N_X, N_GM, N_Y1, N_MEM, N_X1, N_Y2, N_X2, N_Y3 = range(8)
C_MIX, C_XAT, C_MEM, C_FFN, C_LRE, C_LIM, C_LDT, C_D, C_BS, C_END = 0, 16, 32, 48, 64, 80, 96, 112, 116, 120

TWO_PI = 2 * math.pi
PI_A = 6.28125
PI_B = 0.0019350051879882812
PI_C = TWO_PI - PI_A - PI_B
ROUND = 1.5 * 2 ** 23
PI_MAX = 3.1415925


class Chain:

    def __init__(self, engine, sem):
        self.engine, self.sem, self.count, self.offset = engine, sem, 0, 0

    def enter(self, reg, first, per):
        self.entered, self.per = self.count, per
        self.offset = (reg - first) * per if first else reg * per

    def leave(self, n):
        assert self.count - self.entered == self.per, (self.count - self.entered, self.per)
        self.count, self.offset = self.entered + n * self.per, 0

    def link(self, instruction):
        instruction.then_inc(self.sem, 1)
        self.count += 1
        self.engine.wait_ge(self.sem, self.offset + self.count)


def trunk(nc, x, mem, mix_pre_gain, mix_post_gain, w_in, gm_v_gain, gm_w_s, gm_b_s,
          s5_lam_re, s5_lam_im, s5_log_dt, s5_b_re, s5_b_im, s5_c_re, s5_c_im, s5_d,
          s5_w_glu, w_br_a, w_br_b, w_br_c, w_out, xattn_pre_gain, xattn_post_gain,
          mem_gain, w_xq, w_xkv, w_xo, ffn_pre_gain, ffn_post_gain, w_ffn_in, w_ffn_out, out):
    with ExitStack() as ctx:
        base = (nc.sbuf_base + 31) // 32 * 32
        KB = 1024

        def at(name, kb, shape, dt=F32):
            return nc.alloc_sbuf_tensor_at(name, [P] + shape, dt, offset=base + int(kb * KB))

        def ps(name, shape):
            return ctx.enter_context(nc.psum_tensor(name, shape, F32))

        def sem(name):
            return ctx.enter_context(nc.semaphore(name))

        raw = at("raw", 0, [RING, UK, NC])
        w_hi = at("w_hi", 16, [RING, UK, NC], F32R)
        w_lo = at("w_lo", 32, [RING, UK, NC], F32R)
        xT_hi = at("xT_hi", 48, [KT, SEQ], F32R)
        xT_lo = at("xT_lo", 64, [KT, SEQ], F32R)
        x_tok = at("x_tok", 80, [HALVES, D])
        proj = at("proj", 80, [32, HALVES, P])
        yaT_hi = at("yaT_hi", 80, [8, SEQ], F32R)
        yaT_lo = at("yaT_lo", 88, [8, SEQ], F32R)
        ycT_hi = at("ycT_hi", 96, [4, SEQ], F32R)
        ycT_lo = at("ycT_lo", 100, [4, SEQ], F32R)
        gT_hi = at("gT_hi", 112, [4, SEQ], F32R)
        gT_lo = at("gT_lo", 116, [4, SEQ], F32R)
        ybT_hi = at("ybT_hi", 120, [4, SEQ], F32R)
        ybT_lo = at("ybT_lo", 124, [4, SEQ], F32R)
        vgain = at("vgain", 120, [NC])
        yc = at("yc", 128, [HALVES, NC])
        gates = at("gates", 132, [12, HALVES, NC])
        cosT = at("cosT", 132, [S5_PAIRS, P])
        sinT = at("sinT", 140, [S5_PAIRS, P])
        tabA = at("tabA", 148, [S5_PAIRS, P // 2])
        tabB = at("tabB", 152, [S5_PAIRS, P // 2])
        m1 = at("m1", 148, [4, SEQ])
        m2 = at("m2", 152, [4, SEQ])
        v_re = at("v_re", 156, [4, SEQ])
        v_im = at("v_im", 160, [4, SEQ])
        s5u = at("s5u", 180, [S5_TILES, HALVES, P])
        Bn = at("Bn", 184, [S5_PAIRS, 2, 32])
        Cn = at("Cn", 188, [S5_TILES, 2, P])
        rows = at("rows", 192, [P])
        u_st = at("u_st", 192, [HALVES, P])
        B_st = at("B_st", 193, [2, 4, 32])
        C_st = at("C_st", 194, [2, P])
        uB = at("uB", 195, [2, SEQ])
        Cp = at("Cp", 197, [2, P])
        y_sb = at("y_sb", 198, [SEQ])
        g_sb = at("g_sb", 199, [SEQ])
        ang = at("ang", 200, [8, S5_PAIRS])
        sinA = at("sinA", 200.5, [8, S5_PAIRS])
        cosA = at("cosA", 201, [8, S5_PAIRS])
        prm = at("prm", 201.5, [16, S5_PAIRS])
        carry = at("carry", 202.5 - 4 * 4 * 4 / 1024, [4, 4])
        sig_g = at("sig_g", 132, [HALVES, NC])
        q_st = at("q_st", 180, [2, HALVES, P])
        k_st = at("k_st", 182, [2, HALVES, P])
        v_st = at("v_st", 184, [2, HALVES, P])
        qT = at("qT", 186, [2, SEQ])
        kT = at("kT", 188, [2, SEQ])
        z_sb = at("z_sb", 190, [384])
        ez = at("ez", 191.5, [384])
        lz = at("lz", 193, [384])
        sp = at("sp", 194.5, [384])
        zm = at("zm", 196, [384])
        wz = at("wz", 197.5, [384])
        ws_st = at("ws_st", 199, [P])
        wsT = at("wsT", 199.5, [P])
        yb = at("yb", 200, [HALVES, P])
        xres = at("xres", 180, [HALVES, D])
        mg = at("mg", 196, [HALVES, NC])
        mt = at("mt", 200, [NC])
        mT_hi = at("mT_hi", 80, [KT, SEQ], F32R)
        mT_lo = at("mT_lo", 96, [KT, SEQ], F32R)
        mq = at("mq", 112, [HALVES, NC])
        yg = at("yg", 116, [HALVES, D])
        post_gain = at("post_gain", 132, [D])
        k_tok = at("k_tok", 140, [HALVES, XHEADS, XDIM])
        v_tok = at("v_tok", 144, [HALVES, XHEADS, XDIM])
        q_tok = at("q_tok", 148, [HALVES, XHEADS, XDIM])
        kxT = at("kxT", 152, [XHEADS, SEQ])
        qxT = at("qxT", 156, [XHEADS, SEQ])
        prob = at("prob", 160, [XHEADS, HALVES, SEQ])
        pT = at("pT", 168, [XHEADS, 2, SEQ])
        oT_hi = at("oT_hi", 176, [XHEADS, SEQ], F32R)
        oT_lo = at("oT_lo", 196, [XHEADS, SEQ], F32R)
        xsm = at("xsm", 200, [4, XHEADS * HALVES])
        hT_hi = at("hT_hi", 80, [FFN // P, SEQ], F32R)
        hT_lo = at("hT_lo", 124, [FFN // P, SEQ], F32R)
        silu_g = at("silu_g", 168, [HALVES, NC])
        hb = at("hb", 172, [HALVES, NC])
        yg3 = at("yg3", 48, [HALVES, D])
        post_gain3 = at("post_gain3", 64, [D])
        junk = at("junk", 202.5, [NC])
        ident = at("ident", 204.5, [P])
        lt = at("lt", 205, [P])
        gt = at("gt", 205.5, [P])
        le = at("le", 206, [P])
        ones = at("ones", 206.5, [P])
        cols = at("cols", 207, [P])
        ss = at("ss", 207.5, [4, HALVES, 4])
        inv = at("inv", 207.625, [8, HALVES])
        rstd = at("rstd", 207.6875, [8, HALVES])
        halfpi = at("halfpi", 207.75, [1])
        scrap = at("scrap", 207.78125, [4])

        acc = ps("acc", [P, HALVES, NC])
        side = ps("side", [P, 4, NC])
        tr = ps("tr", [P, 2, NC])

        def bank(b, h):
            return acc[:, h] if b == 0 else tr[:, h] if b == 3 else side[:, 2 * (b - 1) + h]

        w_landed = [sem(f"w_landed{i}") for i in range(RING)]
        hi_ready, lo_ready, unit_used = sem("hi_ready"), sem("lo_ready"), sem("unit_used")
        acc0_full = sem("acc0_full")
        acc_taken = [sem("acc0_taken"), sem("acc1_taken")]
        turned, turn_hi, turn_lo = sem("turned"), sem("turn_hi"), sem("turn_lo")
        inv_ready, rstd_ready = sem("inv_ready"), sem("rstd_ready")
        act_own, dve_own, pool_own = sem("act_own"), sem("dve_own"), sem("pool_own")
        x_landed = [sem(f"x_landed{i}") for i in range(4)]
        gain_row_landed, rows_landed, ldt_spread = sem("gain_row_landed"), sem("rows_landed"), sem("ldt_spread")
        x_squared = sem("x_squared")
        const_ready, cols_turned, cols_ready = sem("const_ready"), sem("cols_turned"), sem("cols_ready")
        bc_zero, bc_landed, vgain_landed = sem("bc_zero"), sem("bc_landed"), sem("vgain_landed")
        prm_dt, prm_ang, prm_sin, table_ready = (
            sem("prm_dt"), sem("prm_ang"), sem("prm_sin"), sem("table_ready"))
        s5_staged, s5_turned, s5_uB, s5_Cp, s5_bu = (
            sem("s5_staged"), sem("s5_turned"), sem("s5_uB"), sem("s5_Cp"), sem("s5_bu"))
        s5_x, s5_y, s5_ysb, s5_gelu, gT_hi_ready, gT_ready = (
            sem("s5_x"), sem("s5_y"), sem("s5_ysb"), sem("s5_gelu"), sem("gT_hi_ready"), sem("gT_ready"))
        gm_gelu, yc_ready = sem("gm_gelu"), sem("yc_ready")
        qkv_staged, qk_turned, qT_ready, kT_ready, z_done, z_ready, l_ready = (
            sem("qkv_staged"), sem("qk_turned"), sem("qT_ready"), sem("kT_ready"), sem("z_done"),
            sem("z_ready"), sem("l_ready"))
        sp_ready, tail_done, lw_ready, w_exp, wz_ready, ya_done, ya_hi, ya_lo = (
            sem("sp_ready"), sem("tail_done"), sem("lw_ready"), sem("w_exp"), sem("wz_ready"),
            sem("ya_done"), sem("ya_hi"), sem("ya_lo"))
        ws_landed, ws_turned, wsT_ready, mixed_done, yb_ready, yb_turned, yb_hi, yb_lo = (
            sem("ws_landed"), sem("ws_turned"), sem("wsT_ready"), sem("mixed_done"), sem("yb_ready"),
            sem("yb_turned"), sem("yb_hi"), sem("yb_lo"))
        mg_ready, xres_landed, gain_landed, mq_landed, mq_squared = (
            sem("mg_ready"), sem("xres_landed"), sem("gain_landed"), sem("mq_landed"), sem("mq_squared"))
        squared, x1_ready, x2_ready = sem("squared"), sem("x1_ready"), sem("x2_ready")
        k_turned, kx_ready, q_turned, qx_ready = sem("k_turned"), sem("kx_ready"), sem("q_turned"), sem("qx_ready")
        xz_done, xmax_ready, xexp_done, xp_ready, p_turned, pT_ready, xo_done, xo_hi, xo_lo = (
            sem("xz_done"), sem("xmax_ready"), sem("xexp_done"), sem("xp_ready"), sem("p_turned"),
            sem("pT_ready"), sem("xo_done"), sem("xo_hi"), sem("xo_lo"))
        y3_scaled, out_ready, out1_ready, out_landed = (
            sem("y3_scaled"), sem("out_ready"), sem("out1_ready"), sem("out_landed"))

        block = ctx.enter_context(nc.Block())

        def kview(w):
            return w.rearrange("(k p) n -> p k n", p=P)

        w_in_k, w_glu_k, wa_k, wb_k, wc_k = (kview(w[0]) for w in (w_in, s5_w_glu, w_br_a, w_br_b, w_br_c))
        w_out_k, w_xq_k, w_xkv_k, w_xo_k = (kview(w[0]) for w in (w_out, w_xq, w_xkv, w_xo))
        w_fi_k, w_fo_k = kview(w_ffn_in[0]), kview(w_ffn_out[0])
        x_v = x[0].rearrange("(h p) d -> p h d", p=P)
        mem_v = mem[0].rearrange("(h p) d -> p h d", p=P)
        out_v = out[0].rearrange("(h p) d -> p h d", p=P)

        @block.sync
        def _(sp_):
            def load(u, slot, src):
                if not isinstance(u, int) or u >= RING:
                    sp_.wait_ge(lo_ready, u - (RING - 1))
                sp_.dma_start(raw[:, slot], src).then_inc(w_landed[slot], 16)

            def load_chunk(u, j0, w, col, units, k0=0):
                for j in range(units):
                    load(u + j0 + j, (j0 + j) % RING,
                         w[:, k0 + UK * j:k0 + UK * (j + 1), bass.ds(col, NC)])

            def load_x(n):
                sp_.dma_start(x_tok[:, :, n * NC:(n + 1) * NC], x_v[:, :, n * NC:(n + 1) * NC]).then_inc(x_landed[n], 16)

            load_x(0)
            load_chunk(U_S5, 0, w_in_k, OFF_S5, 1)
            load_x(1)
            load_chunk(U_S5, 1, w_in_k, OFF_S5, 1, UK)
            load_x(2)
            load_chunk(U_S5, 2, w_in_k, OFF_S5, 1, 2 * UK)
            load_x(3)
            load_chunk(U_S5, 3, w_in_k, OFF_S5, 1, 3 * UK)
            sp_.dma_start(junk[C_LDT:C_LDT + S5_PAIRS, 0:2], s5_log_dt[0].rearrange("(q e) -> q e", e=2)).then_inc(rows_landed, 16)
            for r0, v in ((C_LRE, s5_lam_re), (C_LIM, s5_lam_im)):
                sp_.dma_start(rows[r0:r0 + S5_PAIRS, :].rearrange("q (e n) -> q e n", e=2),
                              v[0].rearrange("(q e) n -> q e n", e=2)).then_inc(rows_landed, 16)
            for r0, v in ((C_XAT, xattn_pre_gain), (C_MEM, mem_gain), (C_FFN, ffn_pre_gain)):
                sp_.dma_start(rows[r0:r0 + KT, :], v[0].rearrange("(k p) -> k p", p=P)).then_inc(rows_landed, 16)
            sp_.dma_start(rows[C_D:C_D + 4, :], s5_d[0].rearrange("(k p) -> k p", p=P)).then_inc(rows_landed, 16)
            sp_.dma_start(rows[C_BS:C_BS + 4, :], gm_b_s[0]).then_inc(rows_landed, 16)
            load_chunk(U_S5, 4, w_in_k, OFF_S5, CU - 4, 4 * UK)
            for c in range(2):
                load_chunk(U_PRE, CU * c, w_in_k, OFF_GATES + (8 + c) * NC, CU)
            with sp_.Fori(0, 4) as i:
                for c in range(2):
                    load_chunk(i * 16 + U_PROJ, CU * c, w_in_k, i * (2 * NC) + c * NC, CU)
            for c in range(2):
                load_chunk(U_MID, CU * c, w_in_k, OFF_GATES + (10 + c) * NC, CU)
            for c in range(2):
                load_chunk(U_GLU, 2 * c, w_glu_k, c * NC, 2)
            with sp_.Fori(0, 4) as i:
                for c in range(2):
                    load_chunk(i * 16 + U_GATE, CU * c, w_in_k, i * (2 * NC) + (OFF_GATES + c * NC), CU)
            with sp_.Fori(0, 4) as i:
                load_chunk(i * 8 + U_BR, 0, wa_k, i * NC, 4)
                load_chunk(i * 8 + U_BR, 4, wb_k, i * NC, 2)
                load_chunk(i * 8 + U_BR, 6, wc_k, i * NC, 2)
            with sp_.Fori(0, 4) as i:
                load_chunk(i * 8 + U_OUT, 0, w_out_k, i * NC, CU)
            load_chunk(U_MK, 0, w_xkv_k, 0, CU)
            load_chunk(U_XQ, 0, w_xq_k, 0, CU)
            load_chunk(U_MV, 0, w_xkv_k, NC, CU)
            for c in range(4):
                load_chunk(U_XO, 2 * c, w_xo_k, c * NC, 2)
            with sp_.Fori(0, 11) as i:
                load_chunk(i * 16 + U_FI, 0, w_fi_k, i * NC, CU)
                load_chunk(i * 16 + U_FI, CU, w_fi_k, i * NC + FFN, CU)
            with sp_.Fori(0, 2) as i:
                for c in range(2):
                    load_chunk(i * 44 + U_FO, 22 * c, w_fo_k, i * (2 * NC) + c * NC, 22)
            for h in range(HALVES):
                sp_.wait_ge(out_ready, h + 1)
                sp_.dma_start(out_v[:, h, 0:NC], xres[:, h, 0:NC]).then_inc(out_landed, 16)
            for n in range(1, 4):
                sp_.wait_ge(out_ready, n + 2)
                sp_.wait_ge(out1_ready, n)
                sp_.dma_start(out_v[:, :, n * NC:(n + 1) * NC], xres[:, :, n * NC:(n + 1) * NC]).then_inc(out_landed, 16)
            sp_.wait_ge(out_landed, 16 * 5)

        @block.gpsimd
        def _(pool):
            own = Chain(pool, pool_own)
            g = nc.gpsimd
            g.memset(halfpi[:], math.pi / 2).then_inc(const_ready, 1)
            own.link(g.memset(ident[:], 0.0))
            g.affine_select(out=ident[:], in_=ident[:], compare_op=ALU.not_equal, fill=1.0, base=0,
                            pattern=[[-1, P]], channel_multiplier=1).then_inc(const_ready, 1)
            g.memset(Bn[:], 0.0).then_inc(bc_zero, 1)
            g.memset(Cn[:], 0.0).then_inc(bc_zero, 1)
            own.link(g.memset(ones[:], 1.0))
            g.affine_select(out=lt[:], in_=ones[:], compare_op=ALU.is_gt, fill=0.0, base=0,
                            pattern=[[1, P]], channel_multiplier=-1).then_inc(const_ready, 1)
            g.affine_select(out=gt[:], in_=ones[:], compare_op=ALU.is_gt, fill=0.0, base=0,
                            pattern=[[-1, P]], channel_multiplier=1).then_inc(const_ready, 1)
            g.affine_select(out=le[:], in_=ones[:], compare_op=ALU.is_ge, fill=0.0, base=0,
                            pattern=[[1, P]], channel_multiplier=-1).then_inc(const_ready, 1)
            pool.wait_ge(bc_zero, 2)
            for r, b in enumerate((s5_b_re, s5_b_im)):
                bv = b[0].rearrange("(q e) n c -> e n q c", e=2)
                for e in range(2):
                    g.dma_start(Bn[e * STATE:(e + 1) * STATE, :, r, e * GCH:(e + 1) * GCH], bv[e]).then_inc(bc_landed, 16)
            for r, c_ in enumerate((s5_c_re, s5_c_im)):
                cv = c_[0].rearrange("(t q e) c n -> q e c t n", q=4, e=2)
                for q in range(4):
                    for e in range(2):
                        p0 = q * 32 + e * GCH
                        g.dma_start(Cn[p0:p0 + GCH, :, r, e * STATE:(e + 1) * STATE], cv[q, e]).then_inc(bc_landed, 16)

            pool.wait_ge(prm_sin, 2)
            own.link(g.memset(cosT[:, :, 0:1], 1.0))
            own.link(g.memset(sinT[:, :, 0:1], 0.0))
            for k in range(7):
                L = 1 << k
                c_, s_ = cosT[:, :, 0:L], sinT[:, :, 0:L]
                ck = cosA[:, k, :].unsqueeze(2).to_broadcast([P, S5_PAIRS, L])
                sk = sinA[:, k, :].unsqueeze(2).to_broadcast([P, S5_PAIRS, L])
                a, b = tabA[:, :, 0:L], tabB[:, :, 0:L]
                g.tensor_tensor(a, c_, ck, ALU.mult)
                own.link(g.tensor_tensor(b, s_, sk, ALU.mult))
                own.link(g.tensor_tensor(cosT[:, :, L:2 * L], a, b, ALU.subtract))
                g.tensor_tensor(a, c_, sk, ALU.mult)
                own.link(g.tensor_tensor(b, s_, ck, ALU.mult))
                last = g.tensor_tensor(sinT[:, :, L:2 * L], a, b, ALU.add)
                if k < 6:
                    own.link(last)
                else:
                    last.then_inc(table_ready, 1)

            def stage_s5(i):
                g.tensor_copy(u_st[:], s5u[:, bass.ds(i, 1)].rearrange("p o h c -> p (o h) c"))
                for r in range(2):
                    g.tensor_copy(B_st[:, r], Bn[:, bass.ds(i * 4, 4), r, :])
                g.tensor_copy(C_st[:], Cn[:, bass.ds(i, 1)].rearrange("p o r c -> p (o r) c")).then_inc(s5_staged, 1)

            for h in range(HALVES):
                pool.wait_ge(acc_taken[h], G_S5 + 1)
            pool.wait_ge(bc_landed, 16 * 20)
            stage_s5(0)
            with pool.Fori(1, S5_TILES) as i:
                pool.wait_ge(s5_turned, i)
                stage_s5(i)

            def stage_head(i):
                for dst, blk in ((q_st, 0), (k_st, 8), (v_st, 16)):
                    last = g.tensor_copy(dst[:], proj[:, bass.ds(i * 2 + blk, 2)])
                last.then_inc(qkv_staged, 1)

            def load_ws(i):
                g.dma_start(ws_st[:], gm_w_s[0][bass.ds(i, 1)].rearrange("o t s -> (o t) s")).then_inc(ws_landed, 16)

            for h in range(HALVES):
                pool.wait_ge(acc_taken[h], G_MID)
            pool.wait_ge(gT_ready, 4)
            stage_head(0)
            load_ws(0)
            with pool.Fori(1, HEADS) as i:
                pool.wait_ge(ya_done, i)
                stage_head(i)
                pool.wait_ge(ws_turned, i)
                load_ws(i)

            pool.wait_ge(yb_lo, 4)
            pool.wait_ge(ya_lo, 4)
            g.dma_start(xres[:], x_v).then_inc(xres_landed, 16)

            def load_mem(i):
                g.dma_start(mq[:], mem_v[:, :, bass.ds(i * NC, NC)]).then_inc(mq_landed, 16)

            load_mem(0)
            pool.wait_ge(mg_ready, 4)
            g.dma_start(post_gain[:], mix_post_gain[0:1].to_broadcast([P, D])).then_inc(gain_landed, 16)
            with pool.Fori(1, 4) as i:
                pool.wait_ge(mq_squared, i)
                load_mem(i)
            for h in range(HALVES):
                pool.wait_ge(acc_taken[h], G_OUT + 4)
            g.dma_start(post_gain[:], xattn_post_gain[0:1].to_broadcast([P, D])).then_inc(gain_landed, 16)
            pool.wait_ge(unit_used, U_FO)
            g.dma_start(post_gain3[:], ffn_post_gain[0:1].to_broadcast([P, D])).then_inc(gain_landed, 16)
            for n in range(1, 4):
                pool.wait_ge(y3_scaled, n)
                q = slice(n * NC, (n + 1) * NC)
                g.tensor_tensor(xres[:, 1, q], xres[:, 1, q], yg3[:, 1, q], ALU.add).then_inc(out1_ready, 1)

        @block.scalar
        def _(act):
            own = Chain(act, act_own)
            a_ = nc.scalar

            def r_of(n, h):
                return rstd[:, n, h:h + 1]

            def split(ub, qb, j):
                u = ub + j
                if isinstance(u, int) and u >= U_END:
                    return
                act.wait_ge(w_landed[j % RING], (qb + j // RING + 1) * 16)
                if not isinstance(u, int) or u >= RING:
                    act.wait_ge(unit_used, u - (RING - 1))
                a_.activation(w_hi[:, j % RING], raw[:, j % RING], ACT.Copy).then_inc(hi_ready, 1)

            def wait_acc(h, g, u_last):
                if h == 0:
                    act.wait_ge(acc0_full, g + 1)
                else:
                    act.wait_ge(unit_used, u_last + 1)

            def take(g, u_last, dst, func, norm=None, b=0):
                for h in range(HALVES):
                    wait_acc(h, g, u_last)
                    src = bank(b, h)
                    d = dst(h)
                    if len(d.shape) == 3:
                        src = src.rearrange("p (b c) -> p b c", c=P)
                    a_.activation(d, src, func, scale=r_of(norm, h) if norm is not None else 1.0).then_inc(acc_taken[h], 1)

            def square(g, u_last, n, col, before, b=0):
                for h in range(HALVES):
                    wait_acc(h, g, u_last)
                    a_.activation(junk[:], bank(b, h), ACT.Square,
                                  accum_out=ss[:, n % 4, h, bass.ds(col, 1)]).then_inc(squared, 1)
                    act.wait_ge(squared, before + (h + 1))

            def square_quarter(n, quarter, before):
                for h in range(HALVES):
                    a_.activation(junk[:], xres[:, h, quarter * NC:(quarter + 1) * NC], ACT.Square,
                                  accum_out=ss[:, n % 4, h, quarter:quarter + 1]).then_inc(squared, 1)
                    act.wait_ge(squared, before + h + 1)

            def turn_hi_parts(t, dst, k0, gain=None):
                for b in range(2):
                    act.wait_ge(turned, t + b + 1)
                    if gain is None:
                        last = a_.activation(dst[:, bass.ds(k0 + 2 * b, 2)].rearrange("p k t -> p (k t)"), tr[:, b], ACT.Copy)
                    else:
                        for k in range(2):
                            last = a_.activation(dst[:, bass.ds(k0 + (2 * b + k), 1)].rearrange("p k t -> p (k t)"),
                                                 tr[:, b, k * SEQ:(k + 1) * SEQ], ACT.Copy,
                                                 scale=cols[:, bass.ds(k0 + (gain + 2 * b + k), 1)])
                    last.then_inc(turn_hi, 1)

            def root(n, k):
                act.wait_ge(inv_ready, k + 1)
                a_.activation(rstd[:, n], inv[:, n], ACT.Sqrt).then_inc(rstd_ready, 1)

            def preload(k, func):
                a_.activation(scrap[:, k:k + 1], halfpi[:], func)

            act.dma_start(rows[C_MIX:C_MIX + KT, :], mix_pre_gain[0].rearrange("(k p) -> k p", p=P)).then_inc(gain_row_landed, 16)
            act.wait_ge(const_ready, 1)
            preload(0, ACT.Exp)

            act.wait_ge(cols_turned, 1)
            a_.activation(cols[:, 0:KT], side[:, 0, 0:KT], ACT.Copy).then_inc(cols_ready, 1)
            act.wait_ge(cols_ready, 1)
            turn_hi_parts(T_X, xT_hi, 0, C_MIX)
            split(0, 0, 0)
            split(0, 0, 1)
            turn_hi_parts(T_X + 2, xT_hi, 4, C_MIX)
            split(0, 0, 2)
            split(0, 0, 3)

            for j in range(CU):
                if j == 0:
                    act.wait_ge(cols_turned, 2)
                    a_.activation(cols[:, KT:C_END], side[:, 1, KT:C_END], ACT.Copy).then_inc(cols_ready, 1)
                    act.wait_ge(cols_ready, 2)
                    a_.activation(prm[:, 0], cols[:, C_LDT:C_LDT + S5_PAIRS], ACT.Exp).then_inc(prm_dt, 1)
                if j in (0, 2):
                    turn_hi_parts(T_X + j + 4, xT_hi, 2 * j + 8, C_MIX)
                if 1 <= j < 5:
                    for h in range(HALVES):
                        a_.activation(junk[:], x_tok[:, h, (j - 1) * NC:j * NC], ACT.Square,
                                      accum_out=ss[:, N_X % 4, h, j - 1:j]).then_inc(x_squared, 1)
                        act.wait_ge(x_squared, 2 * j - 1 + h)
                if j == 5:
                    act.wait_ge(prm_ang, 1)
                    a_.activation(prm[:, 2], prm[:, 3], ACT.Exp).then_inc(prm_sin, 1)
                    a_.activation(cosA[:], cosA[:], ACT.Sin, scale=-1.0, bias=halfpi[:])
                    a_.activation(prm[:, 1], ang[:, 0], ACT.Sin, scale=0.5)
                    a_.activation(sinA[:], ang[:], ACT.Sin).then_inc(prm_sin, 1)
                if j == 6:
                    root(N_X, 0)
                if j == 7:
                    act.wait_ge(rstd_ready, 1)
                    take(G_S5, U_S5 + j, lambda h: s5u[:, :, h, :], ACT.Copy, N_X)
                split(U_S5, 0, j + RING)
            act.dma_start(vgain[:], gm_v_gain[0:1].to_broadcast([P, NC])).then_inc(vgain_landed, 16)

            def gate_chunks(ub, qb, g, slot, n, step, accs=(0, 3)):
                for j in range(CU * n):
                    step(j)
                    if j % CU == CU - 1:
                        c = j // CU
                        take(g + c, ub + j,
                             lambda h: gates[:, bass.ds(slot + c, 1), h, :].rearrange("p o n -> p (o n)"), ACT.Sigmoid, N_X, accs[c])
                    split(ub, qb, j + RING)

            gate_chunks(U_PRE, U_PRE // RING, G_PRE, 8, 2, lambda j: None, (3, 0))

            with act.Fori(0, 4) as i:
                ub, qb = i * 16 + U_PROJ, i * 4 + U_PROJ // RING
                for j in range(16):
                    if j == 0:
                        act.wait_ge(s5_turned, i + 1)
                        a_.activation(uB[:].rearrange("p a b -> p (a b)"), side[:, 0], ACT.Copy).then_inc(s5_uB, 1)
                    if j % CU == CU - 1:
                        c = j // CU
                        take(i * 2 + (G_PROJ + c), ub + j,
                             lambda h: proj[:, bass.ds(i * 8 + 4 * c, 4), h, :], ACT.Copy, N_X)
                    if j == 15:
                        act.wait_ge(s5_ysb, i + 1)
                        a_.activation(g_sb[:], y_sb[:], ACT.Gelu_apprx_tanh).then_inc(s5_gelu, 1)
                        act.wait_ge(s5_gelu, i + 1)
                        a_.activation(gT_hi[:, bass.ds(i, 1)].rearrange("p k t -> p (k t)"), g_sb[:], ACT.Copy).then_inc(gT_hi_ready, 1)
                    split(ub, qb, j + RING)

            def gelu_step(j):
                if j == 0:
                    act.wait_ge(acc_taken[1], G_MID)
                    a_.activation(proj[:, 24:32], proj[:, 24:32], ACT.Gelu_apprx_tanh).then_inc(gm_gelu, 1)
                if j == 1:
                    act.wait_ge(gm_gelu, 1)
                    for h in range(HALVES):
                        a_.activation(junk[:].rearrange("p (g c) -> p g c", c=P), proj[:, 28:32, h, :], ACT.Square,
                                      accum_out=ss[:, N_GM % 4, h, 0:1]).then_inc(squared, 1)
                        act.wait_ge(squared, h + 1)
                if j == 3:
                    root(N_GM, 1)

            gate_chunks(U_MID, U_MID // RING, G_MID, 10, 2, gelu_step)
            for j in range(4):
                if j == 1:
                    take(G_GLU, U_GLU + j, lambda h: yc[:, h], ACT.Copy)
                if j == 3:
                    take(G_GLU + 1, U_GLU + j, lambda h: sig_g[:, h], ACT.Sigmoid, None, 3)
                split(U_GLU, U_GLU // RING, j + RING)

            act.wait_ge(yc_ready, 1)
            with act.Fori(0, 4) as i:
                own.enter(i, 0, 2)

                def head_step(j):
                    if j == 1:
                        act.wait_ge(qk_turned, i + 1)
                        a_.activation(qT[:].rearrange("p a b -> p (a b)"), side[:, 0], ACT.Copy).then_inc(qT_ready, 1)
                    if j == 4:
                        act.wait_ge(z_done, i + 1)
                        a_.activation(z_sb[:], side[:, 2, 0:384], ACT.Copy, scale=HDIM ** -0.5).then_inc(z_ready, 1)
                        act.wait_ge(z_ready, i + 1)
                        own.link(a_.activation(ez[:], z_sb[:], ACT.Abs))
                        own.link(a_.activation(ez[:], ez[:], ACT.Exp, scale=-1.0))
                        a_.activation(lz[:], ez[:], ACT.Ln, bias=1.0).then_inc(l_ready, 1)
                    if j == 10:
                        act.wait_ge(yb_turned, i + 1)
                        a_.activation(ybT_hi[:, bass.ds(i, 1)].rearrange("p k t -> p (k t)"), side[:, 1, SEQ:], ACT.Copy).then_inc(yb_hi, 1)
                    if j == 9:
                        act.wait_ge(lw_ready, i + 1)
                        a_.activation(wz[:], zm[:], ACT.Exp).then_inc(w_exp, 1)
                    if j == 13:
                        act.wait_ge(ya_done, i + 1)
                        a_.activation(yaT_hi[:, bass.ds(i * 2, 2)].rearrange("p k t -> p (k t)"), side[:, 2], ACT.Copy).then_inc(ya_hi, 1)

                gate_chunks(i * 16 + U_GATE, i * 4 + U_GATE // RING, i * 2 + G_GATE, i * 2, 2, head_step)
                own.leave(4)

            def branches(i, before):
                ub, qb = i * 8 + U_BR, i * 2 + U_BR // RING
                for j in range(8):
                    if j == 1 and before:
                        turn_hi_parts(i * 2 + (T_BR - 2), xT_hi, i * 4 - 4)
                    if j == 2 and not before:
                        turn_hi_parts(T_GLU, ycT_hi, 0)
                    split(ub, qb, j + RING)

            branches(0, False)
            with act.Fori(1, 4) as i:
                branches(i, True)

            preload(1, ACT.Sqrt)
            for n in range(4):
                for j in range(CU):
                    if n == 0 and j == 2:
                        turn_hi_parts(T_BR + 6, xT_hi, 12)
                    if j == 4:
                        turn_hi_parts(T_MEM + 2 * n, mT_hi, 4 * n, C_MEM)
                    if j == 5:
                        own.link(a_.activation(junk[:], mq[:, 0], ACT.Square, accum_out=ss[:, N_MEM % 4, 0, n:n + 1]))
                        a_.activation(junk[:], mq[:, 1], ACT.Square, accum_out=ss[:, N_MEM % 4, 1, n:n + 1]).then_inc(mq_squared, 1)
                        act.wait_ge(mq_squared, n + 1)
                    if j == 7:
                        square(G_OUT + n, U_OUT + CU * n + j, N_Y1, n, 2 * n + 2, n % 2)
                    split(U_OUT, U_OUT // RING, CU * n + j + RING)

            for j in range(CU):
                if j == 0:
                    root(N_Y1, 2)
                if j >= 5:
                    turn_hi_parts(T_X1 + 2 * (j - 5), xT_hi, 4 * (j - 5), C_XAT)
                if j == 6:
                    root(N_MEM, 3)
                if j == 7:
                    act.wait_ge(rstd_ready, 4)
                    take(G_MK, U_MK + j, lambda h: k_tok[:, h].rearrange("p a b -> p (a b)"), ACT.Copy, N_MEM)
                split(U_MK, U_MK // RING, j + RING)
            for j in range(CU):
                if j == 0:
                    turn_hi_parts(T_X1 + 6, xT_hi, 12, C_XAT)
                if j < 4:
                    square_quarter(N_X1, j, 10 + 2 * j)
                if j == 2:
                    act.wait_ge(k_turned, 1)
                    a_.activation(kxT[:, 0:2].rearrange("p a b -> p (a b)"), side[:, 0], ACT.Copy).then_inc(kx_ready, 1)
                if j == 5:
                    root(N_X1, 4)
                if j == 7:
                    act.wait_ge(rstd_ready, 5)
                    take(G_XQ, U_XQ + j, lambda h: q_tok[:, h].rearrange("p a b -> p (a b)"), ACT.Copy, N_X1, 2)
                split(U_XQ, U_XQ // RING, j + RING)
            def exps(heads):
                for hd in heads:
                    for h in range(HALVES):
                        c = hd * HALVES + h
                        last = a_.activation(prob[:, hd, h], side[:, hd, h * SEQ:(h + 1) * SEQ], ACT.Exp,
                                             scale=XDIM ** -0.5, bias=xsm[:, 1, c:c + 1], accum_out=xsm[:, 2, c:c + 1])
                    last.then_inc(xexp_done, 1)

            for j in range(CU):
                if j == 0:
                    act.wait_ge(q_turned, 1)
                    a_.activation(qxT[:, 0:2].rearrange("p a b -> p (a b)"), side[:, 0], ACT.Copy).then_inc(qx_ready, 1)
                if j == 3:
                    act.wait_ge(xmax_ready, 1)
                    exps((0, 1))
                if j == 4:
                    exps((2, 3))
                if j == 5:
                    preload(2, ACT.Sqrt)
                if j == 6:
                    for hd in range(2):
                        act.wait_ge(p_turned, hd + 1)
                        a_.activation(pT[:, hd].rearrange("p a b -> p (a b)"), side[:, hd], ACT.Copy).then_inc(pT_ready, 1)
                if j == 7:
                    take(G_MV, U_MV + j, lambda h: v_tok[:, h].rearrange("p a b -> p (a b)"), ACT.Copy, N_MEM)
                    for b in range(2):
                        act.wait_ge(xo_done, b + 1)
                        a_.activation(oT_hi[:, 2 * b:2 * b + 2].rearrange("p a b -> p (a b)"), tr[:, b], ACT.Copy).then_inc(xo_hi, 1)
                split(U_MV, U_MV // RING, j + RING)
            for j in range(8):
                if j % 2:
                    square(G_XO + j // 2, U_XO + j, N_Y2, j // 2, 18 + j - 1, j // 2 % 3)
                if j == 7:
                    root(N_Y2, 5)
                    turn_hi_parts(T_X2, xT_hi, 0, C_FFN)
                split(U_XO, U_XO // RING, j + RING)
            turn_hi_parts(T_X2 + 2, xT_hi, 4, C_FFN)

            def ffn_in(i, first):
                ub, qb = i * 16 + U_FI, i * 4 + U_FI // RING
                for j in range(16):
                    if first and j in (0, 2):
                        turn_hi_parts(T_X2 + 4 + j, xT_hi, 8 + 2 * j, C_FFN)
                    if first and 1 <= j < 5:
                        square_quarter(N_X2, j - 1, 24 + 2 * j)
                    if first and j == 6:
                        root(N_X2, 6)
                    if not first and j == 3:
                        turn_hi_parts(i * 2 + (T_FFN - 2), hT_hi, i * 4 - 4)
                    if j == 7:
                        if first:
                            act.wait_ge(rstd_ready, 7)
                        for h in range(HALVES):
                            wait_acc(h, i * 2 + G_FI, ub + j)
                            a_.activation(silu_g[:, h], acc[:, h], ACT.Silu, scale=r_of(N_X2, h)).then_inc(acc_taken[h], 1)
                    split(ub, qb, j + RING)

            ffn_in(0, True)
            with act.Fori(1, 11) as i:
                ffn_in(i, False)
            preload(3, ACT.Sqrt)
            for n in range(4):
                for j in range(22 * n, 22 * n + 22):
                    if j == 2:
                        turn_hi_parts(T_FFN + 20, hT_hi, 40)
                    if j == 22 * n + 21:
                        square(G_FO + n, U_FO + j, N_Y3, n, 34 + 2 * n, n % 2)
                    split(U_FO, U_FO // RING, j + RING)
            root(N_Y3, 7)
            act.wait_ge(rstd_ready, 8)
            for n in range(1, 4):
                act.wait_ge(acc_taken[1], G_FO + (n + 1))
                q = slice(n * NC, (n + 1) * NC)
                a_.activation(yg3[:, 1, q], yg3[:, 1, q], ACT.Copy, scale=r_of(N_Y3, 1)).then_inc(y3_scaled, 1)

        @block.vector
        def _(dve):
            own = Chain(dve, dve_own)
            v_ = nc.vector

            def split(ub, j):
                u = ub + j
                if isinstance(u, int) and u >= U_END:
                    return
                s = j % RING
                dve.wait_ge(hi_ready, u + 1)
                v_.tensor_tensor(w_lo[:, s], raw[:, s], w_hi[:, s].bitcast(F32), ALU.subtract).then_inc(lo_ready, 1)

            def wait_acc(h, g, u_last):
                if h == 0:
                    dve.wait_ge(acc0_full, g + 1)
                else:
                    dve.wait_ge(unit_used, u_last + 1)

            def turn_lo_parts(t, dst_hi, dst_lo, k0, gain=None, k0_gain=None):
                for b in range(2):
                    dve.wait_ge(turn_hi, t + b + 1)
                    if gain is None:
                        ks = bass.ds(k0 + 2 * b, 2)
                        last = v_.tensor_tensor(dst_lo[:, ks].rearrange("p k t -> p (k t)"), tr[:, b],
                                                dst_hi[:, ks].rearrange("p k t -> p (k t)").bitcast(F32), ALU.subtract)
                    else:
                        for k in range(2):
                            ks = bass.ds(k0 + (2 * b + k), 1)
                            last = v_.scalar_tensor_tensor(
                                dst_lo[:, ks].rearrange("p k t -> p (k t)"), tr[:, b, k * SEQ:(k + 1) * SEQ],
                                cols[:, bass.ds(k0 + (gain + 2 * b + k), 1)],
                                dst_hi[:, ks].rearrange("p k t -> p (k t)").bitcast(F32), ALU.mult, ALU.subtract)
                    last.then_inc(turn_lo, 1)

            def inverse(n, width, squares):
                if squares:
                    dve.wait_ge(squared, squares)
                parts = 1 if n == N_GM else 4
                own.link(v_.tensor_reduce(inv[:, n], ss[:, n % 4, :, 0:parts], AX.X, ALU.add))
                own.link(v_.tensor_scalar(inv[:, n], inv[:, n], 1.0 / width, EPS, ALU.mult, ALU.add))
                v_.reciprocal(inv[:, n], inv[:, n]).then_inc(inv_ready, 1)

            def gained(sq, dst, gain, col, b=0, norm=None):
                for h in range(HALVES):
                    dve.wait_ge(squared, sq + h)
                    if norm is not None and h == 1:
                        inverse(norm, D, 0)
                    v_.tensor_tensor(dst[:, h, bass.ds(col, NC)], bank(b, h), gain[:, bass.ds(col, NC)],
                                     ALU.mult).then_inc(acc_taken[h], 1)

            def residual(n, src, norm, ready, g_end):
                for h in range(HALVES):
                    if n == 3:
                        dve.wait_ge(acc_taken[h], g_end)
                    q = slice(n * NC, (n + 1) * NC)
                    last = v_.scalar_tensor_tensor(xres[:, h, q], src[:, h, q], rstd[:, norm, h:h + 1],
                                                   xres[:, h, q], ALU.mult, ALU.add)
                last.then_inc(ready, 1)

            turn_lo_parts(T_X, xT_hi, xT_lo, 0, C_MIX)
            split(0, 0)
            split(0, 1)
            turn_lo_parts(T_X + 2, xT_hi, xT_lo, 4, C_MIX)
            dve.wait_ge(rows_landed, 16 * 8)
            v_.tensor_copy(rows[C_LDT:C_LDT + S5_PAIRS].rearrange("q (e n) -> q e n", e=2),
                           junk[C_LDT:C_LDT + S5_PAIRS, 0:2].unsqueeze(2).to_broadcast([S5_PAIRS, 2, STATE])).then_inc(ldt_spread, 1)
            split(0, 2)
            split(0, 3)

            DT, S2, EX, XR, TH, KR, RR, XC, PO, MAG, F_RE, F_IM, T1, T2, T3, DEN = range(16)

            def p_(k):
                return prm[:, k]

            def reduce_angle(a, k):
                own.link(v_.tensor_scalar(k, a, 1 / TWO_PI, ROUND, ALU.mult, ALU.add))
                own.link(v_.tensor_scalar(k, k, -ROUND, None, ALU.add))
                for part in (PI_A, PI_B, PI_C):
                    own.link(v_.scalar_tensor_tensor(a, k, -part, a, ALU.mult, ALU.add))

            lre, lim = cols[:, C_LRE:C_LRE + S5_PAIRS], cols[:, C_LIM:C_LIM + S5_PAIRS]

            def s5_angles(step):
                if step == 0:
                    dve.wait_ge(prm_dt, 1)
                    v_.tensor_tensor(p_(XR), lre, p_(DT), ALU.mult)
                    own.link(v_.tensor_tensor(ang[:, 0], lim, p_(DT), ALU.mult))
                    reduce_angle(ang[:, 0], p_(KR))
                    for k in range(1, 8):
                        last = v_.tensor_scalar(ang[:, k], ang[:, 0], float(1 << k), None, ALU.mult)
                    own.link(last)
                else:
                    reduce_angle(ang[:], sinA[:])
                    own.link(v_.tensor_scalar(ang[:], ang[:], PI_MAX, -PI_MAX, ALU.min, ALU.max))
                    v_.scalar_tensor_tensor(cosA[:], ang[:], -1.0, ang[:], ALU.mult, ALU.max).then_inc(prm_ang, 1)

            def s5_magnitude():
                dve.wait_ge(prm_sin, 2)
                own.link(v_.tensor_scalar(p_(XC), p_(XR), 0.5, -0.5, ALU.min, ALU.max))
                own.link(v_.tensor_scalar(p_(PO), p_(XC), 1.0 / math.factorial(10), None, ALU.mult))
                for k in range(9, 0, -1):
                    own.link(v_.scalar_tensor_tensor(p_(PO), p_(PO), 1.0 / math.factorial(k), p_(XC), ALU.add, ALU.mult))
                own.link(v_.tensor_tensor(p_(T1), p_(XC), p_(XR), ALU.not_equal))
                own.link(v_.scalar_tensor_tensor(p_(T2), p_(EX), -1.0, p_(PO), ALU.add, ALU.subtract))
                own.link(v_.tensor_tensor(p_(T2), p_(T2), p_(T1), ALU.mult))
                own.link(v_.tensor_tensor(p_(PO), p_(PO), p_(T2), ALU.add))
                own.link(v_.tensor_scalar(p_(MAG), p_(PO), 1.0, None, ALU.add))

            def s5_factor():
                own.link(v_.tensor_tensor(p_(T1), p_(PO), cosA[:, 0], ALU.mult))
                own.link(v_.scalar_tensor_tensor(p_(T2), p_(S2), -2.0, p_(S2), ALU.mult, ALU.mult))
                own.link(v_.tensor_tensor(p_(T1), p_(T1), p_(T2), ALU.add))
                own.link(v_.tensor_tensor(p_(T2), p_(MAG), sinA[:, 0], ALU.mult))
                own.link(v_.tensor_tensor(p_(DEN), lre, lre, ALU.mult))
                own.link(v_.tensor_tensor(p_(T3), lim, lim, ALU.mult))
                own.link(v_.tensor_tensor(p_(DEN), p_(DEN), p_(T3), ALU.add))
                own.link(v_.reciprocal(p_(DEN), p_(DEN)))
                own.link(v_.tensor_tensor(p_(F_RE), p_(T1), lre, ALU.mult))
                own.link(v_.tensor_tensor(p_(T3), p_(T2), lim, ALU.mult))
                own.link(v_.tensor_tensor(p_(F_RE), p_(F_RE), p_(T3), ALU.add))
                own.link(v_.tensor_tensor(p_(F_RE), p_(F_RE), p_(DEN), ALU.mult))
                own.link(v_.tensor_tensor(p_(F_IM), p_(T2), lre, ALU.mult))
                own.link(v_.tensor_tensor(p_(T3), p_(T1), lim, ALU.mult))
                own.link(v_.tensor_tensor(p_(F_IM), p_(F_IM), p_(T3), ALU.subtract))
                own.link(v_.tensor_tensor(p_(F_IM), p_(F_IM), p_(DEN), ALU.mult))

            for j in range(CU):
                if j in (0, 2):
                    turn_lo_parts(T_X + j + 4, xT_hi, xT_lo, 2 * j + 8, C_MIX)
                if j in (1, 3):
                    s5_angles(j // 2)
                if j == 5:
                    dve.wait_ge(x_squared, 8)
                    inverse(N_X, D, 0)
                split(U_S5, j + RING)
            for j in range(2 * CU):
                if j == 4:
                    s5_magnitude()
                if j == 8:
                    s5_factor()
                split(U_PRE, j + RING)
            dve.wait_ge(table_ready, 1)

            with dve.Fori(0, 4) as i:
                own.enter(i, 0, 12)
                ub = i * 16 + U_PROJ

                def blocks(a):
                    return a.rearrange("p q (c t) -> p q c t", c=2)

                b_re, b_im = blocks(side[:, :, 0:SEQ]), blocks(side[:, :, SEQ:2 * SEQ])
                ct, st = (tab[:, bass.ds(i * 4, 4)].unsqueeze(2).to_broadcast([P, 4, 2, P]) for tab in (cosT, sinT))
                M1, M2, VR, VI = (blocks(a[:]) for a in (m1, m2, v_re, v_im))

                def mul(o, a, b):
                    return v_.tensor_tensor(o, a, b, ALU.mult)

                for j in range(16):
                    if j == 1:
                        dve.wait_ge(s5_turned, i + 1)
                        fr = prm[:, F_RE, bass.ds(i * 4, 4)].unsqueeze(2).to_broadcast([P, 4, 32])
                        fi = prm[:, F_IM, bass.ds(i * 4, 4)].unsqueeze(2).to_broadcast([P, 4, 32])
                        cr = tr[:, 0, 0:P].rearrange("p (q c) -> p q c", q=4)
                        ci = tr[:, 0, P:2 * P].rearrange("p (q c) -> p q c", q=4)
                        t = [m1[:, k, 0:P].rearrange("p (q c) -> p q c", q=4) for k in range(4)]
                        mul(t[0], cr, fr)
                        mul(t[1], ci, fi)
                        mul(t[2], cr, fi)
                        own.link(mul(t[3], ci, fr))
                        v_.tensor_tensor(Cp[:, 0], m1[:, 0, 0:P], m1[:, 1, 0:P], ALU.subtract)
                        v_.scalar_tensor_tensor(Cp[:, 1], m1[:, 2, 0:P], -1.0, m1[:, 3, 0:P], ALU.mult, ALU.subtract).then_inc(s5_Cp, 1)
                    if j == 3:
                        dve.wait_ge(s5_Cp, i + 1)
                        dve.wait_ge(s5_bu, i + 1)
                        mul(M1, b_re, ct)
                        own.link(mul(M2, b_im, st))
                    if j == 4:
                        own.link(v_.tensor_tensor(v_re[:], m1[:], m2[:], ALU.add))
                    if j == 5:
                        mul(M1, b_im, ct)
                        own.link(mul(M2, b_re, st))
                    if j == 6:
                        own.link(v_.tensor_tensor(v_im[:], m1[:], m2[:], ALU.subtract))
                    if j in (7, 9):
                        for q in range(4):
                            mag = prm[:, MAG, bass.ds(i * 4 + q, 1)].to_broadcast([P, P])
                            for r, v in enumerate((VR, VI)):
                                blk = v[:, q, (j - 7) // 2]
                                before = 0.0 if j == 7 else carry[:, r, q:q + 1]
                                last = v_.tensor_tensor_scan(blk, mag, blk, before, ALU.mult, ALU.add)
                        own.link(last)
                    if j == 8:
                        c7, s7 = cosA[:, 7, bass.ds(i * 4, 4)], sinA[:, 7, bass.ds(i * 4, 4)]
                        vr, vi = v_re[:, :, P - 1], v_im[:, :, P - 1]
                        mul(carry[:, 0], vr, c7)
                        mul(carry[:, 1], vi, c7)
                        mul(carry[:, 2], vi, s7)
                        own.link(mul(carry[:, 3], vr, s7))
                        v_.tensor_tensor(carry[:, 0], carry[:, 0], carry[:, 2], ALU.subtract)
                        own.link(v_.tensor_tensor(carry[:, 1], carry[:, 1], carry[:, 3], ALU.add))
                    if j == 10:
                        mul(M1, VR, ct)
                    if j == 11:
                        own.link(mul(M2, VI, st))
                    if j == 12:
                        own.link(v_.tensor_tensor(m1[:], m1[:], m2[:], ALU.subtract))
                        mul(M2, VR, st)
                    if j == 13:
                        own.link(mul(VI, VI, ct))
                        v_.tensor_tensor(v_im[:], v_im[:], m2[:], ALU.add).then_inc(s5_x, 1)
                    if j == 15:
                        dve.wait_ge(s5_y, i + 1)
                        v_.scalar_tensor_tensor(y_sb[:], uB[:, 0], cols[:, bass.ds(i + C_D, 1)], tr[:, 1, 0:SEQ],
                                                ALU.mult, ALU.add).then_inc(s5_ysb, 1)
                        dve.wait_ge(gT_hi_ready, i + 1)
                        k1 = bass.ds(i, 1)
                        v_.tensor_tensor(gT_lo[:, k1].rearrange("p k t -> p (k t)"), g_sb[:],
                                         gT_hi[:, k1].rearrange("p k t -> p (k t)").bitcast(F32), ALU.subtract).then_inc(gT_ready, 1)
                    split(ub, j + RING)
                own.leave(4)

            for j in range(16):
                if j == 2:
                    inverse(N_GM, NC, 2)
                if j == 4:
                    dve.wait_ge(rstd_ready, 2)
                    dve.wait_ge(vgain_landed, 16)
                    for h in range(HALVES):
                        pv = proj[:, 28:32, h, :]
                        v_.scalar_tensor_tensor(pv, pv, rstd[:, N_GM, h:h + 1],
                                                       vgain[:].rearrange("p (g c) -> p g c", c=P), ALU.mult, ALU.mult)
                split(U_MID, j + RING)
            for j in range(4):
                if j == 3:
                    for h in range(HALVES):
                        dve.wait_ge(acc_taken[h], G_GATE)
                    v_.tensor_tensor(yc[:], yc[:], sig_g[:], ALU.mult).then_inc(yc_ready, 1)
                split(U_GLU, j + RING)

            with dve.Fori(0, 4) as i:
                own.enter(i, 0, 2)
                ub = i * 16 + U_GATE
                for j in range(16):
                    if j == 1:
                        dve.wait_ge(qk_turned, i + 1)
                        v_.tensor_copy(kT[:].rearrange("p a b -> p (a b)"), side[:, 1]).then_inc(kT_ready, 1)
                    if j == 3:
                        dve.wait_ge(ws_turned, i + 1)
                        v_.tensor_tensor(wsT[:], side[:, 3, 0:P], le[:], ALU.mult).then_inc(wsT_ready, 1)
                    if j == 5:
                        dve.wait_ge(l_ready, i + 1)
                        own.link(v_.scalar_tensor_tensor(sp[:], z_sb[:], 0.0, lz[:], ALU.max, ALU.add))
                        own.link(v_.tensor_tensor(zm[:], z_sb[:], sp[:], ALU.subtract))
                        v_.tensor_tensor(sp[:, 0:P], sp[:, 0:P], lt[:], ALU.mult)
                        v_.tensor_tensor(sp[:, SEQ:], sp[:, SEQ:], lt[:], ALU.mult).then_inc(sp_ready, 1)
                    if j == 6:
                        dve.wait_ge(mixed_done, i + 1)
                        v_.scalar_tensor_tensor(yb[:], side[:, 1, 0:SEQ].rearrange("p (h c) -> p h c", h=2),
                                                cols[:, bass.ds(i + C_BS, 1)],
                                                proj[:, bass.ds(i + 24, 1)].rearrange("p o h c -> p (o h) c"),
                                                ALU.add, ALU.mult).then_inc(yb_ready, 1)
                    if j == 8:
                        dve.wait_ge(tail_done, i + 1)
                        v_.tensor_tensor(zm[:], zm[:], side[:, 3, 0:384], ALU.subtract).then_inc(lw_ready, 1)
                    if j == 12:
                        dve.wait_ge(yb_hi, i + 1)
                        k1 = bass.ds(i, 1)
                        v_.tensor_tensor(ybT_lo[:, k1].rearrange("p k t -> p (k t)"), side[:, 1, SEQ:],
                                         ybT_hi[:, k1].rearrange("p k t -> p (k t)").bitcast(F32), ALU.subtract).then_inc(yb_lo, 1)
                    if j == 10:
                        dve.wait_ge(w_exp, i + 1)
                        v_.tensor_tensor(wz[:, 0:P], wz[:, 0:P], lt[:], ALU.mult)
                        v_.tensor_tensor(wz[:, SEQ:], wz[:, SEQ:], lt[:], ALU.mult).then_inc(wz_ready, 1)
                    if j == 14:
                        dve.wait_ge(ya_hi, i + 1)
                        k2 = bass.ds(i * 2, 2)
                        v_.tensor_tensor(yaT_lo[:, k2].rearrange("p k t -> p (k t)"), side[:, 2],
                                         yaT_hi[:, k2].rearrange("p k t -> p (k t)").bitcast(F32), ALU.subtract).then_inc(ya_lo, 1)
                    split(ub, j + RING)
                own.leave(4)

            def branches(i, before):
                ub = i * 8 + U_BR
                for j in range(8):
                    if j == 1 and before:
                        turn_lo_parts(i * 2 + (T_BR - 2), xT_hi, xT_lo, i * 4 - 4)
                    if j == 2 and not before:
                        turn_lo_parts(T_GLU, ycT_hi, ycT_lo, 0)
                    if j in (3, 5, 7):
                        br = (j - 3) // 2
                        for h in range(HALVES):
                            wait_acc(h, i * 3 + (G_BR + br), ub + j)
                            if br == 0 and h == 0:
                                dve.wait_ge(acc_taken[1], G_BR)
                            gate = gates[:, bass.ds(i + 4 * br, 1), h].rearrange("p o n -> p (o n)")
                            if br == 0:
                                v_.tensor_tensor(mg[:, h], bank(br, h), gate, ALU.mult).then_inc(acc_taken[h], 1)
                            else:
                                v_.tensor_tensor(mt[:], bank(br, h), gate, ALU.mult).then_inc(acc_taken[h], 1)
                                dve.wait_ge(acc_taken[h], i * 3 + (G_BR + br + 1))
                                last = v_.tensor_tensor(mg[:, h], mg[:, h], mt[:], ALU.add)
                                if br == 2 and h == 1:
                                    last.then_inc(mg_ready, 1)
                                    dve.wait_ge(mg_ready, i + 1)
                                else:
                                    own.link(last)
                    split(ub, j + RING)

            branches(0, False)
            with dve.Fori(1, 4) as i:
                own.enter(i, 1, 3)
                branches(i, True)
                own.leave(3)

            for n in range(4):
                for j in range(CU):
                    if n == 0 and j == 2:
                        turn_lo_parts(T_BR + 6, xT_hi, xT_lo, 12)
                    if j == 4:
                        turn_lo_parts(T_MEM + 2 * n, mT_hi, mT_lo, 4 * n, C_MEM)
                    if j == 7:
                        dve.wait_ge(gain_landed, 16)
                        gained(2 * n + 3, yg, post_gain, n * NC, n % 2, N_Y1 if n == 3 else None)
                    split(U_OUT, CU * n + j + RING)

            for j in range(CU):
                if j == 0:
                    dve.wait_ge(rstd_ready, 3)
                    dve.wait_ge(xres_landed, 16)
                if 1 <= j < 5:
                    residual(j - 1, yg, N_Y1, x1_ready, G_MK)
                if j >= 5:
                    turn_lo_parts(T_X1 + 2 * (j - 5), xT_hi, xT_lo, 4 * (j - 5), C_XAT)
                if j == 5:
                    dve.wait_ge(mq_squared, 4)
                    inverse(N_MEM, D, 0)
                split(U_MK, j + RING)
            for j in range(CU):
                if j == 0:
                    turn_lo_parts(T_X1 + 6, xT_hi, xT_lo, 12, C_XAT)
                if j == 2:
                    dve.wait_ge(k_turned, 2)
                    v_.tensor_copy(kxT[:, 2:4].rearrange("p a b -> p (a b)"), side[:, 1]).then_inc(kx_ready, 1)
                if j == 4:
                    inverse(N_X1, D, 18)
                split(U_XQ, j + RING)
            MX, NB, SUM, INV = range(4)
            for j in range(CU):
                if j == 0:
                    dve.wait_ge(q_turned, 2)
                    v_.tensor_copy(qxT[:, 2:4].rearrange("p a b -> p (a b)"), side[:, 1]).then_inc(qx_ready, 1)
                if j == 2:
                    dve.wait_ge(xz_done, 1)
                    own.link(v_.tensor_reduce(xsm[:, MX], side[:].rearrange("p a (h m) -> p (a h) m", h=2), AX.X, ALU.max))
                    v_.tensor_scalar(xsm[:, NB], xsm[:, MX], -(XDIM ** -0.5), None, ALU.mult).then_inc(xmax_ready, 1)
                if j in (4, 5):
                    for hd in (0, 1) if j == 4 else (2, 3):
                        dve.wait_ge(xexp_done, hd + 1)
                        own.link(v_.reciprocal(xsm[:, INV, 2 * hd:2 * hd + 2], xsm[:, SUM, 2 * hd:2 * hd + 2]))
                        for h in range(HALVES):
                            last = v_.tensor_scalar(prob[:, hd, h], prob[:, hd, h], xsm[:, INV, 2 * hd + h:2 * hd + h + 1], None, ALU.mult)
                        last.then_inc(xp_ready, 1)
                if j == 6:
                    for hd in range(2, 4):
                        dve.wait_ge(p_turned, hd + 1)
                        v_.tensor_copy(pT[:, hd].rearrange("p a b -> p (a b)"), side[:, hd]).then_inc(pT_ready, 1)
                if j == 7:
                    for b in range(2):
                        dve.wait_ge(xo_hi, b + 1)
                        v_.tensor_tensor(oT_lo[:, 2 * b:2 * b + 2].rearrange("p a b -> p (a b)"), tr[:, b],
                                         oT_hi[:, 2 * b:2 * b + 2].rearrange("p a b -> p (a b)").bitcast(F32), ALU.subtract).then_inc(xo_lo, 1)
                split(U_MV, j + RING)
            for j in range(8):
                if j % 2:
                    if j == 1:
                        dve.wait_ge(gain_landed, 32)
                    gained(19 + 2 * (j // 2), yg, post_gain, (j // 2) * NC, j // 2 % 3, N_Y2 if j == 7 else None)
                if j == 7:
                    dve.wait_ge(rstd_ready, 6)
                    residual(0, yg, N_Y2, x2_ready, G_XO + 4)
                    residual(1, yg, N_Y2, x2_ready, G_XO + 4)
                    turn_lo_parts(T_X2, xT_hi, xT_lo, 0, C_FFN)
                split(U_XO, j + RING)
            residual(2, yg, N_Y2, x2_ready, G_XO + 4)
            turn_lo_parts(T_X2 + 2, xT_hi, xT_lo, 4, C_FFN)

            def ffn_in(i, first):
                ub = i * 16 + U_FI
                for j in range(16):
                    if first and j == 0:
                        residual(3, yg, N_Y2, x2_ready, G_XO + 4)
                    if first and j in (0, 2):
                        turn_lo_parts(T_X2 + 4 + j, xT_hi, xT_lo, 8 + 2 * j, C_FFN)
                    if first and j == 5:
                        inverse(N_X2, D, 34)
                    if not first and j == 3:
                        turn_lo_parts(i * 2 + (T_FFN - 2), hT_hi, hT_lo, i * 4 - 4)
                    if j == 15:
                        if first:
                            dve.wait_ge(rstd_ready, 7)
                        for h in range(HALVES):
                            wait_acc(h, i * 2 + (G_FI + 1), ub + j)
                            dve.wait_ge(acc_taken[h], i * 2 + (G_FI + 1))
                            last = v_.scalar_tensor_tensor(hb[:, h], bank(1, h), rstd[:, N_X2, h:h + 1], silu_g[:, h],
                                                           ALU.mult, ALU.mult)
                            last.then_inc(acc_taken[h], 1)
                    split(ub, j + RING)

            ffn_in(0, True)
            with dve.Fori(1, 11) as i:
                ffn_in(i, False)

            for n in range(4):
                for j in range(22 * n, 22 * n + 22):
                    if j == 2:
                        turn_lo_parts(T_FFN + 20, hT_hi, hT_lo, 40)
                    if j == 22 * n + 21:
                        if n == 0:
                            dve.wait_ge(gain_landed, 48)
                        gained(35 + 2 * n, yg3, post_gain3, n * NC, n % 2, N_Y3 if n == 3 else None)
                    split(U_FO, j + RING)
            dve.wait_ge(rstd_ready, 8)
            for n in range(4):
                for h in range(HALVES if n == 0 else 1):
                    if n == 3:
                        dve.wait_ge(acc_taken[h], G_FO + 4)
                    q = slice(n * NC, (n + 1) * NC)
                    v_.scalar_tensor_tensor(xres[:, h, q], yg3[:, h, q], rstd[:, N_Y3, h:h + 1],
                                            xres[:, h, q], ALU.mult, ALU.add).then_inc(out_ready, 1)

        @block.tensor
        def _(pe):
            def chunk(ub, j0, g, units, hi, lo, side_step=None, first=True, last=True, k0=0, b=0, lag=1):
                for j in range(units):
                    s = (j0 + j) % RING
                    pe.wait_ge(lo_ready, ub + (j0 + j + 1))
                    for h in range(HALVES):
                        if first and j == 0 and lag:
                            pe.wait_ge(acc_taken[h], g + (1 - lag))
                        tok = slice(h * P, (h + 1) * P)
                        for k in range(UK):
                            kt = k0 + UK * j + k
                            begin, end = first and j == 0 and k == 0, last and j == units - 1 and k == UK - 1
                            pe.matmul(bank(b, h), hi[:, kt, tok], w_hi[:, s, k], start=begin, stop=False)
                            pe.matmul(bank(b, h), hi[:, kt, tok], w_lo[:, s, k], start=False, stop=False)
                            mm = pe.matmul(bank(b, h), lo[:, kt, tok], w_hi[:, s, k], start=False, stop=end)
                        if h == 0 and last and j == units - 1:
                            mm.then_inc(acc0_full, 1)
                    mm.then_inc(unit_used, 1)
                    if side_step is not None:
                        side_step(j0 + j)

            def turn(t, src):
                for b in range(2):
                    if not isinstance(t, int) or t + b >= 2:
                        pe.wait_ge(turn_lo, t + (b - 1))
                    for k in range(2):
                        for h in range(HALVES):
                            c = (2 * b + k) * P
                            tt = pe.transpose(tr[:, b, k * SEQ + h * P:k * SEQ + (h + 1) * P], src[:, h, c:c + P], ident[:])
                    tt.then_inc(turned, 1)

            def x_turn(n):
                pe.wait_ge(x_landed[n], 16)
                turn(T_X + 2 * n, x_tok[:, :, n * NC:(n + 1) * NC])

            def s5_units(j0, n):
                pe.wait_ge(turn_lo, j0 // 2 * 2 + 2)
                chunk(U_S5, j0, G_S5, n, xT_hi, xT_lo, first=(j0 == 0), last=(j0 + n == CU), k0=UK * j0, lag=0)

            pe.wait_ge(const_ready, 2)
            pe.wait_ge(gain_row_landed, 16)
            pe.transpose(side[:, 0, 0:KT], rows[0:KT, :], ident[0:KT, 0:KT]).then_inc(cols_turned, 1)
            x_turn(0)
            x_turn(1)
            s5_units(0, 1)
            s5_units(1, 1)
            pe.wait_ge(ldt_spread, 1)
            pe.transpose(side[:, 1, 0:C_END], rows[0:C_END, :], ident[0:C_END, 0:C_END]).then_inc(cols_turned, 1)
            x_turn(2)
            s5_units(2, 1)
            s5_units(3, 1)
            x_turn(3)
            s5_units(4, 1)
            s5_units(5, 1)
            s5_units(6, 2)

            for c in range(2):
                chunk(U_PRE, CU * c, G_PRE + c, CU, xT_hi, xT_lo, b=3 - 3 * c, lag=2 * c)

            with pe.Fori(0, 4) as i:
                def s5_step(j):
                    if j == 0:
                        pe.wait_ge(s5_staged, i + 1)
                        for h in range(HALVES):
                            pe.transpose(side[:, 0, h * P:(h + 1) * P], u_st[:, h], ident[:])
                        for r in range(2):
                            pe.transpose(side[:, 0, SEQ + r * P:SEQ + (r + 1) * P], B_st[:, r].rearrange("p q c -> p (q c)"), ident[:])
                            tt = pe.transpose(tr[:, 0, r * P:(r + 1) * P], C_st[:, r], ident[:])
                        tt.then_inc(s5_turned, 1)
                    if j == 2:
                        pe.wait_ge(s5_uB, i + 1)
                        for r in range(2):
                            for q in range(4):
                                rws = slice(32 * q, 32 * q + 32)
                                mm = pe.matmul(side[:, q, r * SEQ:(r + 1) * SEQ], uB[rws, 1, r * P:(r + 1) * P],
                                               uB[rws, 0, :], start=True, stop=True)
                        mm.then_inc(s5_bu, 1)
                    if j == 15:
                        pe.wait_ge(s5_x, i + 1)
                        for r, part in enumerate((m1, v_im)):
                            for q in range(4):
                                rws = slice(32 * q, 32 * q + 32)
                                mm = pe.matmul(tr[rws, 1, 0:SEQ], Cp[:, r, rws], part[:, q], start=(r == 0), stop=(r == 1))
                        mm.then_inc(s5_y, 1)

                for c in range(2):
                    chunk(i * 16 + U_PROJ, CU * c, i * 2 + (G_PROJ + c), CU, xT_hi, xT_lo, s5_step)
            for c in range(2):
                if c == 1:
                    pe.wait_ge(gT_ready, 4)
                chunk(U_MID, CU * c, G_MID + c, CU, xT_hi, xT_lo, b=3 * c, lag=1 + c)
            for c in range(2):
                chunk(U_GLU, 2 * c, G_GLU + c, 2, gT_hi, gT_lo, b=3 * c, lag=2)

            with pe.Fori(0, 4) as i:
                def head_step(j):
                    if j == 0:
                        pe.wait_ge(qkv_staged, i + 1)
                        for dst, src in ((0, q_st), (1, k_st)):
                            for dc in range(2):
                                for h in range(HALVES):
                                    tt = pe.transpose(side[:, dst, dc * SEQ + h * P:dc * SEQ + (h + 1) * P], src[:, dc, h], ident[:])
                        tt.then_inc(qk_turned, 1)
                    if j == 1:
                        pe.wait_ge(ws_landed, (i + 1) * 16)
                        pe.transpose(side[:, 3, 0:P], ws_st[:], ident[:]).then_inc(ws_turned, 1)
                    if j == 3:
                        pe.wait_ge(qT_ready, i + 1)
                        pe.wait_ge(kT_ready, i + 1)
                        for dc in range(2):
                            pe.matmul(side[:, 2, 0:SEQ], kT[:, dc, 0:P], qT[:, dc, :], start=(dc == 0), stop=(dc == 1))
                        for dc in range(2):
                            mm = pe.matmul(side[:, 2, SEQ:SEQ + P], kT[:, dc, P:], qT[:, dc, P:], start=(dc == 0), stop=(dc == 1))
                        mm.then_inc(z_done, 1)
                    if j == 5:
                        pe.wait_ge(wsT_ready, i + 1)
                        for c in range(2):
                            mm = pe.matmul(side[:, 1, c * P:(1 + c) * P], wsT[:],
                                           proj[:, bass.ds(i + 28, 1), c].rearrange("p o c -> p (o c)"), start=True, stop=True)
                        mm.then_inc(mixed_done, 1)
                    if j == 7:
                        pe.wait_ge(sp_ready, i + 1)
                        pe.matmul(side[:, 3, 0:SEQ], gt[:], sp[:, 0:SEQ], start=True, stop=False)
                        pe.matmul(side[:, 3, P:SEQ], ones[:], sp[:, SEQ:], start=False, stop=True)
                        pe.matmul(side[:, 3, SEQ:SEQ + P], gt[:], sp[:, SEQ:], start=True, stop=True).then_inc(tail_done, 1)
                    if j == 9:
                        pe.wait_ge(yb_ready, i + 1)
                        for h in range(HALVES):
                            tt = pe.transpose(side[:, 1, SEQ + h * P:SEQ + (h + 1) * P], yb[:, h], ident[:])
                        tt.then_inc(yb_turned, 1)
                    if j == 12:
                        pe.wait_ge(wz_ready, i + 1)
                        for dc in range(2):
                            pe.matmul(side[:, 2, dc * SEQ:(dc + 1) * SEQ], v_st[:, dc, 0], wz[:, 0:SEQ], start=True, stop=False)
                            mm = pe.matmul(side[:, 2, dc * SEQ + P:(dc + 1) * SEQ], v_st[:, dc, 1], wz[:, SEQ:], start=False, stop=True)
                        mm.then_inc(ya_done, 1)

                for c in range(2):
                    chunk(i * 16 + U_GATE, CU * c, i * 2 + (G_GATE + c), CU, xT_hi, xT_lo, head_step, b=3 * c, lag=2)

            def branches(i, before):
                def step(j):
                    if j == 1 and before:
                        pe.wait_ge(mg_ready, i)
                        turn(i * 2 + (T_BR - 2), mg[:])
                    if j == 2 and not before:
                        for h in range(HALVES):
                            pe.wait_ge(acc_taken[h], G_BR)
                        turn(T_GLU, yc[:])

                ub = i * 8 + U_BR
                chunk(ub, 0, i * 3 + G_BR, 4, yaT_hi, yaT_lo, step, lag=3 if before else 2)
                chunk(ub, 4, i * 3 + (G_BR + 1), 2, ybT_hi, ybT_lo, b=1, lag=3)
                if not before:
                    pe.wait_ge(turn_lo, T_GLU + 2)
                chunk(ub, 6, i * 3 + (G_BR + 2), 2, ycT_hi, ycT_lo, b=2, lag=3)

            pe.wait_ge(ya_lo, 4)
            pe.wait_ge(yb_lo, 4)
            branches(0, False)
            with pe.Fori(1, 4) as i:
                branches(i, True)

            for n in range(4):
                def out_step(j):
                    if j == 1:
                        pe.wait_ge(mg_ready, 4)
                        turn(T_BR + 6, mg[:])
                    if j == CU * n + 3:
                        pe.wait_ge(mq_landed, (n + 1) * 16)
                        turn(n * 2 + T_MEM, mq[:])

                if n == 0:
                    pe.wait_ge(turn_lo, T_BR + 6)
                chunk(U_OUT, CU * n, n + G_OUT, 6, xT_hi, xT_lo, out_step, last=False, b=n % 2, lag=2)
                if n == 0:
                    pe.wait_ge(turn_lo, T_BR + 8)
                chunk(U_OUT, CU * n + 6, n + G_OUT, 2, xT_hi, xT_lo, first=False, k0=6 * UK, b=n % 2)

            def x1_step(j):
                if 4 <= j < 8:
                    pe.wait_ge(x1_ready, j - 3)
                    turn(T_X1 + 2 * (j - 4), xres[:, :, (j - 4) * NC:(j - 3) * NC])

            def heads_turned(src, done):
                for b in range(2):
                    for hd in range(2 * b, 2 * b + 2):
                        for h in range(HALVES):
                            c = (hd % 2) * SEQ + h * P
                            tt = pe.transpose(side[:, b, c:c + P], src[:, h, hd], ident[:])
                    tt.then_inc(done, 1)

            pe.wait_ge(turn_lo, T_MEM + 8)
            chunk(U_MK, 0, G_MK, CU, mT_hi, mT_lo, x1_step, lag=2)

            def k_step(j):
                if j == 1:
                    for h in range(HALVES):
                        pe.wait_ge(acc_taken[h], G_MK + 1)
                    heads_turned(k_tok, k_turned)

            for n in range(4):
                pe.wait_ge(turn_lo, T_X1 + 2 * n + 2)
                chunk(U_XQ, 2 * n, G_XQ, 2, xT_hi, xT_lo, k_step, first=(n == 0), last=(n == 3), k0=4 * n, b=2, lag=2)

            def soft_step(j):
                if j == 0:
                    for h in range(HALVES):
                        pe.wait_ge(acc_taken[h], G_XQ + 1)
                    pe.wait_ge(kx_ready, 2)
                    heads_turned(q_tok, q_turned)
                if j == 2:
                    pe.wait_ge(qx_ready, 2)
                    for hd in range(XHEADS):
                        for h in range(HALVES):
                            mm = pe.matmul(side[:, hd, h * SEQ:(h + 1) * SEQ], qxT[:, hd, h * P:(h + 1) * P], kxT[:, hd], start=True, stop=True)
                    mm.then_inc(xz_done, 1)
                if j == 6:
                    for hd in range(XHEADS):
                        pe.wait_ge(xp_ready, hd + 1)
                        for m in range(2):
                            for h in range(HALVES):
                                c = m * SEQ + h * P
                                tt = pe.transpose(side[:, hd, c:c + P], prob[:, hd, h, m * P:(m + 1) * P], ident[:])
                        tt.then_inc(p_turned, 1)

            chunk(U_MV, 0, G_MV, CU, mT_hi, mT_lo, soft_step, lag=2)
            pe.wait_ge(pT_ready, 4)
            for pair in range(2):
                for m in range(2):
                    pe.wait_ge(acc_taken[m], G_MV + 1)
                    for b in range(2):
                        mm = pe.matmul(tr[:, b, pair * SEQ:(pair + 1) * SEQ], v_tok[:, m, 2 * b + pair], pT[:, 2 * b + pair, m],
                                       start=(m == 0), stop=(m == 1))
                        if pair == 1 and m == 1:
                            mm.then_inc(xo_done, 1)
            for k in range(2):
                pe.wait_ge(xo_lo, k + 1)
                chunk(U_XO, k, G_XO, 1, oT_hi, oT_lo, first=(k == 0), last=(k == 1), k0=UK * k)
            for c in range(1, 4):
                chunk(U_XO, 2 * c, G_XO + c, 2, oT_hi, oT_lo, b=c % 3, lag=3)

            def x2_turn(n):
                pe.wait_ge(x2_ready, n + 1)
                turn(T_X2 + 2 * n, xres[:, :, n * NC:(n + 1) * NC])

            x2_turn(0)
            x2_turn(1)
            for n in range(4):
                pe.wait_ge(turn_lo, T_X2 + 2 * n + 2)
                chunk(U_FI, 2 * n, G_FI, 2, xT_hi, xT_lo, first=(n == 0), last=(n == 3), k0=4 * n)
                if n < 2:
                    x2_turn(n + 2)

            def ffn_in(i, first):
                def step(j):
                    if j == 2:
                        for h in range(HALVES):
                            pe.wait_ge(acc_taken[h], i * 2 + G_FI)
                        turn(i * 2 + (T_FFN - 2), hb[:])

                if not first:
                    chunk(i * 16 + U_FI, 0, i * 2 + G_FI, CU, xT_hi, xT_lo, step, lag=2)
                chunk(i * 16 + U_FI, CU, i * 2 + (G_FI + 1), CU, xT_hi, xT_lo, b=1, lag=2)

            ffn_in(0, True)
            with pe.Fori(1, 11) as i:
                ffn_in(i, False)

            def last_step(j):
                if j == 1:
                    for h in range(HALVES):
                        pe.wait_ge(acc_taken[h], G_FO)
                    turn(T_FFN + 20, hb[:])

            pe.wait_ge(turn_lo, T_FFN + 20)
            for n in range(4):
                chunk(U_FO, 22 * n, G_FO + n, 20, hT_hi, hT_lo, last_step, last=False, b=n % 2, lag=2)
                if n == 0:
                    pe.wait_ge(turn_lo, T_FFN + 22)
                chunk(U_FO, 22 * n + 20, G_FO + n, 2, hT_hi, hT_lo, first=False, k0=20 * UK, b=n % 2)


_INS = ["x", "mem", "mix_pre_gain", "mix_post_gain", "w_in", "gm_v_gain", "gm_w_s", "gm_b_s",
        "s5_lam_re", "s5_lam_im", "s5_log_dt", "s5_b_re", "s5_b_im", "s5_c_re", "s5_c_im", "s5_d",
        "s5_w_glu", "w_br_a", "w_br_b", "w_br_c", "w_out", "xattn_pre_gain", "xattn_post_gain",
        "mem_gain", "w_xq", "w_xkv", "w_xo", "ffn_pre_gain", "ffn_post_gain", "w_ffn_in", "w_ffn_out"]


def kernel(**inputs):
    import numpy as _np
    import concourse.bacc as _bacc
    from concourse import mybir as _mybir
    from concourse.bass_utils import run_bass_kernel_spmd as _run

    nc = _bacc.Bacc("TRN2", target_bir_lowering=False, num_devices=1)
    arrays, args = {}, []
    for name in _INS:
        a = _np.ascontiguousarray(inputs[name])
        arrays[f"in_{name}"] = a
        args.append(nc.dram_tensor(f"in_{name}", a.shape, _mybir.dt.from_np(a.dtype), kind="ExternalInput").ap())
    args.append(nc.dram_tensor("out_0", (1, SEQ, D), F32, kind="ExternalOutput").ap())
    trunk(nc, *args)
    r = _run(nc, [arrays], core_ids=[0])
    return r.results[0]["out_0"]
```
